# Optimizing a Trainium2 kernel written in Bass

```python
import math
import jax
import jax.numpy as jnp
from jax import lax
import numpy as np

D_MODEL = 1024
BATCH = 1
SEQ = 256
DEPTH = 2
DEC_BATCH = 8
DEC_SEQ = 4
PAST_LEN = 1024
PAGE_SIZE = 128

HEAD_DIM = 64
A_HEADS = 6
A_BRANCHES = ((128, 1), (512, 4), (2048, 16))
A_MAX_WINDOW = 2048
B_HEADS = 10
B_KV_HEADS = 2
B_BLOCK = 256
B_TOPK = 3
Q_CHUNK = 128
C_WIDTH = 512
C_GROUP = 16
C_GROUPS = C_WIDTH // C_GROUP
C_STATE = 64
D_HEADS = 8
D_Q_LORA = 256
D_KV_LORA = 128
D_NOPE = 64
D_ROPE = 32
D_VDIM = 64
ROPE_THETA = 10000.0
P_HEADS = 8
P_NKEYS = 128
P_EXPERTS = P_NKEYS * P_NKEYS
P_DKEY = 256
P_TOPK = 16
P_CHUNK = 256
EPS = 1e-6
N_EVEN = (DEPTH + 1) // 2
N_ODD = DEPTH // 2
EVEN_IN = 3 * A_HEADS * HEAD_DIM + B_HEADS * HEAD_DIM + 2 * B_KV_HEADS * HEAD_DIM
EVEN_OUT = (A_HEADS + B_HEADS) * HEAD_DIM
ODD_IN = C_WIDTH + D_Q_LORA + D_KV_LORA + D_ROPE
ODD_OUT = C_WIDTH + D_HEADS * D_VDIM

kernel_name = 'hybrid_dilated_moba_s5_mla_peer_step'

F32 = jnp.float32

def rms_norm(x, g):
    xf = x.astype(F32)
    y = xf * lax.rsqrt(jnp.mean(xf * xf, axis=-1, keepdims=True) + EPS)
    return (y * g.astype(F32)).astype(x.dtype)

def split_cols(z, sizes):
    offs = np.cumsum(sizes)[:-1].tolist()
    return jnp.split(z, offs, axis=-1)

def split_slopes():
    n = A_HEADS + B_HEADS
    s = 2.0 ** (-8.0 * jnp.arange(1, n + 1, dtype=F32) / n)
    return s[:A_HEADS], s[A_HEADS:]

def rope(x, pos):
    half = x.shape[-1] // 2
    freqs = ROPE_THETA ** (-jnp.arange(half, dtype=F32) / half)
    ang = pos.astype(F32)[:, None] * freqs
    shape = (1, ang.shape[0]) + (1,) * (x.ndim - 3) + (half,)
    cos, sin = jnp.cos(ang).reshape(shape), jnp.sin(ang).reshape(shape)
    x1, x2 = x[..., :half].astype(F32), x[..., half:].astype(F32)
    return jnp.concatenate([x1 * cos - x2 * sin, x1 * sin + x2 * cos], axis=-1).astype(x.dtype)

def mix_out(parts, w_out, dtype):
    B, T = parts[0].shape[:2]
    return jnp.concatenate([p.reshape(B, T, -1) for p in parts], axis=-1).astype(dtype) @ w_out

def chunked_queries(fn, arrays, qpos):
    tq = qpos.shape[0]
    chunk = Q_CHUNK if tq % Q_CHUNK == 0 else tq
    n_c = tq // chunk
    def split(a):
        return jnp.swapaxes(a.reshape((a.shape[0], n_c, chunk) + a.shape[2:]), 0, 1)
    xs = tuple(split(a) for a in arrays) + (qpos.reshape(n_c, chunk),)
    out = jnp.swapaxes(lax.map(lambda args: fn(*args), xs), 0, 1)
    return out.reshape((out.shape[0], n_c * chunk) + out.shape[3:])

def dilated_branch_prompt(q, k, v, slopes, window, dilation):
    B, S, H, hd = q.shape
    L = window // dilation
    unit = dilation * L
    s_pad = -(-S // unit) * unit
    m = s_pad // dilation
    nb = m // L
    def strided(t):
        t = jnp.pad(t, [(0, 0), (0, s_pad - S), (0, 0), (0, 0)])
        t = t.reshape(B, m, dilation, H, hd).transpose(0, 2, 1, 3, 4)
        return t.reshape(B, dilation, nb, L, H, hd)
    def with_prev(t):
        prev = jnp.pad(t, [(0, 0), (0, 0), (1, 0), (0, 0), (0, 0), (0, 0)])[:, :, :-1]
        return jnp.concatenate([prev, t], axis=3)
    qs = strided(q)
    kk, vv = with_prev(strided(k)), with_prev(strided(v))
    s = jnp.einsum('brnqhd,brnkhd->brnhqk', qs, kk).astype(F32) / math.sqrt(hd)
    n_idx = jnp.arange(nb)
    mq = n_idx[:, None] * L + jnp.arange(L)[None, :]
    mk = (n_idx[:, None] - 1) * L + jnp.arange(2 * L)[None, :]
    gap = mq[:, :, None] - mk[:, None, :]
    valid = (gap >= 0) & (gap <= L) & (mk[:, None, :] >= 0)
    dist = (gap * dilation).astype(F32)[:, None]
    s = jnp.where(valid[:, None], s - slopes[:, None, None] * dist, -jnp.inf)
    lse = jax.nn.logsumexp(s, axis=-1)
    p = jnp.exp(s - lse[..., None])
    o = jnp.einsum('brnhqk,brnkhd->brnqhd', p, vv.astype(F32))
    o = o.reshape(B, dilation, m, H, hd).transpose(0, 2, 1, 3, 4).reshape(B, s_pad, H, hd)[:, :S]
    lse = lse.transpose(0, 1, 2, 4, 3).reshape(B, dilation, m, H).transpose(0, 2, 1, 3)
    return o, lse.reshape(B, s_pad, H)[:, :S]

def dilated_branch_sample(q, kk, vv, lb, slopes, window, dilation):
    B, T, H, hd = q.shape
    L = window // dilation
    steps = jnp.arange(L + 1)
    idx = lb + jnp.arange(T)[:, None] - steps[None, :] * dilation
    valid = idx >= 0
    idx_c = jnp.maximum(idx, 0)
    kg, vg = kk[:, idx_c], vv[:, idx_c]
    s = jnp.einsum('bthd,btkhd->bhtk', q, kg).astype(F32) / math.sqrt(hd)
    dist = (steps * dilation).astype(F32)
    s = jnp.where(valid[None, None], s - slopes[:, None, None] * dist, -jnp.inf)
    lse = jax.nn.logsumexp(s, axis=-1)
    p = jnp.exp(s - lse[..., None])
    o = jnp.einsum('bhtk,btkhd->bthd', p, vg.astype(F32))
    return o, lse.transpose(0, 2, 1)

def merge_branches(outs, lses):
    w = jax.nn.softmax(jnp.stack(lses, axis=0), axis=0)
    return sum(w[i][..., None] * outs[i] for i in range(len(outs)))

def moba_attend(q, qpos, k, v, slopes):
    B, Tq, H, hd = q.shape
    nblk = k.shape[1] // B_BLOCK
    G = H // B_KV_HEADS
    kb = k.reshape(B, nblk, B_BLOCK, B_KV_HEADS, hd)
    vb = v.reshape(B, nblk, B_BLOCK, B_KV_HEADS, hd)
    kbar = jnp.mean(kb.astype(F32), axis=2)
    n_sel = min(B_TOPK, nblk)
    sl = slopes.reshape(B_KV_HEADS, G)
    bi = jnp.arange(B)[:, None, None, None]
    gi = jnp.arange(B_KV_HEADS)[None, None, :, None]
    def one(qq, pp):
        C = pp.shape[0]
        qg = qq.reshape(B, C, B_KV_HEADS, G, hd)
        gate = jnp.einsum('bckgd,bnkd->bckn', qg.astype(F32), kbar)
        own = pp // B_BLOCK
        past = jnp.arange(nblk)[None, :] < own[:, None]
        gate = jnp.where(past[None, :, None, :], gate, -jnp.inf)
        _, sel = lax.top_k(gate, n_sel)
        sel_ok = sel < own[None, :, None, None]
        idx = jnp.concatenate([sel, jnp.broadcast_to(own[None, :, None, None], (B, C, B_KV_HEADS, 1))], axis=-1)
        ok = jnp.concatenate([sel_ok, jnp.ones((B, C, B_KV_HEADS, 1), bool)], axis=-1)
        kg = kb[bi, idx, :, gi]
        vg = vb[bi, idx, :, gi]
        s = jnp.einsum('bckgd,bcknsd->bckgns', qg, kg).astype(F32) / math.sqrt(hd)
        kpos = idx[..., None] * B_BLOCK + jnp.arange(B_BLOCK)
        dist = pp[None, :, None, None, None] - kpos
        valid = ok[..., None] & (dist >= 0)
        s = s - sl[None, None, :, :, None, None] * dist[:, :, :, None].astype(F32)
        s = jnp.where(valid[:, :, :, None], s, -jnp.inf)
        p = jax.nn.softmax(s.reshape(B, C, B_KV_HEADS, G, -1), axis=-1).reshape(s.shape)
        o = jnp.einsum('bckgns,bcknsd->bckgd', p, vg.astype(F32))
        return o.reshape(B, C, H, hd)
    return chunked_queries(one, (q,), qpos)

def even_heads(h, w_in, g_qa, g_ka, g_qb, g_kb):
    B, T, _ = h.shape
    da, dq, dkv = A_HEADS * HEAD_DIM, B_HEADS * HEAD_DIM, B_KV_HEADS * HEAD_DIM
    qa, ka, va, qb, kb, vb = split_cols(h @ w_in, [da, da, da, dq, dkv, dkv])
    def heads(t, n):
        return t.reshape(B, T, n, HEAD_DIM)
    return (rms_norm(heads(qa, A_HEADS), g_qa), rms_norm(heads(ka, A_HEADS), g_ka), heads(va, A_HEADS),
            rms_norm(heads(qb, B_HEADS), g_qb), rms_norm(heads(kb, B_KV_HEADS), g_kb), heads(vb, B_KV_HEADS))

def even_prompt(h, w_in, w_out, g_qa, g_ka, g_qb, g_kb):
    B, S, _ = h.shape
    qa, ka, va, qb, kb, vb = even_heads(h, w_in, g_qa, g_ka, g_qb, g_kb)
    sa, sb = split_slopes()
    outs, lses = [], []
    for window, dilation in A_BRANCHES:
        o, l = dilated_branch_prompt(qa, ka, va, sa, window, dilation)
        outs.append(o)
        lses.append(l)
    oa = merge_branches(outs, lses)
    pad = [(0, 0), (0, -S % B_BLOCK), (0, 0), (0, 0)]
    ob = moba_attend(qb, jnp.arange(S), jnp.pad(kb, pad), jnp.pad(vb, pad), sb)
    keep = min(A_MAX_WINDOW, S)
    return mix_out([oa, ob], w_out, h.dtype), ka[:, S - keep:], va[:, S - keep:], kb, vb

def even_sample(h, buf_k, buf_v, pool_k, pool_v, page_table, w_in, w_out, g_qa, g_ka, g_qb, g_kb):
    B, T, _ = h.shape
    qa, ka, va, qb, kb, vb = even_heads(h, w_in, g_qa, g_ka, g_qb, g_kb)
    sa, sb = split_slopes()
    lb = buf_k.shape[1]
    kk = jnp.concatenate([buf_k, ka], axis=1)
    vv = jnp.concatenate([buf_v, va], axis=1)
    outs, lses = [], []
    for window, dilation in A_BRANCHES:
        o, l = dilated_branch_sample(qa, kk, vv, lb, sa, window, dilation)
        outs.append(o)
        lses.append(l)
    oa = merge_branches(outs, lses)
    def one(args):
        pages, q1, k1, v1 = args
        kp = pool_k[pages].reshape(-1, B_KV_HEADS, HEAD_DIM)
        vp = pool_v[pages].reshape(-1, B_KV_HEADS, HEAD_DIM)
        n_past = kp.shape[0]
        pad = [(0, -(n_past + T) % B_BLOCK), (0, 0), (0, 0)]
        kc = jnp.pad(jnp.concatenate([kp, k1], axis=0), pad)
        vc = jnp.pad(jnp.concatenate([vp, v1], axis=0), pad)
        return moba_attend(q1[None], n_past + jnp.arange(T), kc[None], vc[None], sb)[0]
    ob = lax.map(one, (page_table, qb, kb, vb))
    return mix_out([oa, ob], w_out, h.dtype), ka, va, kb, vb

def s5_scan(u, s0_re, s0_im, a_re, a_im, log_dt, b_re, b_im, c_re, c_im, d_skip, w_glu, b_glu):
    B, T, _ = u.shape
    uf = u.astype(F32).reshape(B, T, C_GROUPS, C_GROUP)
    a_re, a_im = a_re.astype(F32), a_im.astype(F32)
    dt = jnp.exp(log_dt.astype(F32))[:, None]
    mag = jnp.exp(a_re * dt)
    abar_re, abar_im = mag * jnp.cos(a_im * dt), mag * jnp.sin(a_im * dt)
    den = a_re * a_re + a_im * a_im
    nr, ni = abar_re - 1.0, abar_im
    f_re = (nr * a_re + ni * a_im) / den
    f_im = (ni * a_re - nr * a_im) / den
    br, bim = b_re.astype(F32), b_im.astype(F32)
    bbar_re = f_re[..., None] * br - f_im[..., None] * bim
    bbar_im = f_re[..., None] * bim + f_im[..., None] * br
    bu_re = jnp.einsum('btgc,gnc->btgn', uf, bbar_re)
    bu_im = jnp.einsum('btgc,gnc->btgn', uf, bbar_im)
    ar = jnp.broadcast_to(abar_re, bu_re.shape)
    ai = jnp.broadcast_to(abar_im, bu_re.shape)
    def combine(e1, e2):
        a1r, a1i, b1r, b1i = e1
        a2r, a2i, b2r, b2i = e2
        return (a2r * a1r - a2i * a1i, a2r * a1i + a2i * a1r,
                a2r * b1r - a2i * b1i + b2r, a2r * b1i + a2i * b1r + b2i)
    pr, pi, sr, si = lax.associative_scan(combine, (ar, ai, bu_re, bu_im), axis=1)
    if s0_re is not None:
        s0r, s0i = s0_re.astype(F32)[:, None], s0_im.astype(F32)[:, None]
        sr, si = sr + pr * s0r - pi * s0i, si + pr * s0i + pi * s0r
    y = jnp.einsum('btgn,gcn->btgc', sr, c_re.astype(F32)) - jnp.einsum('btgn,gcn->btgc', si, c_im.astype(F32))
    y = y.reshape(B, T, C_WIDTH) + d_skip.astype(F32) * uf.reshape(B, T, C_WIDTH)
    z = jax.nn.gelu(y)
    out = z * jax.nn.sigmoid(z @ w_glu.astype(F32) + b_glu.astype(F32))
    return out, sr[:, -1], si[:, -1]

def odd_heads(h, pos, w_in, g_cq, g_ckv, w_uq, g_qn, g_qr, g_kr):
    B, T, _ = h.shape
    u, cq, ckv, kpe = split_cols(h @ w_in, [C_WIDTH, D_Q_LORA, D_KV_LORA, D_ROPE])
    q = (rms_norm(cq, g_cq) @ w_uq).reshape(B, T, D_HEADS, D_NOPE + D_ROPE)
    q_nope = rms_norm(q[..., :D_NOPE], g_qn)
    q_pe = rope(rms_norm(q[..., D_NOPE:], g_qr), pos)
    return u, q_nope, q_pe, rms_norm(ckv, g_ckv), rope(rms_norm(kpe, g_kr), pos)

def mla_expand(ckv, w_uk, w_uv, g_kn):
    k_nope = rms_norm((ckv @ w_uk).reshape(ckv.shape[:-1] + (D_HEADS, D_NOPE)), g_kn)
    v = (ckv @ w_uv).reshape(ckv.shape[:-1] + (D_HEADS, D_VDIM))
    return k_nope, v

def mla_core(q_nope, q_pe, k_nope, k_pe, v, qpos):
    s = (jnp.einsum('bqhd,bkhd->bhqk', q_nope, k_nope) + jnp.einsum('bqhr,bkr->bhqk', q_pe, k_pe)).astype(F32)
    s = s / math.sqrt(D_NOPE + D_ROPE)
    mask = jnp.arange(k_nope.shape[1])[None, :] <= qpos[:, None]
    p = jax.nn.softmax(jnp.where(mask[None, None], s, -jnp.inf), axis=-1)
    return jnp.einsum('bhqk,bkhd->bqhd', p, v.astype(F32))

def odd_prompt(h, w_in, w_out, s5p, mlap):
    B, S, _ = h.shape
    g_cq, g_ckv, w_uq, w_uk, w_uv, g_qn, g_qr, g_kn, g_kr = mlap
    pos = jnp.arange(S)
    u, q_nope, q_pe, ckv, kpe = odd_heads(h, pos, w_in, g_cq, g_ckv, w_uq, g_qn, g_qr, g_kr)
    oc, s_re, s_im = s5_scan(u, None, None, *s5p)
    k_nope, v = mla_expand(ckv, w_uk, w_uv, g_kn)
    od = chunked_queries(lambda qn, qp, qpos: mla_core(qn, qp, k_nope, kpe, v, qpos), (q_nope, q_pe), pos)
    return mix_out([oc, od], w_out, h.dtype), s_re, s_im, ckv, kpe

def odd_sample(h, s0_re, s0_im, pool_ckv, pool_kpe, page_table, w_in, w_out, s5p, mlap):
    B, T, _ = h.shape
    g_cq, g_ckv, w_uq, w_uk, w_uv, g_qn, g_qr, g_kn, g_kr = mlap
    n_past = page_table.shape[1] * PAGE_SIZE
    pos = n_past + jnp.arange(T)
    u, q_nope, q_pe, ckv, kpe = odd_heads(h, pos, w_in, g_cq, g_ckv, w_uq, g_qn, g_qr, g_kr)
    oc, s_re, s_im = s5_scan(u, s0_re, s0_im, *s5p)
    def one(args):
        pages, qn, qp, cn, kn = args
        c_all = jnp.concatenate([pool_ckv[pages].reshape(-1, D_KV_LORA), cn], axis=0)[None]
        k_all = jnp.concatenate([pool_kpe[pages].reshape(-1, D_ROPE), kn], axis=0)[None]
        k_nope, v = mla_expand(c_all, w_uk, w_uv, g_kn)
        return mla_core(qn[None], qp[None], k_nope, k_all, v, pos)[0]
    od = lax.map(one, (page_table, q_nope, q_pe, ckv, kpe))
    return mix_out([oc, od], w_out, h.dtype), s_re, s_im, ckv, kpe

def peer(h, w_q, sub_k1, sub_k2, u_tab, v_tab):
    B, T, D = h.shape
    n = B * T
    n_pad = -(-n // P_CHUNK) * P_CHUNK
    xs = jnp.pad(h.reshape(n, D), [(0, n_pad - n), (0, 0)]).reshape(n_pad // P_CHUNK, P_CHUNK, D)
    def one(xc):
        q = (xc @ w_q).reshape(P_CHUNK, P_HEADS, 2, P_DKEY // 2)
        s1 = jnp.einsum('thd,hkd->thk', q[:, :, 0], sub_k1)
        s2 = jnp.einsum('thd,hkd->thk', q[:, :, 1], sub_k2)
        v1, i1 = lax.top_k(s1, P_TOPK)
        v2, i2 = lax.top_k(s2, P_TOPK)
        cand = (v1[..., :, None] + v2[..., None, :]).reshape(P_CHUNK, P_HEADS, P_TOPK * P_TOPK)
        cid = (i1[..., :, None] * P_NKEYS + i2[..., None, :]).reshape(P_CHUNK, P_HEADS, P_TOPK * P_TOPK)
        sc, j = lax.top_k(cand, P_TOPK)
        eid = jnp.take_along_axis(cid, j, axis=-1)
        g = jax.nn.softmax(sc.astype(F32), axis=-1)
        act = jax.nn.gelu(jnp.einsum('td,thkd->thk', xc, u_tab[eid]).astype(F32))
        return jnp.einsum('thk,thkd->td', g * act, v_tab[eid].astype(F32)).astype(h.dtype)
    return lax.map(one, xs).reshape(n_pad, D)[:n].reshape(B, T, D)

def setup_inputs(seed: int = 0) -> dict:
    key = jax.random.key(seed)
    ks = iter(jax.random.split(key, 64))
    def nrm(shape, scale):
        return scale * jax.random.normal(next(ks), shape, F32)
    def gain(shape):
        return 1.0 + 0.05 * jax.random.normal(next(ks), shape, F32)
    n_pages = PAST_LEN // PAGE_SIZE
    n_used = DEC_BATCH * n_pages
    n_pool = n_used + max(1, n_used // 4)
    win_buf = min(A_MAX_WINDOW, PAST_LEN)
    page_table = jax.random.permutation(next(ks), n_pool)[:n_used].reshape(DEC_BATCH, n_pages).astype(jnp.int32)
    return {
        'x_prompt': nrm((BATCH, SEQ, D_MODEL), 1.0),
        'x_sample': nrm((DEC_BATCH, DEC_SEQ, D_MODEL), 1.0),
        'cache_a_k': nrm((N_EVEN, DEC_BATCH, win_buf, A_HEADS, HEAD_DIM), 1.0),
        'cache_a_v': nrm((N_EVEN, DEC_BATCH, win_buf, A_HEADS, HEAD_DIM), 1.0),
        'cache_b_k': nrm((N_EVEN, n_pool, PAGE_SIZE, B_KV_HEADS, HEAD_DIM), 1.0),
        'cache_b_v': nrm((N_EVEN, n_pool, PAGE_SIZE, B_KV_HEADS, HEAD_DIM), 1.0),
        'state_c_re': nrm((N_ODD, DEC_BATCH, C_GROUPS, C_STATE), 0.5),
        'state_c_im': nrm((N_ODD, DEC_BATCH, C_GROUPS, C_STATE), 0.5),
        'cache_d_ckv': nrm((N_ODD, n_pool, PAGE_SIZE, D_KV_LORA), 1.0),
        'cache_d_kpe': nrm((N_ODD, n_pool, PAGE_SIZE, D_ROPE), 1.0),
        'page_table': page_table,
        'g_mix': gain((DEPTH, D_MODEL)),
        'g_ffn': gain((DEPTH, D_MODEL)),
        'ev_w_in': nrm((N_EVEN, D_MODEL, EVEN_IN), D_MODEL ** -0.5),
        'ev_w_out': nrm((N_EVEN, EVEN_OUT, D_MODEL), EVEN_OUT ** -0.5),
        'ev_g_qa': gain((N_EVEN, HEAD_DIM)),
        'ev_g_ka': gain((N_EVEN, HEAD_DIM)),
        'ev_g_qb': gain((N_EVEN, HEAD_DIM)),
        'ev_g_kb': gain((N_EVEN, HEAD_DIM)),
        'od_w_in': nrm((N_ODD, D_MODEL, ODD_IN), D_MODEL ** -0.5),
        'od_w_out': nrm((N_ODD, ODD_OUT, D_MODEL), ODD_OUT ** -0.5),
        's5_a_re': -0.5 + nrm((N_ODD, C_GROUPS, C_STATE), 0.01),
        's5_a_im': jnp.pi * jnp.arange(C_STATE, dtype=F32) + nrm((N_ODD, C_GROUPS, C_STATE), 0.01),
        's5_log_dt': jax.random.uniform(next(ks), (N_ODD, C_GROUPS), F32, math.log(1e-3), math.log(1e-1)),
        's5_b_re': nrm((N_ODD, C_GROUPS, C_STATE, C_GROUP), (2.0 * C_GROUP) ** -0.5),
        's5_b_im': nrm((N_ODD, C_GROUPS, C_STATE, C_GROUP), (2.0 * C_GROUP) ** -0.5),
        's5_c_re': nrm((N_ODD, C_GROUPS, C_GROUP, C_STATE), (2.0 * C_STATE) ** -0.5),
        's5_c_im': nrm((N_ODD, C_GROUPS, C_GROUP, C_STATE), (2.0 * C_STATE) ** -0.5),
        's5_d': nrm((N_ODD, C_WIDTH), 1.0),
        's5_w_glu': nrm((N_ODD, C_WIDTH, C_WIDTH), C_WIDTH ** -0.5),
        's5_b_glu': nrm((N_ODD, C_WIDTH), 0.01),
        'mla_g_cq': gain((N_ODD, D_Q_LORA)),
        'mla_g_ckv': gain((N_ODD, D_KV_LORA)),
        'mla_w_uq': nrm((N_ODD, D_Q_LORA, D_HEADS * (D_NOPE + D_ROPE)), D_Q_LORA ** -0.5),
        'mla_w_uk': nrm((N_ODD, D_KV_LORA, D_HEADS * D_NOPE), D_KV_LORA ** -0.5),
        'mla_w_uv': nrm((N_ODD, D_KV_LORA, D_HEADS * D_VDIM), D_KV_LORA ** -0.5),
        'mla_g_qn': gain((N_ODD, D_NOPE)),
        'mla_g_qr': gain((N_ODD, D_ROPE)),
        'mla_g_kn': gain((N_ODD, D_NOPE)),
        'mla_g_kr': gain((N_ODD, D_ROPE)),
        'peer_w_q': nrm((DEPTH, D_MODEL, P_HEADS * P_DKEY), D_MODEL ** -0.5),
        'peer_k1': nrm((DEPTH, P_HEADS, P_NKEYS, P_DKEY // 2), (P_DKEY // 2) ** -0.5),
        'peer_k2': nrm((DEPTH, P_HEADS, P_NKEYS, P_DKEY // 2), (P_DKEY // 2) ** -0.5),
        'peer_u': nrm((DEPTH, P_EXPERTS, D_MODEL), D_MODEL ** -0.5),
        'peer_v': nrm((DEPTH, P_EXPERTS, D_MODEL), 0.25),
    }

def reference(x_prompt, x_sample, cache_a_k, cache_a_v, cache_b_k, cache_b_v, state_c_re, state_c_im,
              cache_d_ckv, cache_d_kpe, page_table, g_mix, g_ffn, ev_w_in, ev_w_out, ev_g_qa, ev_g_ka,
              ev_g_qb, ev_g_kb, od_w_in, od_w_out, s5_a_re, s5_a_im, s5_log_dt, s5_b_re, s5_b_im, s5_c_re,
              s5_c_im, s5_d, s5_w_glu, s5_b_glu, mla_g_cq, mla_g_ckv, mla_w_uq, mla_w_uk, mla_w_uv, mla_g_qn,
              mla_g_qr, mla_g_kn, mla_g_kr, peer_w_q, peer_k1, peer_k2, peer_u, peer_v):
    xp, xs = x_prompt, x_sample
    ak_p, av_p, bk_p, bv_p, cr_p, ci_p, dc_p, dk_p = [], [], [], [], [], [], [], []
    ak_s, av_s, bk_s, bv_s, cr_s, ci_s, dc_s, dk_s = [], [], [], [], [], [], [], []
    for layer in range(DEPTH):
        hp, hs = rms_norm(xp, g_mix[layer]), rms_norm(xs, g_mix[layer])
        if layer % 2 == 0:
            e = layer // 2
            ew = (ev_w_in[e], ev_w_out[e], ev_g_qa[e], ev_g_ka[e], ev_g_qb[e], ev_g_kb[e])
            op, k1, v1, k2, v2 = even_prompt(hp, *ew)
            ak_p.append(k1); av_p.append(v1); bk_p.append(k2); bv_p.append(v2)
            osm, k1, v1, k2, v2 = even_sample(hs, cache_a_k[e], cache_a_v[e], cache_b_k[e], cache_b_v[e],
                                              page_table, *ew)
            ak_s.append(k1); av_s.append(v1); bk_s.append(k2); bv_s.append(v2)
        else:
            o = layer // 2
            s5p = (s5_a_re[o], s5_a_im[o], s5_log_dt[o], s5_b_re[o], s5_b_im[o], s5_c_re[o], s5_c_im[o],
                   s5_d[o], s5_w_glu[o], s5_b_glu[o])
            mlap = (mla_g_cq[o], mla_g_ckv[o], mla_w_uq[o], mla_w_uk[o], mla_w_uv[o], mla_g_qn[o],
                    mla_g_qr[o], mla_g_kn[o], mla_g_kr[o])
            op, sr, si, ckv, kpe = odd_prompt(hp, od_w_in[o], od_w_out[o], s5p, mlap)
            cr_p.append(sr); ci_p.append(si); dc_p.append(ckv); dk_p.append(kpe)
            osm, sr, si, ckv, kpe = odd_sample(hs, state_c_re[o], state_c_im[o], cache_d_ckv[o], cache_d_kpe[o],
                                               page_table, od_w_in[o], od_w_out[o], s5p, mlap)
            cr_s.append(sr); ci_s.append(si); dc_s.append(ckv); dk_s.append(kpe)
        xp = xp + op
        xs = xs + osm
        pw = (peer_w_q[layer], peer_k1[layer], peer_k2[layer], peer_u[layer], peer_v[layer])
        xp = xp + peer(rms_norm(xp, g_ffn[layer]), *pw)
        xs = xs + peer(rms_norm(xs, g_ffn[layer]), *pw)
    return (xp, xs,
            jnp.stack(ak_p), jnp.stack(av_p), jnp.stack(bk_p), jnp.stack(bv_p),
            jnp.stack(cr_p), jnp.stack(ci_p), jnp.stack(dc_p), jnp.stack(dk_p),
            jnp.stack(ak_s), jnp.stack(av_s), jnp.stack(bk_s), jnp.stack(bv_s),
            jnp.stack(cr_s), jnp.stack(ci_s), jnp.stack(dc_s), jnp.stack(dk_s))


_drawn_inputs = setup_inputs


def setup_inputs(seed=0):
    import zlib

    import numpy as np

    out = dict(_drawn_inputs(seed))
    spreads = {}
    factors = {'ev_g_qb': 2.943,
     's5_a_re': 16.459,
     's5_b_glu': 43.199,
     'mla_g_cq': 4.961,
     'mla_g_qn': 5.838,
     'mla_g_qr': 7.048,
     'mla_g_kn': 5.742}
    for name, (base, spread) in spreads.items():
        noise = np.random.default_rng([zlib.crc32(name.encode()), seed]).standard_normal(out[name].shape)
        drawn = base * np.exp(spread * noise) if base else spread * noise
        out[name] = jnp.asarray(drawn.astype(out[name].dtype))
    for name, factor in factors.items():
        out[name] = (out[name] * factor).astype(out[name].dtype)
    return out
```

```python
import math

import numpy as np

import concourse.bass as bass
from concourse import mybir
from contextlib import ExitStack

F32 = mybir.dt.float32
F32R = mybir.dt.float32r
BF16 = mybir.dt.bfloat16
U32 = mybir.dt.uint32
I32 = mybir.dt.int32
ALU = mybir.AluOpType
ACT = mybir.ActivationFunctionType
AX = mybir.AxisListType.X
ds = bass.ds

P = 128
D = 1024
KC = D // P
SEQ, DEC_B, DEC_T = 256, 8, 4
NS = DEC_B * DEC_T
NT = SEQ + NS
TILES = ((0, P, 0), (1, P, P), (2, NS, SEQ))
PAST, PAGE = 1024, 128
PAGES = PAST // PAGE
HD = 64
AH, BH, BKV = 6, 10, 2
GQ = BH // BKV
NORMED = 2 * AH + BH + BKV
EVEN_IN, ODD_IN = 2048, 928
VA0, QB0, KB0, VB0 = 768, 1152, 1792, 1920
AK = 640
AKC = AK // P
BLK = 256
NBLK = PAST // BLK
DH, DN, DR = 8, 64, 32
DQK = DN + DR
CQ, CKV = 256, 128
SCH, SG2 = 16, 8
PH, TOPK, NK = 8, 16, 128
QK = NK // 4
NGT = 12
NG = NT // NGT
EPS = 1e-6
BIG = 1e30
NEG = -3.0e38
TWO_PI = 2.0 * math.pi
MAGIC = 1.5 * 2.0 ** 23
C1 = 6.28125
C2 = float(np.float32(TWO_PI - C1))
C3 = float(np.float32(TWO_PI - C1 - float(np.float32(TWO_PI - C1))))
SCALE_AB = 1.0 / math.sqrt(HD)
SCALE_D = 1.0 / math.sqrt(DQK)


class Carver:

    def __init__(self, regions, base, size):
        self.region, self.size, self.at = regions[base], size, 0

    def skip_to(self, at):
        self.at = at
        return self

    def take(self, *shape, parts=P, dt=F32):
        n = int(np.prod(shape)) // (2 if dt is BF16 else 1)
        assert self.at + n <= self.size, (self.at, n, self.size)
        v = self.region[0:parts, self.at:self.at + n]
        self.at += n
        if dt is not F32:
            v = v.bitcast(dt)
        if len(shape) == 2:
            v = v.rearrange("p (a b) -> p a b", b=shape[1])
        if len(shape) == 3:
            v = v.rearrange("p (a b c) -> p a b c", b=shape[1], c=shape[2])
        if len(shape) == 4:
            v = v.rearrange("p (a b c d) -> p a b c d", b=shape[1], c=shape[2], d=shape[3])
        return v


def bc(ap, axis, n):
    shape = list(ap.shape)
    return ap.unsqueeze(axis).broadcast_to(shape[:axis] + [n] + shape[axis:])


def build(nc, I, O, stop=4):
    ctx = ExitStack()
    with ctx:
        sems = {}

        def sem(name):
            if name not in sems:
                sems[name] = ctx.enter_context(nc.semaphore(name))
            return sems[name]

        R1_0, R1_N = 6112, 19800
        R2_0, R2_N = R1_0 + R1_N, 19000
        RING_0, RING_N = R2_0 + R2_N, 8192
        base = (nc.sbuf_base + 31) // 32 * 32
        arena = {at: ctx.enter_context(nc.sbuf_tensor(name, [P, n], F32))
                 for name, at, n in (("keep", 0, R1_0), ("region1", R1_0, R1_N), ("region2", R2_0, R2_N), ("ring", RING_0, RING_N))}

        def rounded(name, shape, at):
            return nc.alloc_sbuf_tensor_at(name, [P] + shape, F32R, offset=base + 4 * at)

        banks = [ctx.enter_context(nc.psum_tensor(f"bank{i}", [P, 512], F32)) for i in range(8)]

        keep = Carver(arena, 0, 6112)
        X = keep.take(3, D)
        HT = keep.take(KC, NT)
        ident = keep.take(P)
        iota = keep.take(NK)
        before = keep.take(NBLK, NBLK)
        group = keep.take(P)
        gain = keep.take(4, KC)
        ss = keep.take(3)
        rinv = keep.take(3)
        pages = keep.take(PAGES * DEC_B, parts=1, dt=I32)

        r1 = Carver(arena, R1_0, R1_N)
        W_IN0 = r1.take(KC, EVEN_IN)
        r1.skip_to(0)
        KA = r1.take(4, 3, AK)
        VA = r1.take(4, AKC, 3 * P)
        OT0 = r1.take(KC, NT)
        O0 = r1.take(2, D)
        r1.skip_to(17664)
        GAIN0 = r1.take(NORMED, HD)
        r1.skip_to(0)
        W_OUT = r1.take(KC, D)
        r2 = Carver(arena, R2_0, R2_N)
        Z = r2.take(3, EVEN_IN)
        QKT = r2.take(NORMED, NT, parts=HD)
        KVB = r2.take(2, PAGES, 2 * P)
        PTP = r2.take(2, 4, P)
        r2s = r2.at
        RS24 = r2.take(NORMED)
        r3 = Carver(arena, RING_0, RING_N)
        HTOK = r3.take(3, D)
        SQ = r3.take(NORMED, HD)
        r3.skip_to(0)
        TBL0 = r3.take(8, 768)
        SP_ = r3.take(2, 512)
        PP_ = r3.take(2, 512)
        r3.skip_to(0)
        SS_ = r3.take(PAST + NS)
        PTS = r3.take(PAGES + 1, P)
        TBLA = r3.take(2, AK + NS)
        TBLB = r3.take(PAST)
        TBLBN = r3.take(4, NS)
        QBA = r3.take(3, DEC_B, 32)
        QBB = r3.take(DEC_B, 64)
        KNA = r3.take(3, NS)
        KNB = r3.take(NS)
        r2 = Carver(arena, R2_0, R2_N).skip_to(r2s + NORMED)
        MX = r2.take(2, 2)
        SUMS = r2.take(2, 2)
        RSUM = r2.take(2)
        GATE = r2.take(NBLK)
        CMP = r2.take(NBLK, NBLK)
        CMP2 = r2.take(NBLK, NBLK)
        RANK = r2.take(NBLK)
        MX1 = r2.take(1)
        SUM1 = r2.take(1)

        r1 = Carver(arena, R1_0, R1_N)
        W_Q = r1.take(KC, 2048)
        KEYS = r1.take(2 * PH, NK)
        G = Carver(arena, R1_0, R1_N).take(2 * QK, NT)
        r2 = Carver(arena, R2_0, R2_N)
        QT = r2.take(2 * PH, NT)
        SC = r2.take(2 * PH, NK)
        SC2 = r2.take(2 * PH, NK)
        CAND = r2.take(PH, TOPK, TOPK)
        CAND2 = r2.take(PH, TOPK, TOPK)
        EQ = r2.take(PH, TOPK, TOPK)
        TOPV = r2.take(PH, 2, TOPK)
        TOPI = r2.take(PH, 2, TOPK, dt=U32)
        TOPIF = r2.take(PH, 2, TOPK)
        SELV = r2.take(PH, TOPK)
        SELJ = r2.take(PH, TOPK, dt=U32)
        SELAB = r2.take(2, PH, TOPK, dt=U32)
        SELABF = r2.take(2, PH, TOPK)
        ROUTE = r2.take(3, P)
        GSUM = r2.take(PH)
        r2 = Carver(arena, R2_0, R2_N).skip_to(R2_N - 3 * NT - 3 * NT)
        ROUTET = r2.take(3, NT)
        PIECES = r2.take(6, NT, dt=BF16)
        UV = rounded("uv_parts", [2, 4, D], R2_0)
        WR = rounded("weight_parts", [2, 2, SEQ], R2_0 + 8 * D)
        WRS = rounded("sample_weight_parts", [2, 2, NS], R2_0 + 8 * D + 4 * SEQ)
        HR = rounded("h_parts", [2, KC, NT], R2_0 + 8 * D + 4 * NT)
        r2 = Carver(arena, R2_0, R2_N).skip_to(8 * D + 4 * NT + 2 * KC * NT)
        ACTV = r2.take(2, NT)
        ONE1 = r2.take(2, NGT, NK, dt=BF16)
        ONE2 = r2.take(2, NGT, 3 * QK, dt=BF16).rearrange("p s t (e n) -> p s t e n", e=3)
        assert r2.at <= R2_N - 6 * NT
        WFULL = Carver(arena, R1_0, R1_N).skip_to(2 * QK * NT).take(2, NT)
        ZEROS = Carver(arena, R1_0, R1_N).skip_to(2 * QK * NT + 2 * NT).take(512)
        EQ2 = Carver(arena, R1_0, R1_N).skip_to(2 * QK * NT + 2 * NT + 512).take(NGT, QK, dt=BF16)
        MIXS = Carver(arena, R1_0, R1_N).take(2, 512, parts=2 * NS)
        SLOTS = Carver(arena, RING_0, RING_N).take(4, 2, D)

        r1 = Carver(arena, R1_0, R1_N)
        W_IN1 = r1.take(KC, ODD_IN)
        S_D = r1.take(2, 512)
        P_D = r1.take(2, 512)
        PT_D = r1.take(2, 4, P)
        TBLD = r1.take(384)
        O1 = r1.take(3, 512)
        r1 = Carver(arena, R1_0, R1_N)
        BU = r1.take(2, SG2, NT)
        E = r1.take(2, SG2, SEQ)
        XR = r1.take(2, SG2, SEQ)
        T12 = r1.take(2, SG2, SEQ)
        RARR = r1.take(SG2, SEQ)
        r1 = Carver(arena, R1_0, R1_N)
        CKP = r1.take(4, PAGES, 2 * P)
        KPP = r1.take(4, PAGES, P, parts=DR)
        S_SD = r1.take(PAST + NS)
        R_SD = r1.take(PAST + NS)
        PT_SD = r1.take(PAGES + 1, P)
        SQD = r1.take(2, 512)
        CT = r1.take(DH, NS)
        QABS = r1.take(DEC_B, DH, DEC_T)
        QPE = r1.take(DEC_B, DH, DEC_T, parts=DR)
        KPEN = r1.take(NS, parts=DR)
        TBLDN = r1.take(2, NS)
        RKX = r1.take(4, PAGES, DH * DEC_T)
        RKN = r1.take(DH, DEC_T)
        QG = r1.take(DH, NS, parts=DN)
        r2 = Carver(arena, R2_0, R2_N)
        UT = r2.take(4, NT)
        Z2 = r2.take(3, CQ + CKV + DR)
        CQT = r2.take(2, NT)
        CKT = r2.take(NT)
        q_at = r2.at
        Q = r2.take(3, DH, DQK)
        OT1 = Carver(arena, R2_0, R2_N).skip_to(q_at).take(KC, NT)
        kc_at = r2.at
        KCAT = r2.take(2, DH, DQK)
        Y = Carver(arena, R2_0, R2_N).skip_to(kc_at).take(4, NT)
        kr_at = r2.at
        KR = r2.take(3, 512)
        ZG = Carver(arena, R2_0, R2_N).skip_to(kr_at).take(4, NT)
        QCT = r2.take(DH, NT, parts=DQK)
        vd_at = r2.at
        VD = r2.take(3, 512)
        SGM = Carver(arena, R2_0, R2_N).skip_to(vd_at).take(4, NT)
        kct_at = r2.at
        KCT = r2.take(DH, SEQ, parts=DQK)
        r2x = Carver(arena, R2_0, R2_N).skip_to(kct_at)
        BBD = r2x.take(2, SCH, 32)
        BSC = r2x.take(2, SCH, 32)
        CBD = r2.take(2, SCH, 32)
        S5P = r2.take(24, SCH)
        S0 = r2.take(2, SCH, DEC_B)
        DSKIP = r2.take(4)
        BGLU = r2.take(4)
        ST8 = r2.take(3, 32)
        ST8I = r2.take(3, 32)
        RKS = r2.take(4, PAGES, DH)
        BT = r2.take(2, 4, P)
        STMP = r2.take(4, SG2, DEC_B)
        LASTP = r2.take(2, SCH)
        LASTS = r2.take(2, SCH, DEC_B)
        r3 = Carver(arena, RING_0, RING_N)
        HTOK1 = r3.take(3, D)
        GROW = r3.take(CQ + CKV + DR)
        GQN = r3.take(DN)
        GQR = r3.take(DR)
        GKN = r3.take(DN)
        GKNP = r3.take(1, parts=DN)
        COS = r3.take(3, DR // 2)
        SIN = r3.take(3, DR // 2)
        W_UK = r3.take(512)
        W_UV = r3.take(512)
        W_UKT = r3.take(DH, P, parts=DN)
        W_GLU = r3.take(4, 512)
        r3 = Carver(arena, RING_0, RING_N)
        W_UQ = r3.take(2, DH * DQK)
        RT = r3.take(4, DH, DR // 2)

        DB, AB = banks[0:4], banks[4:8]
        d_full, d_free, a_full, a_free = (sem(n) for n in ("dve_bank_full", "dve_bank_free", "act_bank_full", "act_bank_free"))
        block = ctx.enter_context(nc.Block())

        def live(n):
            return stop >= n

        @block.sync
        def _(sp):
            nst = [0]

            def load(out, in_, name):
                sp.dma_start(out, in_).then_inc(sem(name), 16)

            def store(out, in_):
                sp.dma_start(out, in_).then_inc(sem("stored"), 16)
                nst[0] += 16

            load(X[:, 0, :], I["x_prompt"][0:P, :], "x_loaded")
            load(X[:, 1, :], I["x_prompt"][P:SEQ, :], "x_loaded")
            load(X[0:NS, 2, :], I["x_sample"], "x_loaded")
            load(ident, I["ident"], "const_loaded")
            load(iota, I["iota"], "const_loaded")
            load(gain, I["gain"], "const_loaded")
            load(group, I["group"], "const_loaded")
            load(before, I["before"], "const_loaded")
            load(pages, I["page_table"], "pages_loaded")
            for n in range(4):
                load(W_IN0[:, :, 512 * n:512 * n + 512], I["ev_w_in"][:, :, 512 * n:512 * n + 512], f"w_in0_loaded{n}")
            load(GAIN0, I["gain0"].partition_broadcast(P), "gain0_loaded")

            def even_stores(t, rows):
                s = "prompt" if t < 2 else "sample"
                a, b = (t * P, t * P + P) if t < 2 else (0, NS)
                store(O[f"a_k_{s}"][a:b, :], Z[0:rows, t, 384:768])
                store(O[f"a_v_{s}"][a:b, :], Z[0:rows, t, VA0:QB0])
                store(O[f"b_k_{s}"][a:b, :], Z[0:rows, t, KB0:VB0])
                store(O[f"b_v_{s}"][a:b, :], Z[0:rows, t, VB0:EVEN_IN])

            sp.wait_ge(sem("heads_normed"), 3)
            load(TBL0, I["tbl0"], "tbl0_loaded")
            for t, rows, _ in TILES:
                even_stores(t, rows)
            for b in range(4):
                load(KA[:, b, :, :], I["cache_a_kt"][b], f"ka_loaded{b}")
                load(VA[:, b, :, :], I["cache_a_v"][b], f"va_loaded{b}")
            sp.wait_ge(sem("prompt0_done"), 16)
            load(TBLA, I["tbla"], "tbls_loaded")
            load(TBLB, I["tblb"], "tbls_loaded")
            load(TBLBN, I["tblbn"], "tbls_loaded")

            def pages_of(dst, src, b, name, used, count):
                for j in range(PAGES):
                    page = sp.value_load(pages[0:1, b * PAGES + j:b * PAGES + j + 1], min_val=0, max_val=I["pool_kv"].shape[0] - 1)
                    if j == 0 and used is not None:
                        sp.wait_ge(used, count)
                    for d, s in zip(dst, src):
                        sp.dma_start(d[:, j, :], s[ds(page, 1), :, :].rearrange("a p n -> (a p) n")).then_inc(name, 16)

            sp.wait_ge(sem("pages_loaded"), 16)
            for b in range(2):
                pages_of([KVB[:, b, :, :]], [I["pool_kv"]], b, sem(f"kvb_loaded{b}"), None, 0)
            sp.wait_ge(sem("a_cache_used"), 1)
            for b in range(4, DEC_B):
                load(KA[:, b - 4, :, :], I["cache_a_kt"][b], f"ka_loaded{b - 4}")
                load(VA[:, b - 4, :, :], I["cache_a_v"][b], f"va_loaded{b - 4}")
            for b in range(2, DEC_B):
                pages_of([KVB[:, b % 2, :, :]], [I["pool_kv"]], b, sem(f"kvb_loaded{b % 2}"), sem("b_cache_used"), b // 2)
            sp.wait_ge(sem("a_cache_used"), 2)
            load(W_OUT, I["ev_w_out"], "w_out_loaded")

            def peer_loads(l):
                sp.wait_ge(sem("x_updated"), 2 * l + 1)
                for n in range(4):
                    load(W_Q[:, :, 512 * n:512 * n + 512], I["peer_w_q"][l, :, :, 512 * n:512 * n + 512], f"w_q_loaded{n}")
                load(KEYS, I["peer_k"][l], "keys_loaded")
                sp.wait_ge(sem("h_ready"), 6 * (2 * l + 2))
                for s in range(4):
                    sp.dma_start(SLOTS[:, s, 0, :], I["peer_ut"][l, s]).then_inc(sem(f"u_loaded{s}"), 16)
                    sp.dma_start(SLOTS[:, s, 1, :], I["peer_v"][l, s]).then_inc(sem(f"v_loaded{s}"), 16)
                with sp.Fori(1, NK // 4) as i:
                    for s in range(4):
                        sp.wait_ge(sem("u_split"), i * 4 + (l * NK + s - 3))
                        sp.dma_start(SLOTS[:, s, 0, :], I["peer_ut"][l, ds(i * 4 + s, 1), :, :].rearrange("a p n -> (a p) n")).then_inc(sem(f"u_loaded{s}"), 16)
                        sp.wait_ge(sem("v_split"), i * 4 + (l * NK + s - 3))
                        sp.dma_start(SLOTS[:, s, 1, :], I["peer_v"][l, ds(i * 4 + s, 1), :, :].rearrange("a p n -> (a p) n")).then_inc(sem(f"v_loaded{s}"), 16)

            if live(2):
                peer_loads(0)
            if live(3):
                sp.wait_ge(sem("x_updated"), 2)
                load(W_IN1, I["od_w_in"], "w_in1_loaded")
                load(GROW, I["grow"].partition_broadcast(P), "odd_small_loaded")
                load(GQN, I["mla_g_qn"].partition_broadcast(P), "odd_small_loaded")
                load(GQR, I["mla_g_qr"].partition_broadcast(P), "odd_small_loaded")
                load(GKN, I["mla_g_kn"].partition_broadcast(P), "odd_small_loaded")
                load(GKNP, I["mla_g_kn_col"], "odd_small_loaded")
                load(COS, I["cos"], "odd_small_loaded")
                load(SIN, I["sin"], "odd_small_loaded")
                load(W_UK, I["mla_w_uk"], "odd_small_loaded")
                load(W_UV, I["mla_w_uv"], "odd_small_loaded")
                load(W_UKT, I["mla_w_ukt"], "odd_small_loaded")
                load(W_GLU, I["s5_w_glu"], "odd_small_loaded")
                load(TBLD, I["tbld"], "odd_small_loaded")
                load(S5P[:, 0:3, :], I["s5_par"], "odd_small_loaded")
                load(S0, I["state_c"], "odd_small_loaded")
                load(CBD, I["s5_c"], "odd_small_loaded")
                load(DSKIP, I["s5_d"], "odd_small_loaded")
                load(BGLU, I["s5_b_glu"], "odd_small_loaded")
                sp.wait_ge(sem("h_ready"), 18)
                load(W_UQ, I["mla_w_uq"], "w_uq_loaded")
                sp.wait_ge(sem("latents_ready"), 3)
                for t, rows, _ in TILES:
                    s = "prompt" if t < 2 else "sample"
                    a, b = (t * P, t * P + P) if t < 2 else (0, NS)
                    store(O[f"d_ckv_{s}"][a:b, :], Z2[0:rows, t, CQ:CQ + CKV])
                    store(O[f"d_kpe_{s}"][a:b, :], Z2[0:rows, t, CQ + CKV:])
                sp.wait_ge(sem("prompt1_done"), 8)
                load(BBD, I["s5_b"], "s5_b_loaded")
                sp.wait_ge(sem("y_ready"), 4)
                for k, n in enumerate(("c_re", "c_im")):
                    store(O[f"{n}_prompt"], LASTP[:, k, :])
                    store(O[f"{n}_sample"], LASTS[:, k, :, :])
                load(TBLDN, I["tbldn"], "tbldn_loaded")
                for b in range(DEC_B):
                    pages_of([CKP[:, b % 4, :, :], KPP[:, b % 4, :, :]], [I["pool_ckv"], I["pool_kpe"]], b,
                             sem(f"ckp_loaded{b % 4}"), sem("d_cache_used") if b >= 4 else None, 1)
                sp.wait_ge(sem("d_cache_used"), 2)
                load(W_OUT, I["od_w_out"], "w_out_loaded")
            if live(4):
                peer_loads(1)
            sp.wait_ge(sem("x_updated"), min(stop, 4))
            for t, rows, a in TILES:
                if t < 2:
                    store(O["y_prompt"][a:a + P, :], X[:, t, :])
                else:
                    store(O["y_sample"], X[0:NS, t, :])
            sp.wait_ge(sem("stored"), nst[0])

        @block.tensor
        def _(pe):
            nd, na = [0], [0]

            def to_dve():
                if nd[0] >= 4:
                    pe.wait_ge(d_free, nd[0] - 3)
                nd[0] += 1
                return DB[(nd[0] - 1) % 4]

            def to_act():
                if na[0] >= 4:
                    pe.wait_ge(a_free, na[0] - 3)
                na[0] += 1
                return AB[(na[0] - 1) % 4]

            def mm(out, pairs):
                for n, (lhsT, rhs) in enumerate(pairs):
                    ins = pe.matmul(out, lhsT, rhs, start=(n == 0), stop=(n == len(pairs) - 1))
                return ins

            def norm(k):
                for t, rows, _ in TILES:
                    pe.wait_ge(sem("h_tok_ready"), 3 * k + t + 1)
                    for c in range(2):
                        bank = to_dve()
                        for j in range(4):
                            src = HTOK[0:rows, t, (4 * c + j) * P:(4 * c + j + 1) * P]
                            ins = pe.transpose(bank[:, j * P:j * P + rows], src, ident[0:rows, 0:rows])
                        ins.then_inc(d_full, 1)

            def prompt_attention(units, name, q_of, k_of, v_of, probs, pt):
                def scores(u):
                    pair, qt = u
                    nk = P * (qt + 1)
                    bank = to_dve()
                    for hh in range(2):
                        h = 2 * pair + hh
                        ins = pe.matmul(bank[:, hh * nk:hh * nk + nk], q_of(h, qt), k_of(h, nk), start=True, stop=True)
                    ins.then_inc(d_full, 1)

                def values(n, u):
                    pair, qt = u
                    pe.wait_ge(sem(name + "_probs"), n + 1)
                    bank = to_act()
                    for hh in range(2):
                        for kt in range(qt + 1):
                            ins = pe.transpose(bank[:, (hh * (qt + 1) + kt) * P:(hh * (qt + 1) + kt + 1) * P],
                                               probs[:, n % 2, (hh * (qt + 1) + kt) * P:(hh * (qt + 1) + kt + 1) * P], ident)
                    ins.then_inc(a_full, 1)
                    pe.wait_ge(sem(name + "_pt"), n + 1)
                    bank = to_dve()
                    for hh in range(2):
                        ins = mm(bank[:, hh * HD:hh * HD + HD],
                                 [(pt[:, n % 2, hh * (qt + 1) + kt, :], v_of(2 * pair + hh, kt)) for kt in range(qt + 1)])
                    ins.then_inc(d_full, 1)

                for n in range(len(units) + 1):
                    if n < len(units):
                        scores(units[n])
                    if n >= 1:
                        values(n - 1, units[n - 1])

            def turn_probs(probs, chunks, pt_name, count, chain):
                for c0 in range(0, chunks + 1, 4):
                    bank = to_act()
                    for c in range(c0, min(c0 + 4, chunks + 1)):
                        w = P if c < chunks else NS
                        ins = pe.transpose(bank[0:w, (c - c0) * P:(c - c0 + 1) * P], probs[:, c * P:c * P + w], ident)
                    ins.then_inc(a_full, 1)
                pe.wait_ge(sem(pt_name), count)

            def turn_tokens(src, t, rows, c0, c1, signal_ring):
                for c in range(c0, c1, 4):
                    bank = signal_ring()
                    for j in range(4):
                        ins = pe.transpose(bank[:, j * P:j * P + rows], src(c + j), ident[0:rows, 0:rows])
                    ins.then_inc(a_full if signal_ring is to_act else d_full, 1)

            def out_projection(l, OT):
                pe.wait_ge(sem("w_out_loaded"), 16 * (l + 1))
                pe.wait_ge(sem(f"ot_ready{l}"), 1)
                for t, rows, a in TILES:
                    for n in range(2):
                        bank = to_dve()
                        mm(bank[0:rows, :], [(OT[:, c, a:a + rows], W_OUT[:, c, 512 * n:512 * n + 512]) for c in range(KC)]).then_inc(d_full, 1)

            def peer(l):
                norm(2 * l + 1)
                pe.wait_ge(sem("h_ready"), 6 * (2 * l + 2))
                for m in range(2 * PH):
                    if m % 4 == 0:
                        pe.wait_ge(sem(f"w_q_loaded{m // 4}"), 16 * (l + 1))
                    bank = to_act()
                    mm(bank[:, 0:NT], [(W_Q[:, c, m * P:m * P + P], HT[:, c, :]) for c in range(KC)]).then_inc(a_full, 1)
                pe.wait_ge(sem("keys_loaded"), 16 * (l + 1))
                pe.wait_ge(sem("peer_q_ready"), 16 * (l + 1))
                for t, rows, a in TILES:
                    for c in range(4):
                        bank = to_act()
                        for j in range(4):
                            ins = pe.matmul(bank[0:rows, j * P:j * P + P], QT[:, 4 * c + j, a:a + rows], KEYS[:, 4 * c + j, :], start=True, stop=True)
                        ins.then_inc(a_full, 1)
                for t, rows, a in TILES:
                    pe.wait_ge(sem("route_tok_ready"), 3 * l + t + 1)
                    bank = to_dve()
                    for j in range(3):
                        ins = pe.transpose(bank[:, j * P:j * P + rows], ROUTE[0:rows, j, :], ident[0:rows, 0:rows])
                    ins.then_inc(d_full, 1)
                pe.wait_ge(d_free, nd[0])
                pe.wait_ge(a_free, na[0])
                pe.wait_ge(sem("zeros_ready"), l + 1)
                for k in range(6):
                    pe.matmul(banks[k][:, :], ZEROS[:, 0:P], ZEROS, start=True, stop=False, skip_group_check=True)
                if l == 0:
                    pe.nop().then_inc(sem("one_hots_used"), 2)

                def spread(bank, slot, group):
                    pe.wait_ge(sem("one2_ready"), group + 1)
                    pe.wait_ge(sem("g_copied"), group + (1 if slot is not None else 2))
                    s = slot or 0
                    for j in range(NGT):
                        for e in range(3):
                            ins = pe.matmul(bank[:, j * QK:(j + 1) * QK], ONE1[:, s, j, :], ONE2[:, s, j, e, :], start=(e == 0), stop=(e == 2))
                    ins.then_inc(sem("one_hots_used"), 1)

                with pe.Fori(0, NG // 2) as i:
                    for s in range(2):
                        spread(banks[6 + s], s, i * 2 + (4 * l * NG + s))
                pe.wait_ge(sem("g_copied"), (4 * l + 1) * NG + 2)
                e0 = l * NK

                def hidden(s, e):
                    pe.wait_ge(sem("u_split"), e + 1)
                    pe.wait_ge(sem("hidden_bank_free"), e + 2)
                    bank, k = banks[6][:, 0:NT], s % 2
                    for c in range(KC):
                        uh, ul = UV[:, k, 0, c * P:(c + 1) * P], UV[:, k, 1, c * P:(c + 1) * P]
                        pe.matmul(bank, uh, HR[:, 0, c, :], start=(c == 0), stop=False)
                        pe.matmul(bank, uh, HR[:, 1, c, :], start=False, stop=False)
                        ins = pe.matmul(bank, ul, HR[:, 0, c, :], start=False, stop=(c == KC - 1))
                    ins.then_inc(sem("hidden_full"), 1)

                def values(s, e):
                    pe.wait_ge(sem("v_split"), e + 1)
                    pe.wait_ge(sem("weights_ready"), e * 2 + 2)
                    k = s % 2
                    for t, rows, a in TILES:
                        for wp, vps in ((0, (2, 3)), (1, (2,))) if t < 2 else ((None, (2, 3)),):
                            lhsT = WR[:, k, wp, a:a + rows] if t < 2 else WRS[:, k, :, :].rearrange("p w t -> p (w t)")
                            for vp in vps:
                                for n in range(2):
                                    ins = pe.matmul(banks[2 * t + n][0:P if t < 2 else 2 * NS, :], lhsT, UV[:, k, vp, 512 * n:512 * n + 512],
                                                    start=False, stop=False, skip_group_check=True)
                    ins.then_inc(sem("values_done"), 1)

                pe.wait_ge(sem("h_split"), l + 1)
                hidden(0, e0)
                for q in range(4):
                    def body(i, last):
                        for s in range(4):
                            if not (last and q == 3 and s == 3):
                                hidden((s + 1) % 4, i * 4 + (e0 + q * QK + s + 1))
                            values(s, i * 4 + (e0 + q * QK + s))
                            if s < 3 and q < 3:
                                spread(banks[7], None, i * 3 + ((4 * l + q + 1) * NG + s))
                    with pe.Fori(0, QK // 4 - 1) as i:
                        body(i, False)
                    body(QK // 4 - 1, True)
                pe.wait_ge(sem("mix_copied"), l + 1)
                for n in range(2):
                    ins = mm(banks[6 + n][0:NS, :], [(ident[0:2 * NS, NS * w:NS * w + NS], MIXS[:, n, :]) for w in range(2)])
                    ins.then_inc(sem("sample_mix_full"), 1)

            pe.wait_ge(sem("const_loaded"), 80)
            norm(0)
            pe.wait_ge(sem("h_ready"), 6)
            for n in range(4):
                pe.wait_ge(sem(f"w_in0_loaded{n}"), 16)
                for t, rows, a in TILES:
                    bank = to_act()
                    mm(bank[0:rows, :], [(HT[:, c, a:a + rows], W_IN0[:, c, 512 * n:512 * n + 512]) for c in range(KC)]).then_inc(a_full, 1)

            def normed_col(h):
                return h * HD if h < 2 * AH else QB0 + (h - 2 * AH) * HD

            for t, rows, a in TILES:
                pe.wait_ge(sem("heads_normed"), t + 1)
                for c in range(NORMED // 4):
                    bank = to_act()
                    for j in range(4):
                        col = normed_col(4 * c + j)
                        ins = pe.transpose(bank[0:HD, j * P:j * P + rows], Z[0:rows, t, col:col + HD], ident[0:rows, 0:rows])
                    ins.then_inc(a_full, 1)
            pe.wait_ge(sem("qkt_ready"), 18)
            units0 = [(p, qt) for p in range(8) for qt in range(2)]

            def q0(h, qt):
                return QKT[:, h if h < AH else 2 * AH + h - AH, qt * P:qt * P + P]

            def k0(h, nk):
                return QKT[:, AH + h if h < AH else 2 * AH + BH + (h - AH) // GQ, 0:nk]

            def v0(h, kt):
                col = VA0 + h * HD if h < AH else VB0 + (h - AH) // GQ * HD
                return Z[:, kt, col:col + HD]

            prompt_attention(units0, "prompt0", q0, k0, v0, PP_, PTP)
            pe.wait_ge(sem("prompt0_done"), 16)
            for t in range(2):
                turn_tokens(lambda c: O0[:, t, c * P:c * P + P], t, P, 0, 8, to_act)
            pe.wait_ge(sem("q_spread"), 1)
            for r in range(2):
                for i in range(4):
                    pe.wait_ge(sem(f"ka_loaded{i}"), 16 * (r + 1))
                for cols, knew in (((0, 512), False), ((512, AK), True)):
                    bank = to_dve()
                    w = cols[1] - cols[0]
                    for i in range(4):
                        rows = slice(32 * i, 32 * i + 32)
                        b = 4 * r + i
                        ins = mm(bank[rows, 0:w], [(QBA[:, c, b, :], KA[:, i, c, cols[0]:cols[1]]) for c in range(3)])
                        if knew:
                            ins = mm(bank[rows, w:w + NS], [(QBA[:, c, b, :], KNA[:, c, :]) for c in range(3)])
                    ins.then_inc(d_full, 1)
                pe.wait_ge(sem("sa_probs"), r + 1)
                turn_probs(SS_, AKC, "sa_pt", 2 * (r + 1), None)
                bank = to_dve()
                for i in range(4):
                    pe.wait_ge(sem(f"va_loaded{i}"), 16 * (r + 1))
                    for c in range(3):
                        at = 24 * i + 8 * c
                        rows = slice(32 * i + 8 * c, 32 * i + 8 * c + 8)
                        ins = mm(bank[:, at:at + 8], [(VA[:, i, k, c * P:c * P + P], PTS[:, k, rows]) for k in range(AKC)]
                                 + [(Z[0:NS, 2, VA0 + c * P:VA0 + c * P + P], PTS[0:NS, AKC, rows])])
                ins.then_inc(d_full, 1)
            for r in range(4):
                for i in range(2):
                    pe.wait_ge(sem(f"kvb_loaded{i}"), 16 * PAGES * (r + 1))
                for c in range(3):
                    bank = to_dve()
                    for i in range(2):
                        rows = slice(64 * i, 64 * i + 64)
                        b = 2 * r + i
                        if c < 2:
                            ins = pe.matmul(bank[rows, :].rearrange("p (j n) -> p j n", n=P), QBB[:, b, :], KVB[:, i, 4 * c:4 * c + 4, 0:P], start=True, stop=True)
                        else:
                            ins = pe.matmul(bank[rows, 0:NS], QBB[:, b, :], KNB, start=True, stop=True)
                    ins.then_inc(d_full, 1)
                pe.wait_ge(sem("gate_ready"), r + 1)
                bank = to_dve()
                pe.matmul(bank[:, 0:NBLK], group, GATE, start=True, stop=True).then_inc(d_full, 1)
                pe.wait_ge(sem("sb_probs"), r + 1)
                turn_probs(SS_, PAGES, "sb_pt", 3 * (r + 1), None)
                bank = to_dve()
                for i in range(2):
                    rows = slice(64 * i, 64 * i + 64)
                    ins = mm(bank[:, 64 * i:64 * i + 64], [(KVB[:, i, k, P:2 * P], PTS[:, k, rows]) for k in range(PAGES)]
                             + [(Z[0:NS, 2, VB0:EVEN_IN], PTS[0:NS, PAGES, rows])])
                ins.then_inc(d_full, 1)
            out_projection(0, OT0)
            if live(2):
                peer(0)

            def odd():
                norm(2)
                pe.wait_ge(sem("h_ready"), 18)
                pe.wait_ge(sem("w_in1_loaded"), 16)
                for t, rows, a in TILES:
                    bank = to_act()
                    mm(bank[0:rows, 0:416], [(HT[:, c, a:a + rows], W_IN1[:, c, 512:928]) for c in range(KC)]).then_inc(a_full, 1)
                for m in range(4):
                    bank = to_act()
                    mm(bank[:, 0:NT], [(W_IN1[:, c, m * P:m * P + P], HT[:, c, :]) for c in range(KC)]).then_inc(a_full, 1)
                for t, rows, a in TILES:
                    pe.wait_ge(sem("latents_ready"), t + 1)
                    bank = to_dve()
                    for j in range(3):
                        ins = pe.transpose(bank[:, j * P:j * P + rows], Z2[0:rows, t, j * P:j * P + P], ident[0:rows, 0:rows])
                    ins.then_inc(d_full, 1)
                pe.wait_ge(sem("latents_turned"), 3)
                pe.wait_ge(sem("w_uq_loaded"), 16)
                pe.wait_ge(sem("odd_small_loaded"), 16 * 17)
                for t, rows, a in TILES:
                    for n in range(2):
                        bank = to_act()
                        mm(bank[0:rows, 0:384], [(CQT[:, c, a:a + rows], W_UQ[:, c, 384 * n:384 * n + 384]) for c in range(2)]).then_inc(a_full, 1)
                    for w in (W_UK, W_UV):
                        bank = to_act()
                        pe.matmul(bank[0:rows, :], CKT[:, a:a + rows], w, start=True, stop=True).then_inc(a_full, 1)
                for t, rows, a in TILES:
                    pe.wait_ge(sem("qk_ready"), t + 1)
                    for src in (Q, KCAT):
                        if src is KCAT and t == 2:
                            continue
                        for c in range(2):
                            bank = to_act()
                            for j in range(4):
                                ins = pe.transpose(bank[0:DQK, j * P:j * P + rows], src[0:rows, t, 4 * c + j, :], ident[0:rows, 0:rows])
                            ins.then_inc(a_full, 1)
                pe.wait_ge(sem("qct_ready"), 10)
                units = [(p, qt) for p in range(4) for qt in range(2)]
                prompt_attention(units, "prompt1", lambda h, qt: QCT[:, h, qt * P:qt * P + P], lambda h, nk: KCT[:, h, 0:nk],
                                 lambda h, kt: VD[:, kt, h * HD:h * HD + HD], P_D, PT_D)
                pe.wait_ge(sem("prompt1_done"), 8)
                for t in range(2):
                    turn_tokens(lambda c: O1[:, t, c * P:c * P + P], t, P, 0, 4, to_act)
                pe.wait_ge(sem("s5_b_scaled"), 1)
                for k in range(2):
                    bank = to_act()
                    for j in range(4):
                        ins = pe.transpose(bank[:, j * P:j * P + P], BSC[:, k, 4 * j:4 * j + 4, :].rearrange("p s c -> p (s c)"), ident)
                    ins.then_inc(a_full, 1)
                pe.wait_ge(sem("s5_bt_ready"), 2)
                for hf in range(2):
                    for s in range(SG2 * hf, SG2 * hf + SG2):
                        rows = slice(32 * (s % 4), 32 * (s % 4) + 32)
                        for k in range(2):
                            bank = to_act()
                            pe.matmul(bank[:, 0:NT], BT[rows, k, s // 4, :], UT[rows, s // 4, :], start=True, stop=True).then_inc(a_full, 1)
                    pe.wait_ge(sem("states_ready"), hf + 1)
                    for c in range(2 * hf, 2 * hf + 2):
                        bank = to_dve()
                        for q in range(4):
                            s = 4 * c + q
                            rows = slice(32 * q, 32 * q + 32)
                            ins = mm(bank[rows, 0:NT], [(CBD[:, k, s, :], BU[:, k, s % SG2, :]) for k in range(2)])
                        ins.then_inc(d_full, 1)
                pe.wait_ge(sem("zg_ready"), 4)
                for m in range(4):
                    bank = to_act()
                    mm(bank[:, 0:NT], [(W_GLU[:, c, m * P:m * P + P], ZG[:, c, :]) for c in range(4)]).then_inc(a_full, 1)
                pe.wait_ge(sem("qg_ready"), 1)
                bank = to_dve()
                for h in range(DH):
                    ins = pe.matmul(bank[:, h * NS:h * NS + NS], W_UKT[:, h, :], QG[:, h, :], start=True, stop=True)
                ins.then_inc(d_full, 1)
                pe.wait_ge(sem("qabs_ready"), 1)
                for r in range(2):
                    for i in range(4):
                        pe.wait_ge(sem(f"ckp_loaded{i}"), 32 * PAGES * (r + 1))
                        for j in range(PAGES):
                            bank = to_act()
                            pe.matmul(bank[:, :], CKP[:, i, j, 0:P], W_UK, start=True, stop=True).then_inc(a_full, 1)
                    pe.wait_ge(sem("rkx_ready"), 4 * (r + 1))
                    for c in range(3):
                        bank = to_dve()
                        for i in range(4):
                            rows = slice(32 * i, 32 * i + 32)
                            if c < 2:
                                for j in range(4 * c, 4 * c + 4):
                                    ins = pe.matmul(bank[rows, (j % 4) * P:(j % 4 + 1) * P], RKX[:, i, j, :], ident, start=True, stop=True)
                            else:
                                ins = pe.matmul(bank[rows, 0:NS], RKN[0:NS, :, :].rearrange("p h t -> p (h t)"), ident[0:NS, 0:NS], start=True, stop=True)
                        ins.then_inc(d_full, 1)
                    for lat in (True, False):
                        for c in range(3):
                            bank = to_dve()
                            for i in range(4):
                                rows = slice(32 * i, 32 * i + 32)
                                b = 4 * r + i
                                q = (QABS if lat else QPE)[:, b, :, :].rearrange("p h t -> p (h t)")
                                if c < 2:
                                    key = CKP[:, i, 4 * c:4 * c + 4, 0:P] if lat else KPP[:, i, 4 * c:4 * c + 4, :]
                                    ins = pe.matmul(bank[rows, :].rearrange("p (j n) -> p j n", n=P), q, key, start=True, stop=True)
                                else:
                                    ins = pe.matmul(bank[rows, 0:NS], q, CKT[:, SEQ:NT] if lat else KPEN, start=True, stop=True)
                            ins.then_inc(d_full, 1)
                    pe.wait_ge(sem("sd_probs"), r + 1)
                    turn_probs(S_SD, PAGES, "sd_pt", 3 * (r + 1), None)
                    bank = to_dve()
                    for i in range(4):
                        rows = slice(32 * i, 32 * i + 32)
                        ins = mm(bank[:, rows], [(CKP[:, i, k, P:2 * P], PT_SD[:, k, rows]) for k in range(PAGES)]
                                 + [(Z2[0:NS, 2, CQ:CQ + CKV], PT_SD[0:NS, PAGES, rows])])
                    ins.then_inc(d_full, 1)
                pe.wait_ge(sem("ct_ready"), 2)
                bank = to_dve()
                for h in range(DH):
                    ins = pe.matmul(bank[0:NS, h * HD:h * HD + HD], CT[:, h, :], W_UV[:, h * HD:h * HD + HD], start=True, stop=True)
                ins.then_inc(d_full, 1)
                pe.wait_ge(sem("o1_sample_ready"), 1)
                turn_tokens(lambda c: S_SD[0:NS, c * P:c * P + P], 2, NS, 0, 4, to_act)
                out_projection(1, OT1)

            if live(3):
                odd()
            if live(4):
                peer(1)

        @block.scalar
        def _(act):
            nf, chain, done = [0], [0], {}

            def full():
                act.wait_ge(a_full, nf[0] + 1)
                nf[0] += 1
                return AB[(nf[0] - 1) % 4]

            def link(ins):
                chain[0] += 1
                ins.then_inc(sem("act_step"), 1)
                act.wait_ge(sem("act_step"), chain[0])

            def copy_out(out, src, name):
                link(act.copy(out, src))
                act.nop().then_inc(a_free, 1)
                act.nop().then_inc(sem(name), 1)

            def norm(k):
                if k == 0:
                    act.wait_ge(sem("x_loaded"), 48)
                    act.wait_ge(sem("ss_set"), 1)
                else:
                    act.wait_ge(sem("x_updated"), k)
                for t, rows, _ in TILES:
                    ins = act.activation(HTOK[0:rows, t, :], X[0:rows, t, :], ACT.Square, accum_out=ss[0:rows, t:t + 1])
                    ins.then_inc(sem("squares_ready"), 1)
                act.wait_ge(sem("norm_var"), k + 1)
                act.activation(rinv, rinv, ACT.Sqrt).then_inc(sem("norm_rinv"), 1)

            def exps_prompt(units, name, src, dst, scale):
                for n in range(len(units) + 1):
                    if n < len(units):
                        pair, qt = units[n]
                        nk = P * (qt + 1)
                        act.wait_ge(sem(name + "_scores"), n + 1)
                        if n >= 2:
                            act.wait_ge(sem(name + "_done"), n - 1)
                        for hh in range(2):
                            ins = act.activation(dst[:, n % 2, hh * nk:hh * nk + nk], src[:, n % 2, hh * nk:hh * nk + nk], ACT.Exp,
                                                 bias=MX[:, n % 2, hh:hh + 1], scale=scale, accum_out=SUMS[:, n % 2, hh:hh + 1])
                            if hh == 0:
                                link(ins)
                        ins.then_inc(sem(name + "_probs"), 1)
                    if n >= 1:
                        pair, qt = units[n - 1]
                        bank = full()
                        w = 2 * (qt + 1) * P
                        pt = PTP if name == "prompt0" else PT_D
                        copy_out(pt[:, (n - 1) % 2, 0:2 * (qt + 1), :].rearrange("p a b -> p (a b)"), bank[:, 0:w], name + "_pt")

            def sample_softmax(scores, width, name, pt, chunks, r, scale):
                act.wait_ge(sem(name + "_scores"), r + 1)
                act.activation(scores[:, 0:width], scores[:, 0:width], ACT.Exp, bias=MX1, scale=scale, accum_out=SUM1).then_inc(sem(name + "_exp"), 1)
                for c0 in range(0, chunks + 1, 4):
                    bank = full()
                    c1 = min(c0 + 4, chunks)
                    if c1 > c0:
                        ins = act.copy(pt[:, c0:c1, :].rearrange("p a b -> p (a b)"), bank[:, 0:(c1 - c0) * P])
                    if c0 + 4 > chunks:
                        if c1 > c0:
                            link(ins)
                        ins = act.copy(pt[0:NS, chunks, :], bank[0:NS, (chunks - c0) * P:(chunks - c0 + 1) * P])
                    link(ins)
                    act.nop().then_inc(a_free, 1)
                    act.nop().then_inc(sem(name + "_pt"), 1)

            def peer(l):
                norm(2 * l + 1)
                for m in range(2 * PH):
                    copy_out(QT[:, m, :], full()[:, 0:NT], "peer_q_ready")
                for t, rows, a in TILES:
                    if t >= 1:
                        act.wait_ge(sem("scores_used"), 3 * l + t)
                    for c in range(4):
                        copy_out(SC[0:rows, 4 * c:4 * c + 4, :].rearrange("p a b -> p (a b)"), full()[0:rows, :], "peer_scores")
                    act.wait_ge(sem("sel_diff"), 3 * l + t + 1)
                    act.activation(ROUTE[0:rows, 2, :], ROUTE[0:rows, 2, :], ACT.Exp).then_inc(sem("sel_exp"), 1)
                if l == 0:
                    act.nop().then_inc(sem("g_copied"), 2)
                    act.nop().then_inc(sem("hidden_bank_free"), 2)
                act.wait_ge(sem("pieces_ready"), l + 1)
                e0 = l * NK

                def g_copy(bank, row, t0, group):
                    act.wait_ge(sem("one_hots_used"), group + 3)
                    act.copy(G[:, row:row + QK, ds(t0, NGT)].rearrange("p j t -> p t j"),
                             bank[:, 0:NGT * QK].rearrange("p (t j) -> p t j", j=QK)).then_inc(sem("g_copied"), 1)

                def u_high(s, e):
                    act.wait_ge(sem(f"u_loaded{s}"), e * 4 + (16 - 4 * s))
                    act.wait_ge(sem("hidden_full"), e + 1)
                    act.copy(UV[:, s % 2, 0, :], SLOTS[:, s, 0, :]).then_inc(sem("u_high"), 1)

                def v_high(s, e):
                    act.wait_ge(sem(f"v_loaded{s}"), e * 4 + (16 - 4 * s))
                    act.wait_ge(sem("values_done"), e + 1)
                    act.copy(UV[:, s % 2, 2, :], SLOTS[:, s, 1, :]).then_inc(sem("v_high"), 1)

                def hidden_act(s, e):
                    act.wait_ge(sem("hidden_full"), e + 3)
                    act.wait_ge(sem("actv_free"), e + 1)
                    act.activation(ACTV[:, s % 2, :], banks[6][:, 0:NT], ACT.Gelu_apprx_tanh).then_inc(sem("hidden_bank_free"), 1)

                if l == 0:
                    act.nop().then_inc(sem("hidden_full"), 2)
                    act.nop().then_inc(sem("values_done"), 2)
                u_high(0, e0)
                u_high(1, e0 + 1)
                v_high(0, e0)
                with act.Fori(0, NG // 2) as i:
                    for s in range(2):
                        g_copy(banks[6 + s], 0, i * (2 * NGT) + s * NGT, i * 2 + (4 * l * NG + s))
                hidden_act(0, e0)
                for q in range(4):
                    def body(i, last):
                        for s in range(4):
                            e = i * 4 + (e0 + q * QK + s)
                            end = last and q == 3
                            if not (end and s >= 2):
                                u_high((s + 2) % 4, e + 2)
                            if not (end and s == 3):
                                v_high((s + 1) % 4, e + 1)
                            if s >= 1 and q < 3:
                                g_copy(banks[7], (q + 1) % 2 * QK, (i * 3 + (s - 1)) * NGT, i * 3 + ((4 * l + q + 1) * NG + s - 1))
                            if not (end and s == 3):
                                hidden_act((s + 1) % 4, e + 1)
                    with act.Fori(0, QK // 4 - 1) as i:
                        body(i, False)
                    body(QK // 4 - 1, True)
                act.wait_ge(sem("values_done"), (l + 1) * NK + 2)
                for n in range(2):
                    link(act.copy(MIXS[:, n, :], banks[4 + n][0:2 * NS, :]))
                act.nop().then_inc(sem("mix_copied"), 1)

            norm(0)
            for n in range(4):
                for t, rows, a in TILES:
                    copy_out(Z[0:rows, t, 512 * n:512 * n + 512], full()[0:rows, :], "z_ready")
            for t, rows, a in TILES:
                act.wait_ge(sem("heads_var"), t + 1)
                act.activation(RS24[0:rows, :], RS24[0:rows, :], ACT.Sqrt).then_inc(sem("heads_rinv"), 1)
            for t, rows, a in TILES:
                for c in range(NORMED // 4):
                    copy_out(QKT[:, 4 * c:4 * c + 4, a:a + rows], full()[0:HD, :].rearrange("p (j n) -> p j n", n=P)[:, :, 0:rows], "qkt_ready")
            units0 = [(p, qt) for p in range(8) for qt in range(2)]
            exps_prompt(units0, "prompt0", SP_, PP_, 1.0)
            for t in range(2):
                for c in range(2):
                    copy_out(OT0[:, 4 * c:4 * c + 4, t * P:t * P + P], full()[:, :].rearrange("p (j n) -> p j n", n=P), "ot0_prompt")
            for r in range(2):
                sample_softmax(SS_, AK + NS, "sa", PTS, AKC, r, 1.0)
            for r in range(4):
                sample_softmax(SS_, PAST + NS, "sb", PTS, PAGES, r, 1.0)
            act.wait_ge(sem("ot0_sample"), 1)
            act.nop().then_inc(sem("ot_ready0"), 1)
            if live(2):
                peer(0)

            def odd():
                norm(2)
                for t, rows, a in TILES:
                    copy_out(Z2[0:rows, t, :], full()[0:rows, 0:416], "z2_ready")
                for m in range(4):
                    copy_out(UT[:, m, :], full()[:, 0:NT], "ut_ready")
                for t, rows, a in TILES:
                    act.wait_ge(sem("latent_var"), t + 1)
                    act.activation(ST8I[0:rows, t, 0:3], ST8[0:rows, t, 0:3], ACT.Sqrt).then_inc(sem("latent_rinv"), 1)
                for t, rows, a in TILES:
                    for n in range(2):
                        copy_out(Q[0:rows, t, 4 * n:4 * n + 4, :].rearrange("p a b -> p (a b)"), full()[0:rows, 0:384], "qkv_ready")
                    copy_out(KR[0:rows, t, :], full()[0:rows, :], "qkv_ready")
                    copy_out(VD[0:rows, t, :], full()[0:rows, :], "qkv_ready")
                for t, rows, a in TILES:
                    act.wait_ge(sem("qk_var"), t + 1)
                    act.activation(ST8I[0:rows, t, 0:24], ST8[0:rows, t, 0:24], ACT.Sqrt).then_inc(sem("qk_rinv"), 1)
                for t, rows, a in TILES:
                    for dst in (QCT, KCT):
                        if dst is KCT and t == 2:
                            continue
                        for c in range(2):
                            copy_out(dst[:, 4 * c:4 * c + 4, a:a + rows], full()[0:DQK, :].rearrange("p (j n) -> p j n", n=P)[:, :, 0:rows], "qct_ready")
                units = [(p, qt) for p in range(4) for qt in range(2)]
                exps_prompt(units, "prompt1", S_D, P_D, SCALE_D)
                for t in range(2):
                    copy_out(OT1[:, 4:8, t * P:t * P + P], full()[:, :].rearrange("p (j n) -> p j n", n=P), "ot1_prompt")
                act.wait_ge(sem("odd_small_loaded"), 16 * 17)
                act.activation(S5P[:, 3, :], S5P[:, 2, :], ACT.Exp).then_inc(sem("s5_dt"), 1)
                act.wait_ge(sem("s5_angles"), 1)
                act.activation(S5P[:, 7, :], S5P[:, 4, :], ACT.Exp).then_inc(sem("s5_mag"), 1)
                act.activation(S5P[:, 8, :], S5P[:, 6, :], ACT.Sin).then_inc(sem("s5_mag"), 1)
                act.activation(S5P[:, 9, :], S5P[:, 5, :], ACT.Sin).then_inc(sem("s5_mag"), 1)
                for k in range(2):
                    copy_out(BT[:, k, :, :].rearrange("p a b -> p (a b)"), full()[:, :], "s5_bt_ready")
                for hf in range(2):
                    if hf == 1:
                        act.wait_ge(sem("y_ready"), 2)
                    for s in range(SG2):
                        for k in range(2):
                            copy_out(BU[:, k, s, :], full()[:, 0:NT], "bu_ready")
                act.wait_ge(sem("y_ready"), 4)
                for m in range(4):
                    act.activation(ZG[:, m, :], Y[:, m, :], ACT.Gelu_apprx_tanh).then_inc(sem("zg_ready"), 1)
                for m in range(4):
                    bank = full()
                    link(act.activation(SGM[:, m, :], bank[:, 0:NT], ACT.Sigmoid, bias=BGLU[:, m:m + 1]))
                    act.nop().then_inc(a_free, 1)
                    act.nop().then_inc(sem("sgm_ready"), 1)
                for r in range(2):
                    for i in range(4):
                        for j in range(PAGES):
                            n = (4 * r + i) * PAGES + j
                            bank = full()
                            if n >= 2:
                                act.wait_ge(sem("sqd_used"), n - 1)
                            link(act.activation(SQD[:, n % 2, :], bank[:, :], ACT.Square))
                            act.nop().then_inc(a_free, 1)
                            act.nop().then_inc(sem("sqd_ready"), 1)
                        act.wait_ge(sem("rk_var"), 4 * r + i + 1)
                        act.activation(RKS[:, i, :, :], RKS[:, i, :, :], ACT.Sqrt).then_inc(sem("rk_rinv"), 1)
                    sample_softmax(S_SD, PAST + NS, "sd", PT_SD, PAGES, r, SCALE_D)
                act.wait_ge(sem("qabs_ready"), 1)
                bank = full()
                link(act.copy(OT1[:, 4:8, SEQ:NT], bank[:, :].rearrange("p (j n) -> p j n", n=P)[:, :, 0:NS]))
                act.nop().then_inc(a_free, 1)
                act.wait_ge(sem("oc_ready"), 4)
                act.nop().then_inc(sem("ot_ready1"), 1)

            if live(3):
                odd()
            if live(4):
                peer(1)

        @block.vector
        def _(dve):
            nf, chain = [0], [0]

            def full():
                dve.wait_ge(d_full, nf[0] + 1)
                nf[0] += 1
                return DB[(nf[0] - 1) % 4]

            def free():
                dve.nop().then_inc(d_free, 1)

            def step(ins):
                chain[0] += 1
                ins.then_inc(sem("dve_step"), 1)

            def settle():
                dve.wait_ge(sem("dve_step"), chain[0])

            def link(ins):
                step(ins)
                settle()

            def say(name, n=1):
                dve.nop().then_inc(sem(name), n)

            def TT(out, a, b, op):
                link(dve.tensor_tensor(out, a, b, op))

            def TS(out, a, s1, s2, op0, op1=None):
                link(dve.tensor_scalar(out, a, s1, s2, op0, op1) if op1 is not None else dve.tensor_scalar(out, a, s1, None, op0))

            def STT(out, a, s, b, op0, op1):
                link(dve.scalar_tensor_tensor(out=out, in0=a, scalar=s, in1=b, op0=op0, op1=op1))

            def norm(k):
                dve.wait_ge(sem("squares_ready"), 3 * (k + 1))
                TS(rinv, ss, 1.0 / D, EPS, ALU.mult, ALU.add)
                link(dve.reciprocal(rinv, rinv))
                say("norm_var")
                dve.wait_ge(sem("norm_rinv"), k + 1)
                for t, rows, _ in TILES:
                    TS(HTOK[0:rows, t, :], X[0:rows, t, :], rinv[0:rows, t:t + 1], None, ALU.mult)
                    say("h_tok_ready")
                for t, rows, a in TILES:
                    for c in range(2):
                        bank = full()
                        TT(HT[:, 4 * c:4 * c + 4, a:a + rows], bank[:, :].rearrange("p (j n) -> p j n", n=P)[:, :, 0:rows],
                           bc(gain[:, k, 4 * c:4 * c + 4], 2, rows), ALU.mult)
                        free()
                        say("h_ready")

            def prompt_attention(units, name, scores, tables, out, scale):
                def first(n):
                    pair, qt = units[n]
                    nk = P * (qt + 1)
                    bank = full()
                    s = scores[:, n % 2, 0:2 * nk]
                    if n >= 2:
                        dve.wait_ge(sem(name + "_probs"), n - 1)
                    tables(s, bank, pair, qt, nk)
                    free()
                    link(dve.tensor_reduce(MX[:, n % 2, :], s.rearrange("p (h k) -> p h k", h=2), AX, ALU.max, negate=True))
                    if scale != 1.0:
                        TS(MX[:, n % 2, :], MX[:, n % 2, :], scale, None, ALU.mult)
                    say(name + "_scores")

                def second(n):
                    pair, qt = units[n]
                    dve.wait_ge(sem(name + "_probs"), n + 1)
                    link(dve.reciprocal(RSUM, SUMS[:, n % 2, :]))
                    bank = full()
                    TT(out[:, qt, pair * P:pair * P + P].rearrange("p (h d) -> p h d", h=2), bank[:, 0:P].rearrange("p (h d) -> p h d", h=2),
                       bc(RSUM, 2, HD), ALU.mult)
                    free()
                    say(name + "_done")

                for n in range(len(units) + 1):
                    if n < len(units):
                        first(n)
                    if n >= 1:
                        second(n - 1)

            def softmax_rows(scores, width, name, r, scale):
                link(dve.tensor_reduce(MX1, scores[:, 0:width], AX, ALU.max, negate=True))
                if scale != 1.0:
                    TS(MX1, MX1, scale, None, ALU.mult)
                say(name + "_scores")
                dve.wait_ge(sem(name + "_exp"), r + 1)
                link(dve.reciprocal(SUM1, SUM1))
                TS(scores[:, 0:width], scores[:, 0:width], SUM1, None, ALU.mult)
                say(name + "_probs")

            def add_to_x(k):
                for t, rows, a in TILES:
                    for n in range(2):
                        bank = full()
                        TT(X[0:rows, t, 512 * n:512 * n + 512], X[0:rows, t, 512 * n:512 * n + 512], bank[0:rows, :], ALU.add)
                        free()
                say("x_updated")

            def top16(values, rest, top, index, groups, rows):
                for g in groups:
                    step(dve.max(top(g)[:, 0:8], values(g)))
                settle()
                for g in groups:
                    step(dve.match_replace(rest(g), top(g)[:, 0:8], values(g), NEG))
                    step(dve.max_index(index(g)[:, 0:8], top(g)[:, 0:8], values(g)))
                settle()
                for g in groups:
                    step(dve.max(top(g)[:, 8:16], rest(g)))
                settle()
                for g in groups:
                    step(dve.max_index(index(g)[:, 8:16], top(g)[:, 8:16], rest(g)))
                settle()

            def peer(l):
                norm(2 * l + 1)
                for t, rows, a in TILES:
                    R = slice(0, rows)
                    dve.wait_ge(sem("peer_scores"), 12 * l + 4 * (t + 1))
                    top16(lambda g: SC[R, g, :], lambda g: SC2[R, g, :], lambda g: TOPV[R, g // 2, g % 2, :],
                          lambda g: TOPI[R, g // 2, g % 2, :], range(2 * PH), rows)
                    say("scores_used")
                    TT(CAND[R], bc(TOPV[R, :, 0, :], 3, TOPK), bc(TOPV[R, :, 1, :], 2, TOPK), ALU.add)
                    step(dve.tensor_copy(TOPIF[R], TOPI[R]))
                    top16(lambda g: CAND[R, g, :, :].rearrange("p a b -> p (a b)"), lambda g: CAND2[R, g, :, :].rearrange("p a b -> p (a b)"),
                          lambda g: SELV[R, g, :], lambda g: SELJ[R, g, :], range(PH), rows)
                    if t >= 1:
                        dve.wait_ge(sem("route_ready"), 3 * l + t)
                    TT(ROUTE[R, 2, :].rearrange("p (h k) -> p h k", h=PH), SELV[R], SELV[R, :, 0:1].broadcast_to([rows, PH, TOPK]), ALU.subtract)
                    say("sel_diff")
                    step(dve.tensor_scalar(SELAB[R, 0], SELJ[R], 4, None, ALU.logical_shift_right))
                    step(dve.tensor_scalar(SELAB[R, 1], SELJ[R], 15, None, ALU.bitwise_and))
                    settle()
                    link(dve.tensor_copy(SELABF[R], SELAB[R]))
                    for k in range(2):
                        TT(EQ[R].rearrange("p h k c -> p (h k) c"), bc(SELABF[R, k].rearrange("p h k -> p (h k)"), 2, TOPK),
                           bc(iota[R, 0:TOPK], 1, PH * TOPK), ALU.is_equal)
                        TT(EQ[R], EQ[R], bc(TOPIF[R, :, k, :], 2, TOPK), ALU.mult)
                        link(dve.tensor_reduce(ROUTE[R, k, :], EQ[R].rearrange("p h k c -> p (h k) c"), AX, ALU.add))
                    dve.wait_ge(sem("sel_exp"), 3 * l + t + 1)
                    gw = ROUTE[R, 2, :].rearrange("p (h k) -> p h k", h=PH)
                    link(dve.tensor_reduce(GSUM[R], gw, AX, ALU.add))
                    link(dve.reciprocal(GSUM[R], GSUM[R]))
                    TT(gw, gw, bc(GSUM[R], 2, TOPK), ALU.mult)
                    say("route_tok_ready")
                    bank = full()
                    link(dve.tensor_copy(ROUTET[:, :, a:a + rows], bank[:, 0:3 * P].rearrange("p (j n) -> p j n", n=P)[:, :, 0:rows]))
                    free()
                    say("route_ready")
                link(dve.memset(ZEROS, 0.0))
                say("zeros_ready")
                if l == 0:
                    say("actv_free", 2)
                g, rest = ROUTET[:, 2, :], WFULL[:, 0, :]
                link(dve.tensor_copy(PIECES[:, 0, :], ROUTET[:, 1, :]))
                link(dve.tensor_copy(PIECES[:, 4, :], ROUTET[:, 0, :]))
                link(dve.tensor_copy(PIECES[:, 1, :], g))
                TT(rest, g, PIECES[:, 1, :], ALU.subtract)
                link(dve.tensor_copy(PIECES[:, 2, :], rest))
                TT(rest, rest, PIECES[:, 2, :], ALU.subtract)
                link(dve.tensor_copy(PIECES[:, 3, :], rest))
                say("pieces_ready")
                e0 = l * NK

                def u_low(s, e):
                    dve.wait_ge(sem("u_high"), e + 1)
                    dve.tensor_tensor(UV[:, s % 2, 1, :], SLOTS[:, s, 0, :], UV[:, s % 2, 0, :].bitcast(F32), ALU.subtract).then_inc(sem("u_split"), 1)

                def v_low(s, e):
                    dve.wait_ge(sem("v_high"), e + 1)
                    dve.tensor_tensor(UV[:, s % 2, 3, :], SLOTS[:, s, 1, :], UV[:, s % 2, 2, :].bitcast(F32), ALU.subtract).then_inc(sem("v_split"), 1)

                def one_hots(t0, slot, group):
                    dve.wait_ge(sem("one_hots_used"), group + (1 if slot is not None else 2))
                    s = slot or 0
                    q = q_of[0]
                    dve.tensor_tensor(ONE1[:, s], bc(PIECES[:, 4, ds(t0, NGT)], 2, NK), bc(iota, 1, NGT), ALU.is_equal)
                    dve.tensor_tensor(EQ2, bc(PIECES[:, 0, ds(t0, NGT)], 2, QK), bc(iota[:, QK * q:QK * q + QK], 1, NGT), ALU.is_equal).then_inc(sem("eq2_ready"), 1)
                    dve.wait_ge(sem("eq2_ready"), group + 1)
                    dve.tensor_tensor(ONE2[:, s], bc(EQ2, 2, 3), bc(PIECES[:, 1:4, ds(t0, NGT)].rearrange("p e t -> p t e"), 3, QK), ALU.mult)\
                       .then_inc(sem("one2_ready"), 1)
                    dve.wait_ge(sem("one2_ready"), group + 1)

                def weights(s, e, row):
                    k = s % 2
                    dve.wait_ge(sem("hidden_bank_free"), e + 3)
                    dve.wait_ge(sem("values_done"), e + 1)
                    dve.tensor_tensor(WFULL[:, k, :], ACTV[:, k, :], G[:, ds(row, 1), :].rearrange("p a t -> p (a t)"), ALU.mult).then_inc(sem("w_full"), 1)
                    dve.wait_ge(sem("w_full"), e + 1)
                    dve.tensor_copy(WR[:, k, 0, :], WFULL[:, k, 0:SEQ]).then_inc(sem("w_high"), 1)
                    dve.tensor_copy(WRS[:, k, 0, :], WFULL[:, k, SEQ:NT]).then_inc(sem("actv_free"), 1)
                    dve.wait_ge(sem("w_high"), e + 1)
                    dve.tensor_tensor(WR[:, k, 1, :], WFULL[:, k, 0:SEQ], WR[:, k, 0, :].bitcast(F32), ALU.subtract).then_inc(sem("weights_ready"), 1)
                    dve.wait_ge(sem("actv_free"), e + 3)
                    dve.tensor_tensor(WRS[:, k, 1, :], WFULL[:, k, SEQ:NT], WRS[:, k, 0, :].bitcast(F32), ALU.subtract).then_inc(sem("weights_ready"), 1)

                q_of = [0]
                link(dve.tensor_copy(HR[:, 0], HT))
                TT(HR[:, 1], HT, HR[:, 0].bitcast(F32), ALU.subtract)
                say("h_split")
                u_low(0, e0)
                u_low(1, e0 + 1)
                v_low(0, e0)
                with dve.Fori(0, NG // 2) as i:
                    for s in range(2):
                        one_hots(i * (2 * NGT) + s * NGT, s, i * 2 + (4 * l * NG + s))
                dve.wait_ge(sem("g_copied"), (4 * l + 1) * NG + 2)
                weights(0, e0, 0)
                for q in range(4):
                    q_of[0] = q + 1

                    def body(i, last):
                        for s in range(4):
                            e = i * 4 + (e0 + q * QK + s)
                            end = last and q == 3
                            if not (end and s >= 2):
                                u_low((s + 2) % 4, e + 2)
                            if not (end and s == 3):
                                v_low((s + 1) % 4, e + 1)
                            if s < 3 and q < 3:
                                one_hots((i * 3 + s) * NGT, None, i * 3 + ((4 * l + q + 1) * NG + s))
                            if last and s == 3 and q < 3:
                                dve.wait_ge(sem("g_copied"), (4 * l + q + 2) * NG + 2)
                            if not (end and s == 3):
                                row = q % 2 * QK + s + 1
                                weights((s + 1) % 4, e + 1, i * 4 + row if not (last and s == 3) else (q + 1) % 2 * QK)
                    with dve.Fori(0, QK // 4 - 1) as i:
                        body(i, False)
                    body(QK // 4 - 1, True)
                dve.wait_ge(sem("values_done"), (l + 1) * NK + 2)
                for t in range(2):
                    for n in range(2):
                        x = X[:, t, 512 * n:512 * n + 512]
                        TT(x, x, banks[2 * t + n][:, :], ALU.add)
                dve.wait_ge(sem("sample_mix_full"), 2 * (l + 1))
                for n in range(2):
                    x = X[0:NS, 2, 512 * n:512 * n + 512]
                    TT(x, x, banks[6 + n][0:NS, :], ALU.add)
                say("x_updated")

            link(dve.memset(ss, 1.0))
            say("ss_set")
            dve.wait_ge(sem("x_loaded"), 48)
            dve.wait_ge(sem("const_loaded"), 80)
            norm(0)
            dve.wait_ge(sem("gain0_loaded"), 16)
            dve.wait_ge(sem("z_ready"), 12)
            half = NORMED // 2
            for t, rows, a in TILES:
                R = slice(0, rows)
                parts = ((0, half, Z[R, t, 0:half * HD]), (half, NORMED, Z[R, t, QB0:QB0 + half * HD]))
                for lo, hi, z in parts:
                    TT(SQ[R, lo:hi, :].rearrange("p h d -> p (h d)"), z, z, ALU.mult)
                link(dve.tensor_reduce(RS24[R], SQ[R], AX, ALU.add))
                TS(RS24[R], RS24[R], 1.0 / HD, EPS, ALU.mult, ALU.add)
                link(dve.reciprocal(RS24[R], RS24[R]))
                say("heads_var")
                dve.wait_ge(sem("heads_rinv"), t + 1)
                for lo, hi, z in parts:
                    zh = z.rearrange("p (h d) -> p h d", d=HD)
                    TT(zh, zh, bc(RS24[R, lo:hi], 2, HD), ALU.mult)
                    TT(zh, zh, GAIN0[R, lo:hi, :], ALU.mult)
                say("heads_normed")
            dve.wait_ge(sem("tbl0_loaded"), 16)
            dve.wait_ge(sem("qkt_ready"), 18)

            def tables0(s, bank, pair, qt, nk):
                at = 0 if qt == 0 else 256
                STT(s, bank[:, 0:2 * nk], SCALE_AB, TBL0[:, pair, at:at + 2 * nk], ALU.mult, ALU.add)

            prompt_attention([(p, qt) for p in range(8) for qt in range(2)], "prompt0", SP_, tables0, O0, 1.0)
            link(dve.memset(QBA, 0.0))
            link(dve.memset(QBB, 0.0))
            for h in range(AH):
                half_ = slice(64 * (h % 2), 64 * (h % 2) + 64)
                step(dve.tensor_copy(QBA[half_, h // 2, :, 4 * h:4 * h + 4], QKT[:, h, SEQ:NT].rearrange("p (b t) -> p b t", t=DEC_T)))
                step(dve.tensor_copy(KNA[half_, h // 2, :], QKT[:, AH + h, SEQ:NT]))
            for j in range(BH):
                g, hh = j // GQ, j % GQ
                step(dve.tensor_copy(QBB[64 * g:64 * g + 64, :, 32 * g + 4 * hh:32 * g + 4 * hh + 4],
                                     QKT[:, 2 * AH + j, SEQ:NT].rearrange("p (b t) -> p b t", t=DEC_T)))
            for g in range(BKV):
                step(dve.tensor_copy(KNB[64 * g:64 * g + 64, :], QKT[:, 2 * AH + BH + g, SEQ:NT]))
            settle()
            say("q_spread")
            dve.wait_ge(sem("tbls_loaded"), 48)
            for r in range(2):
                bank = full()
                STT(SS_[:, 0:512], bank[:, :], SCALE_AB, TBLA[:, r, 0:512], ALU.mult, ALU.add)
                free()
                bank = full()
                STT(SS_[:, 512:AK + NS], bank[:, 0:AK + NS - 512], SCALE_AB, TBLA[:, r, 512:AK + NS], ALU.mult, ALU.add)
                free()
                softmax_rows(SS_, AK + NS, "sa", r, 1.0)
                bank = full()
                view = bank[:, 0:96].rearrange("p (i c e) -> p i c e", i=4, c=3)
                for e in range(2):
                    out = OT0[64 * e:64 * e + 64, 0:3, SEQ + 16 * r:SEQ + 16 * r + 16].rearrange("p c (i t) -> p i c t", t=DEC_T)
                    for i in range(4):
                        step(dve.tensor_copy(out[:, i], view[64 * e:64 * e + 64, i, :, 4 * e:4 * e + 4]))
                settle()
                free()
                say("a_cache_used")
            for r in range(4):
                for c in range(2):
                    bank = full()
                    link(dve.tensor_reduce(GATE[:, 2 * c:2 * c + 2], bank[:, :].rearrange("p (n k) -> p n k", k=BLK), AX, ALU.add))
                    STT(SS_[:, 512 * c:512 * c + 512], bank[:, :], SCALE_AB, TBLB[:, 512 * c:512 * c + 512], ALU.mult, ALU.add)
                    free()
                bank = full()
                STT(SS_[:, PAST:PAST + NS], bank[:, 0:NS], SCALE_AB, TBLBN[:, r, :], ALU.mult, ALU.add)
                free()
                say("gate_ready")
                bank = full()
                link(dve.tensor_copy(GATE, bank[:, 0:NBLK]))
                free()
                mine, other = bc(GATE, 2, NBLK), bc(GATE, 1, NBLK)
                TT(CMP, other, mine, ALU.is_equal)
                TT(CMP, CMP, before, ALU.mult)
                TT(CMP2, other, mine, ALU.is_gt)
                TT(CMP, CMP, CMP2, ALU.add)
                link(dve.tensor_reduce(RANK, CMP, AX, ALU.add))
                TS(RANK, RANK, 3.0, -BIG, ALU.is_ge, ALU.mult)
                ps = SS_[:, 0:PAST].rearrange("p (n k) -> p n k", k=BLK)
                TT(ps, ps, bc(RANK, 2, BLK), ALU.add)
                softmax_rows(SS_, PAST + NS, "sb", r, 1.0)
                bank = full()
                for j in range(BH):
                    g, hh = j // GQ, j % GQ
                    src = bank[64 * g:64 * g + 64, 0:P].rearrange("p (i e) -> p i e", i=2)[:, :, 32 * g + 4 * hh:32 * g + 4 * hh + 4]
                    dst = OT0[64 * (j % 2):64 * (j % 2) + 64, 3 + j // 2, SEQ + 8 * r:SEQ + 8 * r + 8].rearrange("p (i t) -> p i t", t=DEC_T)
                    step(dve.tensor_copy(dst, src))
                settle()
                free()
                say("b_cache_used")
            dve.wait_ge(sem("ot0_prompt"), 4)
            say("ot0_sample")
            add_to_x(0)
            if live(2):
                peer(0)

            def rope(x1, x2, cos, sin, tmp):
                TT(tmp[0], x1, cos, ALU.mult)
                TT(tmp[1], x2, sin, ALU.mult)
                TT(tmp[2], x1, sin, ALU.mult)
                TT(tmp[3], x2, cos, ALU.mult)
                TT(x1, tmp[0], tmp[1], ALU.subtract)
                TT(x2, tmp[2], tmp[3], ALU.add)

            def cmul(out, a, b, tmp, conj=False):
                TT(tmp[0], a[0], b[0], ALU.mult)
                TT(tmp[1], a[1], b[1], ALU.mult)
                TT(out[0], tmp[0], tmp[1], ALU.add if conj else ALU.subtract)
                TT(tmp[0], a[0], b[1], ALU.mult)
                TT(tmp[1], a[1], b[0], ALU.mult)
                TT(out[1], tmp[0], tmp[1], ALU.subtract if conj else ALU.add)

            def odd():
                link(dve.memset(ST8, 1.0))
                norm(2)
                dve.wait_ge(sem("odd_small_loaded"), 16 * 17)
                dve.wait_ge(sem("z2_ready"), 3)
                spans = ((0, CQ), (CQ, CQ + CKV), (CQ + CKV, CQ + CKV + DR))
                SQL = SGM.rearrange("p a b -> p (a b)")
                for t, rows, a in TILES:
                    R = slice(0, rows)
                    TT(SQL[R, 0:416], Z2[R, t, :], Z2[R, t, :], ALU.mult)
                    for k, (lo, hi) in enumerate(spans):
                        step(dve.tensor_reduce(ST8[R, t, k:k + 1], SQL[R, lo:hi], AX, ALU.add))
                    settle()
                    for k, (lo, hi) in enumerate(spans):
                        TS(ST8[R, t, k:k + 1], ST8[R, t, k:k + 1], 1.0 / (hi - lo), EPS, ALU.mult, ALU.add)
                    link(dve.reciprocal(ST8[R, t, 0:3], ST8[R, t, 0:3]))
                    say("latent_var")
                    dve.wait_ge(sem("latent_rinv"), t + 1)
                    for k, (lo, hi) in enumerate(spans):
                        STT(Z2[R, t, lo:hi], Z2[R, t, lo:hi], ST8I[R, t, k:k + 1], GROW[R, lo:hi], ALU.mult, ALU.mult)
                    lo = CQ + CKV
                    rope(Z2[R, t, lo:lo + 16], Z2[R, t, lo + 16:lo + 32], COS[R, t, :], SIN[R, t, :], [SQL[R, 16 * n:16 * n + 16] for n in range(4)])
                    say("latents_ready")
                    bank = full()
                    link(dve.tensor_copy(CQT[:, :, a:a + rows], bank[:, 0:2 * P].rearrange("p (j n) -> p j n", n=P)[:, :, 0:rows]))
                    link(dve.tensor_copy(CKT[:, a:a + rows], bank[:, 2 * P:2 * P + rows]))
                    free()
                    say("latents_turned")
                SQH = T12.rearrange("p k a b -> p (k a b)")
                for t, rows, a in TILES:
                    R = slice(0, rows)
                    dve.wait_ge(sem("qkv_ready"), 4 * (t + 1))
                    sq = SQH[R, 0:768].rearrange("p (h e) -> p h e", e=DQK)
                    sk = SQH[R, 768:1280].rearrange("p (h e) -> p h e", e=DN)
                    kr = KR[R, t, :].rearrange("p (h e) -> p h e", e=DN)
                    TT(sq, Q[R, t], Q[R, t], ALU.mult)
                    TT(sk, kr, kr, ALU.mult)
                    link(dve.tensor_reduce(ST8[R, t, 0:8], sq[:, :, 0:DN], AX, ALU.add))
                    link(dve.tensor_reduce(ST8[R, t, 8:16], sk, AX, ALU.add))
                    link(dve.tensor_reduce(ST8[R, t, 16:24], sq[:, :, DN:DQK], AX, ALU.add))
                    TS(ST8[R, t, 0:16], ST8[R, t, 0:16], 1.0 / DN, EPS, ALU.mult, ALU.add)
                    TS(ST8[R, t, 16:24], ST8[R, t, 16:24], 1.0 / DR, EPS, ALU.mult, ALU.add)
                    link(dve.reciprocal(ST8[R, t, 0:24], ST8[R, t, 0:24]))
                    say("qk_var")
                    dve.wait_ge(sem("qk_rinv"), t + 1)
                    qn, qp = Q[R, t, :, 0:DN], Q[R, t, :, DN:DQK]
                    TT(qn, qn, bc(ST8I[R, t, 0:8], 2, DN), ALU.mult)
                    TT(qn, qn, bc(GQN[R], 1, DH), ALU.mult)
                    TT(qp, qp, bc(ST8I[R, t, 16:24], 2, DR), ALU.mult)
                    TT(qp, qp, bc(GQR[R], 1, DH), ALU.mult)
                    rope(Q[R, t, :, DN:DN + 16], Q[R, t, :, DN + 16:DQK], bc(COS[R, t, :], 1, DH), bc(SIN[R, t, :], 1, DH), [RTT[R, n] for n in range(4)])
                    if t < 2:
                        kn = KCAT[R, t, :, 0:DN]
                        TT(kn, kr, bc(ST8I[R, t, 8:16], 2, DN), ALU.mult)
                        TT(kn, kn, bc(GKN[R], 1, DH), ALU.mult)
                        link(dve.tensor_copy(KCAT[R, t, :, DN:DQK], bc(Z2[R, t, CQ + CKV:], 1, DH)))
                    say("qk_ready")
                dve.wait_ge(sem("qct_ready"), 10)

                def tables1(s, bank, pair, qt, nk):
                    at = 0 if qt == 0 else P
                    sh = s.rearrange("p (h k) -> p h k", h=2)
                    TT(sh, bank[:, 0:2 * nk].rearrange("p (h k) -> p h k", h=2), bc(TBLD[:, at:at + nk], 1, 2), ALU.add)

                prompt_attention([(p, qt) for p in range(4) for qt in range(2)], "prompt1", S_D, tables1, O1, SCALE_D)
                par = [S5P[:, n, :] for n in range(24)]
                dve.wait_ge(sem("s5_dt"), 1)
                TT(par[4], par[0], par[3], ALU.mult)
                TT(par[5], par[1], par[3], ALU.mult)
                TS(par[10], par[5], 1.0 / TWO_PI, None, ALU.mult)
                TS(par[10], par[10], MAGIC, MAGIC, ALU.add, ALU.subtract)
                for c in (C1, C2, C3):
                    STT(par[5], par[10], -c, par[5], ALU.mult, ALU.add)
                PI_DOWN = 3.1415925
                TS(par[5], par[5], PI_DOWN, -PI_DOWN, ALU.min, ALU.max)
                TS(par[6], par[5], -1.0, None, ALU.mult)
                TT(par[6], par[6], par[5], ALU.max)
                TS(par[6], par[6], -1.0, math.pi / 2, ALU.mult, ALU.add)
                say("s5_angles")
                dve.wait_ge(sem("s5_mag"), 3)
                TT(par[11], par[7], par[8], ALU.mult)
                TT(par[12], par[7], par[9], ALU.mult)
                TS(par[13], par[11], -1.0, None, ALU.add)
                TT(par[14], par[0], par[0], ALU.mult)
                TT(par[15], par[1], par[1], ALU.mult)
                TT(par[14], par[14], par[15], ALU.add)
                link(dve.reciprocal(par[14], par[14]))
                TT(par[15], par[13], par[0], ALU.mult)
                TT(par[16], par[12], par[1], ALU.mult)
                TT(par[15], par[15], par[16], ALU.add)
                TT(par[15], par[15], par[14], ALU.mult)
                TT(par[16], par[12], par[0], ALU.mult)
                TT(par[17], par[13], par[1], ALU.mult)
                TT(par[16], par[16], par[17], ALU.subtract)
                TT(par[16], par[16], par[14], ALU.mult)
                dve.wait_ge(sem("s5_b_loaded"), 16)
                tmp = [T12[:, k, 0:2, :].rearrange("p a b -> p (a b)").rearrange("p (s c) -> p s c", c=32) for k in range(2)]
                f = [bc(par[15], 2, 32), bc(par[16], 2, 32)]
                cmul([BSC[:, 0], BSC[:, 1]], f, [BBD[:, 0], BBD[:, 1]], tmp)
                say("s5_b_scaled")
                TS(CBD[:, 1], CBD[:, 1], -1.0, None, ALU.mult)
                dve.wait_ge(sem("ut_ready"), 4)
                for hf in range(2):
                    S = slice(SG2 * hf, SG2 * hf + SG2)
                    if hf == 0:
                        dve.wait_ge(sem("ot1_prompt"), 2)
                    for s in range(2):
                        step(dve.memset(E[:, s, :, 0:1], 1.0 - s))
                    step(dve.tensor_copy(par[18], par[8]))
                    step(dve.tensor_copy(par[19], par[9]))
                    settle()
                    m = 1
                    while m < SEQ:
                        pw = [bc(par[18][:, S], 2, m), bc(par[19][:, S], 2, m)]
                        t = [T12[:, k, :, 0:m] for k in range(2)]
                        cmul([E[:, k, :, m:2 * m] for k in range(2)], [E[:, k, :, 0:m] for k in range(2)], pw, t)
                        if 2 * m < SEQ:
                            cmul([par[20], par[21]], [par[18], par[19]], [par[18], par[19]], [par[22], par[23]])
                            step(dve.tensor_copy(par[18], par[20]))
                            step(dve.tensor_copy(par[19], par[21]))
                            settle()
                        m *= 2
                    link(dve.tensor_copy(RARR, bc(par[7][:, S], 2, SEQ)))
                    link(dve.memset(RARR[:, :, 0:1], 0.0))
                    dve.wait_ge(sem("bu_ready"), 16 * (hf + 1))
                    bu = [BU[:, k, :, 0:SEQ] for k in range(2)]
                    e = [E[:, k] for k in range(2)]
                    t = [T12[:, k] for k in range(2)]
                    x = [XR[:, k] for k in range(2)]
                    cmul(x, e, bu, t, conj=True)
                    for k in range(2):
                        link(dve.tensor_tensor_scan(t[k].rearrange("p a b -> p (a b)"), RARR.rearrange("p a b -> p (a b)"),
                                                    x[k].rearrange("p a b -> p (a b)"), 0.0, ALU.mult, ALU.add))
                    cmul(bu, e, t, x)
                    ab = [bc(par[11][:, S], 2, DEC_B), bc(par[12][:, S], 2, DEC_B)]
                    prev = [S0[:, k, S, :] for k in range(2)]
                    for n in range(DEC_T):
                        now = [BU[:, k, :, SEQ + n:NT:DEC_T] for k in range(2)]
                        tm = [STMP[:, k] for k in range(4)]
                        cmul([tm[0], tm[1]], ab, prev, [tm[2], tm[3]])
                        for k in range(2):
                            TT(now[k], now[k], tm[k], ALU.add)
                        prev = now
                    for k in range(2):
                        step(dve.tensor_copy(LASTP[:, k, S], BU[:, k, :, SEQ - 1]))
                        step(dve.tensor_copy(LASTS[:, k, S, :], BU[:, k, :, SEQ + DEC_T - 1:NT:DEC_T]))
                    settle()
                    say("states_ready")
                    for c in range(2 * hf, 2 * hf + 2):
                        bank = full()
                        STT(Y[:, c, :], UT[:, c, :], DSKIP[:, c:c + 1], bank[:, 0:NT], ALU.mult, ALU.add)
                        free()
                        say("y_ready")
                for m in range(4):
                    dve.wait_ge(sem("sgm_ready"), m + 1)
                    TT(OT1[:, m, :], ZG[:, m, :], SGM[:, m, :], ALU.mult)
                    say("oc_ready")
                dve.wait_ge(sem("tbldn_loaded"), 16)
                TS(QG.rearrange("p h n -> p (h n)"), QCT[0:DN, :, SEQ:NT], GKNP, None, ALU.mult) if False else \
                    link(dve.tensor_scalar(QG, QCT[0:DN, :, SEQ:NT], GKNP, None, ALU.mult))
                say("qg_ready")
                for k in range(DH):
                    step(dve.tensor_copy(QPE[:, :, k, :], QCT[DN:DQK, k, SEQ:NT].rearrange("p (b t) -> p b t", t=DEC_T)))
                kp = S_SD[0:NS, 0:DR]
                step(dve.tensor_copy(kp, Z2[0:NS, 2, CQ + CKV:]))
                settle()
                link(dve.transpose(KPEN, kp))
                link(dve.tensor_copy(RKN[0:NS], bc(ST8I[0:NS, 2, 8:16], 2, DEC_T)))
                bank = full()
                link(dve.tensor_copy(QABS.rearrange("p b h t -> p h b t"), bank[:, 0:DH * NS].rearrange("p (h b t) -> p h b t", h=DH, t=DEC_T)))
                free()
                say("qabs_ready")
                for r in range(2):
                    for i in range(4):
                        for j in range(PAGES):
                            n = (4 * r + i) * PAGES + j
                            dve.wait_ge(sem("sqd_ready"), n + 1)
                            link(dve.tensor_reduce(RKS[:, i, j, :], SQD[:, n % 2, :].rearrange("p (h e) -> p h e", e=DN), AX, ALU.add))
                            say("sqd_used")
                        TS(RKS[:, i], RKS[:, i], 1.0 / DN, EPS, ALU.mult, ALU.add)
                        link(dve.reciprocal(RKS[:, i], RKS[:, i]))
                        say("rk_var")
                        dve.wait_ge(sem("rk_rinv"), 4 * r + i + 1)
                        link(dve.tensor_copy(RKX[:, i, :, :].rearrange("p j (h t) -> p (j h) t", t=DEC_T), bc(RKS[:, i].rearrange("p j h -> p (j h)"), 2, DEC_T)))
                        say("rkx_ready")
                    cols = ((0, 512), (512, PAST), (PAST, PAST + NS))
                    for lo, hi in cols:
                        bank = full()
                        link(dve.tensor_copy(R_SD[:, lo:hi], bank[:, 0:hi - lo]))
                        free()
                    for lo, hi in cols:
                        bank = full()
                        TT(S_SD[:, lo:hi], R_SD[:, lo:hi], bank[:, 0:hi - lo], ALU.mult)
                        free()
                    for lo, hi in cols:
                        bank = full()
                        TT(S_SD[:, lo:hi], S_SD[:, lo:hi], bank[:, 0:hi - lo], ALU.add)
                        free()
                    TT(S_SD[:, PAST:], S_SD[:, PAST:], TBLDN[:, r, :], ALU.add)
                    softmax_rows(S_SD, PAST + NS, "sd", r, SCALE_D)
                    bank = full()
                    link(dve.tensor_copy(CT[:, :, 16 * r:16 * r + 16].rearrange("p h (i t) -> p i h t", t=DEC_T),
                                         bank[:, 0:P].rearrange("p (i h t) -> p i h t", i=4, t=DEC_T)))
                    free()
                    say("ct_ready")
                    say("d_cache_used")
                bank = full()
                link(dve.tensor_copy(S_SD[0:NS, 0:512], bank[0:NS, :]))
                free()
                say("o1_sample_ready")
                add_to_x(2)

            RTT = Carver(arena, R1_0, R1_N).skip_to(18944 - 2048).take(4, DH, DR // 2)
            if live(3):
                odd()
            if live(4):
                peer(1)
    return nc


def lay_out(x):
    c = np.ascontiguousarray
    f = np.float32
    a = {}
    a["x_prompt"] = c(x["x_prompt"][0])
    a["x_sample"] = c(x["x_sample"].reshape(NS, D))

    def rows(w):
        return c(w.reshape(-1, P, w.shape[-1]).transpose(1, 0, 2))

    a["ev_w_in"], a["ev_w_out"] = rows(x["ev_w_in"][0]), rows(x["ev_w_out"][0])
    a["od_w_in"], a["od_w_out"] = rows(x["od_w_in"][0]), rows(x["od_w_out"][0])
    a["mla_w_uq"] = rows(x["mla_w_uq"][0])
    a["mla_w_uk"], a["mla_w_uv"] = c(x["mla_w_uk"][0]), c(x["mla_w_uv"][0])
    a["mla_w_ukt"] = c(x["mla_w_uk"][0].reshape(P, DH, DN).transpose(2, 1, 0))
    a["s5_w_glu"] = rows(x["s5_w_glu"][0])
    a["peer_w_q"] = c(x["peer_w_q"].reshape(2, KC, P, 2048).transpose(0, 2, 1, 3))
    keys = np.stack([x["peer_k1"], x["peer_k2"]], 2)
    a["peer_k"] = c(keys.transpose(0, 4, 1, 2, 3).reshape(2, P, 2 * PH, NK))
    a["peer_ut"] = c(x["peer_u"].reshape(2, NK, NK, KC, P).transpose(0, 2, 4, 3, 1).reshape(2, NK, P, D))
    a["peer_v"] = c(x["peer_v"].reshape(2, NK, NK, D).transpose(0, 2, 1, 3))
    g = np.stack([x["g_mix"][0], x["g_ffn"][0], x["g_mix"][1], x["g_ffn"][1]])
    a["gain"] = c(g.reshape(4, KC, P).transpose(2, 0, 1))
    a["gain0"] = c(np.concatenate([np.tile(x["ev_g_qa"][0], (AH, 1)), np.tile(x["ev_g_ka"][0], (AH, 1)),
                                   np.tile(x["ev_g_qb"][0], (BH, 1)), np.tile(x["ev_g_kb"][0], (BKV, 1))]))
    a["grow"] = c(np.concatenate([x["mla_g_cq"][0], x["mla_g_ckv"][0], x["mla_g_kr"][0]]))
    a["mla_g_qn"], a["mla_g_qr"], a["mla_g_kn"] = c(x["mla_g_qn"][0]), c(x["mla_g_qr"][0]), c(x["mla_g_kn"][0])
    a["mla_g_kn_col"] = c(x["mla_g_kn"][0].reshape(DN, 1))
    a["page_table"] = c(x["page_table"].reshape(1, -1).astype(np.int32))
    def reach(z):
        far = z[:, :512].reshape(DEC_B, 32, 16, AH * HD)[:, :, 0:DEC_T].reshape(DEC_B, P, AH * HD)
        return np.concatenate([far, z[:, 512:].reshape(DEC_B, 512, AH * HD)], 1)
    a["cache_a_kt"] = c(reach(x["cache_a_k"][0]).reshape(DEC_B, AK, 3, P).transpose(0, 3, 2, 1))
    a["cache_a_v"] = c(reach(x["cache_a_v"][0]).reshape(DEC_B, AKC, P, AH * HD).transpose(0, 2, 1, 3))
    kt = x["cache_b_k"][0].reshape(-1, PAGE, P).transpose(0, 2, 1)
    a["pool_kv"] = c(np.concatenate([kt, x["cache_b_v"][0].reshape(-1, PAGE, P)], 2))
    ck = x["cache_d_ckv"][0]
    a["pool_ckv"] = c(np.concatenate([ck.transpose(0, 2, 1), ck], 2))
    a["pool_kpe"] = c(x["cache_d_kpe"][0].transpose(0, 2, 1))
    def states(z):
        return z.reshape(SCH, P).T
    a["s5_par"] = c(np.stack([states(x["s5_a_re"][0]), states(x["s5_a_im"][0]),
                              states(np.repeat(x["s5_log_dt"][0][:, None], 64, 1))], 1))
    def diag(z):
        out = np.zeros((2, 64, SCH, 2, 16), z.dtype)
        z = z.reshape(SCH, 2, 64, 16)
        for k in range(2):
            out[k, :, :, k, :] = z[:, k].transpose(1, 0, 2)
        return out.reshape(P, SCH, 32)
    a["s5_b"] = c(np.stack([diag(x["s5_b_re"][0]), diag(x["s5_b_im"][0])], 1))
    a["s5_c"] = c(np.stack([diag(x["s5_c_re"][0].transpose(0, 2, 1)), diag(x["s5_c_im"][0].transpose(0, 2, 1))], 1))
    a["state_c"] = c(np.stack([z[0].reshape(DEC_B, SCH, P).transpose(2, 1, 0) for z in (x["state_c_re"], x["state_c_im"])], 1))
    a["s5_d"] = c(x["s5_d"][0].reshape(4, P).T)
    a["s5_b_glu"] = c(x["s5_b_glu"][0].reshape(4, P).T)

    a["ident"] = np.eye(P, dtype=f)
    a["iota"] = c(np.broadcast_to(np.arange(NK, dtype=f), (P, NK)))
    p = np.arange(P)
    row = np.stack([p // 32, p % DEC_T])
    a["group"] = c((row[:, :, None] == row[:, None, :]).all(0).astype(f))
    a["before"] = c(np.broadcast_to(np.tri(NBLK, k=-1, dtype=f), (P, NBLK, NBLK)))
    nh = AH + BH
    slopes = 2.0 ** (-8.0 * np.arange(1, nh + 1) / nh)

    def a_bias(dist, h):
        n = ((dist <= 128) * 1 + ((dist % 4 == 0) & (dist <= 512)) + ((dist % 16 == 0) & (dist <= 2048))) * (dist >= 0)
        return np.where(n > 0, -slopes[h] * dist + np.log(np.maximum(n, 1)), -BIG)

    def b_bias(dist, h):
        return np.where(dist >= 0, -slopes[h] * dist, -BIG)

    q = np.arange(P)[:, None]
    tbl = np.zeros((P, 8, 768))
    for h in range(nh):
        fn = a_bias if h < AH else b_bias
        for qt in range(2):
            nk = P * (qt + 1)
            at = (0 if qt == 0 else 256) + (h % 2) * nk
            tbl[:, h // 2, at:at + nk] = fn(q + P * qt - np.arange(nk)[None, :], h)
    a["tbl0"] = tbl.astype(f)
    far = (np.arange(32)[:, None] * 16 + np.arange(DEC_T)[None, :]).reshape(-1)
    kpos = np.concatenate([far, np.arange(512, PAST)])
    ta = np.zeros((P, 2, AK + NS))
    tb, tbn = np.zeros((P, PAST)), np.zeros((P, 4, NS))
    tdn = np.zeros((P, 2, NS))
    nb, ntk = np.arange(NS) // DEC_T, np.arange(NS) % DEC_T
    for p in range(P):
        i, h, t = p // 32, (p % 32) // 4, p % 4
        for r in range(2):
            if h < AH:
                ta[p, r, :AK] = a_bias(PAST + t - kpos, h)
                ta[p, r, AK:] = np.where(nb == 4 * r + i, a_bias(t - ntk, h), -BIG)
            tdn[p, r] = np.where((nb == 4 * r + i) & (ntk <= t), 0, -BIG)
        i, g, hh, t = p // 64, (p % 64) // 32, (p % 32) // 4, p % 4
        if hh < GQ:
            h = AH + GQ * g + hh
            tb[p] = b_bias(PAST + t - np.arange(PAST), h)
            for r in range(4):
                tbn[p, r] = np.where(nb == 2 * r + i, b_bias(t - ntk, h), -BIG)
    a["tbla"], a["tblb"], a["tblbn"], a["tbldn"] = ta.astype(f), tb.astype(f), tbn.astype(f), tdn.astype(f)
    td = np.zeros((P, 384))
    td[:, 0:P] = np.where(q >= np.arange(P)[None, :], 0, -BIG)
    td[:, P:] = np.where(q + P >= np.arange(SEQ)[None, :], 0, -BIG)
    a["tbld"] = td.astype(f)
    half = DR // 2
    freqs = (np.float32(10000.0) ** (-np.arange(half, dtype=f) / np.float32(half))).astype(f)
    pos = np.zeros((P, 3), f)
    pos[:, 0], pos[:, 1] = np.arange(P), np.arange(P) + P
    pos[0:NS, 2] = PAST + np.arange(NS) % DEC_T
    ang = (pos[:, :, None] * freqs).astype(f)
    a["cos"], a["sin"] = np.cos(ang.astype(np.float64)).astype(f), np.sin(ang.astype(np.float64)).astype(f)
    return a


OUTS = {
    "y_prompt": (SEQ, D), "y_sample": (NS, D),
    "a_k_prompt": (SEQ, AH * HD), "a_v_prompt": (SEQ, AH * HD), "b_k_prompt": (SEQ, BKV * HD), "b_v_prompt": (SEQ, BKV * HD),
    "c_re_prompt": (P, SCH), "c_im_prompt": (P, SCH), "d_ckv_prompt": (SEQ, CKV), "d_kpe_prompt": (SEQ, DR),
    "a_k_sample": (NS, AH * HD), "a_v_sample": (NS, AH * HD), "b_k_sample": (NS, BKV * HD), "b_v_sample": (NS, BKV * HD),
    "c_re_sample": (P, SCH, DEC_B), "c_im_sample": (P, SCH, DEC_B), "d_ckv_sample": (NS, CKV), "d_kpe_sample": (NS, DR),
}


def finish(r):
    lead = {"prompt": (1, 1, SEQ), "sample": (1, DEC_B, DEC_T)}
    out = []
    for name in OUTS:
        v, kind = r[name], name.rsplit("_", 1)[1]
        if name[0] == "y":
            out.append(v.reshape(lead[kind][1:] + (D,)))
        elif name[0] in "ab":
            out.append(v.reshape(lead[kind] + (-1, HD)))
        elif name[0] == "d":
            out.append(v.reshape(lead[kind] + (-1,)))
        elif kind == "prompt":
            out.append(np.ascontiguousarray(v.T).reshape(1, 1, 32, 64))
        else:
            out.append(np.ascontiguousarray(v.transpose(2, 1, 0)).reshape(1, DEC_B, 32, 64))
    return tuple(out)


def declare(nc, arrays):
    ins = {n: nc.dram_tensor(f"in_{n}", a.shape, mybir.dt.from_np(a.dtype), kind="ExternalInput").ap() for n, a in arrays.items()}
    outs = {n: nc.dram_tensor(n, s, F32, kind="ExternalOutput").ap() for n, s in OUTS.items()}
    return ins, outs


def kernel(**inputs):
    import concourse.bacc as bacc
    from concourse.bass_utils import run_bass_kernel_spmd
    arrays = lay_out({n: np.asarray(v) for n, v in inputs.items()})
    nc = bacc.Bacc("TRN2", target_bir_lowering=False, num_devices=1)
    build(nc, *declare(nc, arrays))
    r = run_bass_kernel_spmd(nc, [{f"in_{n}": a for n, a in arrays.items()}], core_ids=[0])
    return finish(r.results[0])
```

```python
import math

import numpy as np

import concourse.bass as bass
from concourse import mybir
from contextlib import ExitStack

F32 = mybir.dt.float32
F32R = mybir.dt.float32r
BF16 = mybir.dt.bfloat16
U32 = mybir.dt.uint32
I32 = mybir.dt.int32
ALU = mybir.AluOpType
ACT = mybir.ActivationFunctionType
AX = mybir.AxisListType.X
ds = bass.ds

P = 128
D = 1024
KC = D // P
SEQ, DEC_B, DEC_T = 256, 8, 4
NS = DEC_B * DEC_T
NT = SEQ + NS
TILES = ((0, P, 0), (1, P, P), (2, NS, SEQ))
PAST, PAGE = 1024, 128
PAGES = PAST // PAGE
HD = 64
AH, BH, BKV = 6, 10, 2
GQ = BH // BKV
NORMED = 2 * AH + BH + BKV
EVEN_IN, ODD_IN = 2048, 928
VA0, QB0, KB0, VB0 = 768, 1152, 1792, 1920
AK = 640
AKC = AK // P
BLK = 256
NBLK = PAST // BLK
DH, DN, DR = 8, 64, 32
DQK = DN + DR
CQ, CKV = 256, 128
SCH, SG2 = 16, 8
PH, TOPK, NK = 8, 16, 128
QK = NK // 4
NGT = 12
NG = NT // NGT
BEFORE = QK - NG // 2
EPS = 1e-6
BIG = 1e30
NEG = -3.0e38
TWO_PI = 2.0 * math.pi
MAGIC = 1.5 * 2.0 ** 23
C1 = 6.28125
C2 = float(np.float32(TWO_PI - C1))
C3 = float(np.float32(TWO_PI - C1 - float(np.float32(TWO_PI - C1))))
SCALE_AB = 1.0 / math.sqrt(HD)
SCALE_D = 1.0 / math.sqrt(DQK)


class Carver:

    def __init__(self, regions, base, size):
        self.region, self.size, self.at = regions[base], size, 0

    def skip_to(self, at):
        self.at = at
        return self

    def take(self, *shape, parts=P, dt=F32):
        n = int(np.prod(shape)) // (2 if dt is BF16 else 1)
        assert self.at + n <= self.size, (self.at, n, self.size)
        v = self.region[0:parts, self.at:self.at + n]
        self.at += n
        if dt is not F32:
            v = v.bitcast(dt)
        if len(shape) == 2:
            v = v.rearrange("p (a b) -> p a b", b=shape[1])
        if len(shape) == 3:
            v = v.rearrange("p (a b c) -> p a b c", b=shape[1], c=shape[2])
        if len(shape) == 4:
            v = v.rearrange("p (a b c d) -> p a b c d", b=shape[1], c=shape[2], d=shape[3])
        return v


def bc(ap, axis, n):
    shape = list(ap.shape)
    return ap.unsqueeze(axis).broadcast_to(shape[:axis] + [n] + shape[axis:])


def build(nc, I, O, stop=4):
    ctx = ExitStack()
    with ctx:
        sems = {}

        def sem(name):
            if name not in sems:
                sems[name] = ctx.enter_context(nc.semaphore(name))
            return sems[name]

        R1_0, R1_N = 6112, 19800
        R2_0, R2_N = R1_0 + R1_N, 19000
        RING_0, RING_N = R2_0 + R2_N, 8192
        base = (nc.sbuf_base + 31) // 32 * 32
        arena = {at: ctx.enter_context(nc.sbuf_tensor(name, [P, n], F32))
                 for name, at, n in (("keep", 0, R1_0), ("region1", R1_0, R1_N), ("region2", R2_0, R2_N), ("ring", RING_0, RING_N))}

        def rounded(name, shape, at):
            return nc.alloc_sbuf_tensor_at(name, [P] + shape, F32R, offset=base + 4 * at)

        banks = [ctx.enter_context(nc.psum_tensor(f"bank{i}", [P, 512], F32)) for i in range(8)]

        keep = Carver(arena, 0, 6112)
        X = keep.take(3, D)
        HT = keep.take(KC, NT)
        ident = keep.take(P)
        iota = keep.take(NK)
        before = keep.take(NBLK, NBLK)
        group = keep.take(P)
        gain = keep.take(4, KC)
        ss = keep.take(3)
        rinv = keep.take(3)
        pages = keep.take(PAGES * DEC_B, parts=1, dt=I32)

        r1 = Carver(arena, R1_0, R1_N)
        W_IN0 = r1.take(KC, EVEN_IN)
        r1.skip_to(0)
        KA = r1.take(4, 3, AK)
        VA = r1.take(4, AKC, 3 * P)
        OT0 = r1.take(KC, NT)
        O0 = r1.take(2, D)
        r1.skip_to(17664)
        GAIN0 = r1.take(NORMED, HD)
        r1.skip_to(0)
        W_OUT = r1.take(KC, D)
        r2 = Carver(arena, R2_0, R2_N)
        Z = r2.take(3, EVEN_IN)
        QKT = r2.take(NORMED, NT, parts=HD)
        KVB = r2.take(2, PAGES, 2 * P)
        KVB2 = Carver(arena, R2_0, R2_N).skip_to(3 * EVEN_IN).take(2, PAGES, 2 * P)
        KVS = [KVB[:, 0], KVB[:, 1], KVB2[:, 0], KVB2[:, 1]]
        PTP = r2.take(2, 4, P)
        r2s = r2.at
        RS24 = r2.take(NORMED)
        r3 = Carver(arena, RING_0, RING_N)
        HTOK = r3.take(3, D)
        SQ = r3.take(NORMED, HD)
        r3.skip_to(0)
        TBL0 = r3.take(8, 768)
        SP_ = r3.take(2, 512)
        PP_ = r3.take(2, 512)
        r3.skip_to(0)
        SS_ = r3.take(2, PAST + NS)
        PTS = r3.take(PAGES + 1, P)
        TBLA = r3.take(2, AK + NS)
        TBLB = r3.take(PAST)
        TBLBN = r3.take(4, NS)
        QBA = r3.take(3, DEC_B, 32)
        QBB = r3.take(DEC_B, 64)
        KNA = r3.take(3, NS)
        KNB = r3.take(NS)
        OS_ = r3.take(3 * P)
        SUNITS = [("a", 0), ("b", 0), ("b", 1), ("a", 1), ("b", 2), ("b", 3)]
        r2 = Carver(arena, R2_0, R2_N).skip_to(r2s + NORMED)
        MX = r2.take(2, 2)
        SUMS = r2.take(4, 2)
        RSUM = r2.take(2)
        GATE = r2.take(NBLK)
        CMP = r2.take(NBLK, NBLK)
        CMP2 = r2.take(NBLK, NBLK)
        RANK = r2.take(NBLK)
        MX1 = r2.take(2)
        SUM1 = r2.take(2)

        r1 = Carver(arena, R1_0, R1_N)
        W_Q = r1.take(KC, 2048)
        KEYS = r1.take(2 * PH, NK)
        G = Carver(arena, R1_0, R1_N).take(2 * QK, NT)
        r2 = Carver(arena, R2_0, R2_N)
        QT = r2.take(2 * PH, NT)
        TOPV = r2.take(3, PH, 2, TOPK)
        TOPI = r2.take(3, PH, 2, TOPK, dt=U32)
        TOPIF = r2.take(PH, 2, TOPK)
        SELV = r2.take(3, PH, TOPK)
        SELJ = r2.take(3, PH, TOPK, dt=U32)
        SC2 = r2.take(4, NK)
        CAND = r2.take(2, TOPK, TOPK)
        CAND2 = r2.take(2, TOPK, TOPK)
        EQ = r2.take(PH, TOPK, TOPK)
        SELAB = r2.take(2, PH, TOPK, dt=U32)
        SELABF = r2.take(2, PH, TOPK)
        ROUTE = r2.take(3, 3, P)
        GSUM = r2.take(PH)
        HR_AT = 8 * D + 4 * NT + 2 * NT + NGT * NK + 3 * NGT * QK
        assert r2.at <= HR_AT
        r2 = Carver(arena, R2_0, R2_N).skip_to(R2_N - 3 * NT - 3 * NT)
        ROUTET = r2.take(3, NT)
        PIECES = r2.take(6, NT, dt=BF16)
        UV = rounded("uv_parts", [2, 4, D], R2_0)
        WR = rounded("weight_parts", [2, 2, SEQ], R2_0 + 8 * D)
        WRS = rounded("sample_weight_parts", [2, 2, NS], R2_0 + 8 * D + 4 * SEQ)
        HR = rounded("h_parts", [2, KC, NT], R2_0 + HR_AT)
        UA = rounded("u_parts_ahead", [4, 2, D], RING_0)[:, :, 1, :]
        r2 = Carver(arena, R2_0, R2_N).skip_to(8 * D + 4 * NT)
        ACTV = r2.take(2, NT)
        ONE1 = r2.take(2, NGT, NK, dt=BF16)
        ONE2 = r2.take(2, NGT, 3 * QK, dt=BF16).rearrange("p s t (e n) -> p s t e n", e=3)
        assert r2.at == HR_AT and HR_AT + 2 * KC * NT <= R2_N - 6 * NT
        WFULL = Carver(arena, R1_0, R1_N).skip_to(2 * QK * NT).take(2, NT)
        ZEROS = Carver(arena, R1_0, R1_N).skip_to(2 * QK * NT + 2 * NT).take(P)
        EQ2 = Carver(arena, R1_0, R1_N).skip_to(2 * QK * NT + 2 * NT + P).take(2, NGT, QK, dt=BF16)
        MIXS = Carver(arena, R1_0, R1_N).skip_to(QK * NT).take(2, 512, parts=2 * NS)
        SLOTS = Carver(arena, RING_0, RING_N).take(4, 2, D)

        r1 = Carver(arena, R1_0, R1_N)
        W_IN1 = r1.take(KC, ODD_IN)
        assert r1.at <= QK * NT
        S_D = r1.take(2, 512)
        P_D = r1.take(2, 512)
        PT_D = r1.take(2, 4, P)
        TBLD = r1.take(384)
        O1 = r1.take(3, 512)
        r1 = Carver(arena, R1_0, R1_N)
        BU = r1.take(2, SG2, NT)
        E = r1.take(2, SG2, SEQ)
        XR = r1.take(2, SG2, SEQ)
        T12 = r1.take(2, SG2, SEQ)
        RARR = r1.take(SG2, SEQ)
        r1 = Carver(arena, R1_0, R1_N)
        S_SD = r1.take(PAST + NS)
        PT_SD = r1.take(PAGES + 1, P)
        CT = r1.take(DH, NS)
        QABS = r1.take(DEC_B, DH, DEC_T)
        QPE = r1.take(DEC_B, DH, DEC_T)
        KPEN = r1.take(NS, parts=DR)
        TBLDN = r1.take(2, NS)
        RKN = r1.take(DH, DEC_T)
        RKNX = r1.take(NS)
        QG = r1.take(DH, NS, parts=DN)
        OSD = r1.take(P)
        assert r1.at + PAGES * 2 * P >= 2 * SG2 * NT
        ckp_at = r1.at
        CKP = r1.take(7, PAGES, 2 * P)
        CKP_OF = (1, 2, 3, 4, 5, 6, 0, 1)
        W_OUTAB = Carver(arena, R1_0, R1_N).skip_to(ckp_at + 3 * PAGES * 2 * P).take(2, KC, 512)
        KPP1 = r1.take(PAGES, P)
        r2 = Carver(arena, R2_0, R2_N)
        UT = r2.take(4, NT)
        Z2 = r2.take(3, CQ + CKV + DR)
        CQT = r2.take(2, NT)
        CKT = r2.take(NT)
        q_at = r2.at
        Q = r2.take(3, DH, DQK)
        OT1 = Carver(arena, R2_0, R2_N).skip_to(q_at).take(KC, NT)
        kc_at = r2.at
        KCAT = r2.take(2, DH, DQK)
        Y = Carver(arena, R2_0, R2_N).skip_to(kc_at).take(4, NT)
        kr_at = r2.at
        KR = r2.take(3, 512)
        ZG = Carver(arena, R2_0, R2_N).skip_to(kr_at).take(4, NT)
        QCT = r2.take(DH, NT, parts=DQK)
        vd_at = r2.at
        VD = r2.take(3, 512)
        SGM = Carver(arena, R2_0, R2_N).skip_to(vd_at).take(4, NT)
        kct_at = r2.at
        KCT = r2.take(DH, SEQ, parts=DQK)
        r2x = Carver(arena, R2_0, R2_N).skip_to(kct_at)
        BBD = r2x.take(2, SCH, 32)
        BSC = r2x.take(2, SCH, 32)
        r2x.skip_to(kct_at)
        KSQ = r2x.take(2, 512)
        PGB = r2x.take(2, 4, P)
        CBD = r2.take(2, SCH, 32)
        S5P = r2.take(24, SCH)
        S0 = r2.take(2, SCH, DEC_B)
        DSKIP = r2.take(4)
        BGLU = r2.take(4)
        ST8 = r2.take(3, 32)
        ST8I = r2.take(3, 32)
        BT = r2.take(2, 4, P)
        STMP = r2.take(4, SG2, DEC_B)
        LASTP = r2.take(2, SCH)
        LASTS = r2.take(2, SCH, DEC_B)
        r3 = Carver(arena, RING_0, RING_N)
        HTOK1 = r3.take(3, D)
        GROW = r3.take(CQ + CKV + DR)
        GQN = r3.take(DN)
        GQR = r3.take(DR)
        GKN = r3.take(DN)
        GKNP = r3.take(1, parts=DN)
        COS = r3.take(3, DR // 2)
        SIN = r3.take(3, DR // 2)
        W_UK = r3.take(512)
        W_UV = r3.take(512)
        W_UKT = r3.take(DH, P, parts=DN)
        W_GLU = r3.take(4, 512)
        r3 = Carver(arena, RING_0, RING_N)
        RK = r3.take(2, PAST)
        SUMW = r3.take(4, DH * DEC_T)
        KPP0 = r3.take(PAGES, P)
        KPP = (KPP0, KPP1)
        r3.skip_to(0)
        W_UQ = r3.take(2, DH * DQK)
        RT = r3.take(4, DH, DR // 2)

        DB, AB = banks[0:4], banks[4:8]
        d_full, d_free, a_full, a_free = (sem(n) for n in ("dve_bank_full", "dve_bank_free", "act_bank_full", "act_bank_free"))
        block = ctx.enter_context(nc.Block())

        def live(n):
            return stop >= n

        def pages_of(queue, dst, src, b, name, first=0, count=PAGES):
            for j in range(count):
                at = b * PAGES + first + j
                page = queue.value_load(pages[0:1, at:at + 1], min_val=0, max_val=src.shape[0] - 1)
                queue.dma_start(dst[:, j, :], src[ds(page, 1), :, :].rearrange("a p n -> (a p) n")).then_inc(sem(name), 16)

        @block.sync
        def _(sp):
            nst = [0]

            def load(out, in_, name):
                sp.dma_start(out, in_).then_inc(sem(name), 16)

            def store(out, in_):
                sp.dma_start(out, in_).then_inc(sem("stored"), 16)
                nst[0] += 16

            load(X[:, 0, :], I["x_prompt"][0:P, :], "x_loaded")
            load(X[:, 1, :], I["x_prompt"][P:SEQ, :], "x_loaded")
            load(X[0:NS, 2, :], I["x_sample"], "x_loaded")
            load(ident, I["ident"], "const_loaded")
            load(iota, I["iota"], "const_loaded")
            load(gain, I["gain"], "const_loaded")
            load(group, I["group"], "const_loaded")
            load(before, I["before"], "const_loaded")
            load(pages, I["page_table"], "pages_loaded")
            for n in range(4):
                load(W_IN0[:, :, 512 * n:512 * n + 512], I["ev_w_in"][:, :, 512 * n:512 * n + 512], f"w_in0_loaded{n}")
            load(GAIN0, I["gain0"].partition_broadcast(P), "gain0_loaded")

            def even_stores(t, rows):
                s = "prompt" if t < 2 else "sample"
                a, b = (t * P, t * P + P) if t < 2 else (0, NS)
                store(O[f"a_k_{s}"][a:b, :], Z[0:rows, t, 384:768])
                store(O[f"a_v_{s}"][a:b, :], Z[0:rows, t, VA0:QB0])
                store(O[f"b_k_{s}"][a:b, :], Z[0:rows, t, KB0:VB0])
                store(O[f"b_v_{s}"][a:b, :], Z[0:rows, t, VB0:EVEN_IN])

            sp.wait_ge(sem("heads_normed"), 3)
            load(TBL0, I["tbl0"], "tbl0_loaded")
            for t, rows, _ in TILES:
                even_stores(t, rows)
            for b in range(4):
                load(KA[:, b, :, :], I["cache_a_kt"][b], "ka_loaded")
                load(VA[:, b, :, :], I["cache_a_v"][b], "va_loaded")
            sp.wait_ge(sem("pages_loaded"), 16)
            pages_of(sp, KVS[1], I["pool_kv"], 1, "kvb_loaded1")
            sp.wait_ge(sem("prompt0_done"), 16)
            load(TBLA, I["tbla"], "tbls_loaded")
            load(TBLB, I["tblb"], "tbls_loaded")
            load(TBLBN, I["tblbn"], "tbls_loaded")

            sp.wait_ge(sem("q_spread"), 1)
            pages_of(sp, KVS[3], I["pool_kv"], 3, "kvb_loaded3")
            sp.wait_ge(sem("sample0_done"), 1)
            for b in range(4, DEC_B):
                load(KA[:, b - 4, :, :], I["cache_a_kt"][b], "ka_loaded")
                load(VA[:, b - 4, :, :], I["cache_a_v"][b], "va_loaded")
            for b in (5, 7):
                sp.wait_ge(sem("sample0_done"), b // 2)
                pages_of(sp, KVS[b % 4], I["pool_kv"], b, f"kvb_loaded{b % 4}")
            sp.wait_ge(sem("sample0_done"), 4)
            load(W_OUT, I["ev_w_out"], "w_out_loaded")

            def peer_loads(l):
                sp.wait_ge(sem("x_updated"), 2 * l + 1)
                for n in range(4):
                    load(W_Q[:, :, 512 * n:512 * n + 512], I["peer_w_q"][l, :, :, 512 * n:512 * n + 512], f"w_q_loaded{n}")
                    if n == 0:
                        load(KEYS, I["peer_k"][l], "keys_loaded")
                sp.wait_ge(sem("h_ready"), 6 * (2 * l + 2))
                for s in range(4):
                    sp.dma_start(SLOTS[:, s, 0, :], I["peer_ut"][l, s]).then_inc(sem(f"u_loaded{s}"), 16)

                def slot_loads(i, u, v):
                    for s in range(4):
                        if u:
                            sp.wait_ge(sem("u_split"), i * 4 + (l * NK + s - 3))
                            sp.dma_start(SLOTS[:, s, 0, :], I["peer_ut"][l, ds(i * 4 + s, 1), :, :].rearrange("a p n -> (a p) n")).then_inc(sem(f"u_loaded{s}"), 16)
                        if v:
                            sp.wait_ge(sem("v_split"), i * 4 + (l * NK + s - 3))
                            sp.dma_start(SLOTS[:, s, 1, :], I["peer_v"][l, ds(i * 4 + s, 1), :, :].rearrange("a p n -> (a p) n")).then_inc(sem(f"v_loaded{s}"), 16)

                with sp.Fori(1, QK // 4 + 1) as i:
                    slot_loads(i, True, False)
                sp.wait_ge(sem("hidden_full"), l * NK + QK + 2)
                for s in range(4):
                    sp.dma_start(SLOTS[:, s, 1, :], I["peer_v"][l, s]).then_inc(sem(f"v_loaded{s}"), 16)
                with sp.Fori(1, QK // 4 + 1) as i:
                    slot_loads(i, False, True)
                PRE = 3 * QK // 4 + 2
                with sp.Fori(QK // 4 + 1, PRE) as i:
                    slot_loads(i, True, True)
                if l == 0 and live(3):
                    sp.wait_ge(sem("weights_ready"), 2 * 3 * QK)
                    load(W_IN1, I["od_w_in"], "w_in1_loaded")
                with sp.Fori(PRE, NK // 4) as i:
                    slot_loads(i, True, True)

            if live(2):
                peer_loads(0)
            if live(3):
                sp.wait_ge(sem("x_updated"), 2)
                load(GROW, I["grow"].partition_broadcast(P), "odd_small_loaded")
                load(GQN, I["mla_g_qn"].partition_broadcast(P), "odd_small_loaded")
                load(GQR, I["mla_g_qr"].partition_broadcast(P), "odd_small_loaded")
                load(GKN, I["mla_g_kn"].partition_broadcast(P), "odd_small_loaded")
                load(GKNP, I["mla_g_kn_col"], "odd_small_loaded")
                load(COS, I["cos"], "odd_small_loaded")
                load(SIN, I["sin"], "odd_small_loaded")
                load(W_UK, I["mla_w_uk"], "odd_small_loaded")
                load(W_UV, I["mla_w_uv"], "odd_small_loaded")
                load(W_UKT, I["mla_w_ukt"], "odd_small_loaded")
                load(W_GLU, I["s5_w_glu"], "odd_small_loaded")
                load(TBLD, I["tbld"], "odd_small_loaded")
                load(S5P[:, 0:3, :], I["s5_par"], "odd_small_loaded")
                load(S0, I["state_c"], "odd_small_loaded")
                load(CBD, I["s5_c"], "odd_small_loaded")
                load(DSKIP, I["s5_d"], "odd_small_loaded")
                load(BGLU, I["s5_b_glu"], "odd_small_loaded")
                sp.wait_ge(sem("h_ready"), 18)
                load(W_UQ, I["mla_w_uq"], "w_uq_loaded")
                sp.wait_ge(sem("latents_ready"), 3)
                for t, rows, _ in TILES:
                    s = "prompt" if t < 2 else "sample"
                    a, b = (t * P, t * P + P) if t < 2 else (0, NS)
                    store(O[f"d_ckv_{s}"][a:b, :], Z2[0:rows, t, CQ:CQ + CKV])
                    store(O[f"d_kpe_{s}"][a:b, :], Z2[0:rows, t, CQ + CKV:])
                sp.wait_ge(sem("prompt1_done"), 8)
                load(BBD, I["s5_b"], "s5_b_loaded")
                sp.wait_ge(sem("states_ready"), 2)
                for k, n in enumerate(("c_re", "c_im")):
                    store(O[f"{n}_prompt"], LASTP[:, k, :])
                    store(O[f"{n}_sample"], LASTS[:, k, :, :])
                for b in range(3):
                    pages_of(sp, CKP[:, CKP_OF[b]], I["pool_ckv"], b, "ckp0_loaded")
                sp.wait_ge(sem("y_ready"), 4)
                load(TBLDN, I["tbldn"], "tbldn_loaded")
                for b in (4, 5, 6):
                    pages_of(sp, CKP[:, CKP_OF[b]], I["pool_ckv"], b, "ckp1_loaded")
                sp.wait_ge(sem("pages_used"), 1)
                pages_of(sp, CKP[:, CKP_OF[7]], I["pool_ckv"], 7, "ckp1_loaded", 0, PAGES // 2)
                sp.wait_ge(sem("pages_used"), 4)
                load(W_OUTAB[:, 0], I["od_w_out"][:, :, 0:512], "w_out1_loaded0")
                sp.wait_ge(sem("pages_used"), 6)
                load(W_OUTAB[:, 1], I["od_w_out"][:, :, 512:D], "w_out1_loaded1")
            if live(4):
                peer_loads(1)
            sp.wait_ge(sem("x_updated"), min(stop, 4))
            for t, rows, a in TILES:
                if t < 2:
                    store(O["y_prompt"][a:a + P, :], X[:, t, :])
                else:
                    store(O["y_sample"], X[0:NS, t, :])
            sp.wait_ge(sem("stored"), nst[0])

        @block.gpsimd
        def _(pool):
            pool.wait_ge(sem("pages_loaded"), 16)
            pool.wait_ge(sem("heads_normed"), 3)
            pages_of(pool, KVS[0], I["pool_kv"], 0, "kvb_loaded0")
            pool.wait_ge(sem("q_spread"), 1)
            pages_of(pool, KVS[2], I["pool_kv"], 2, "kvb_loaded2")
            for b in (4, 6):
                pool.wait_ge(sem("sample0_done"), b // 2)
                pages_of(pool, KVS[b % 4], I["pool_kv"], b, f"kvb_loaded{b % 4}")

            def peer(l):
                def u_low_ahead(s, e):
                    pool.wait_ge(sem("u_high"), e + 1)
                    pool.tensor_tensor(UA[:, 2 * (s % 2) + 1, :], SLOTS[:, s, 0, :], UA[:, 2 * (s % 2), :].bitcast(F32), ALU.subtract).then_inc(sem("u_split"), 1)

                with pool.Fori(0, BEFORE // 4) as i:
                    for s in range(4):
                        u_low_ahead(s, i * 4 + (l * NK + s))
                with pool.Fori(BEFORE // 4, QK // 4) as i:
                    for s in range(4):
                        u_low_ahead(s, i * 4 + (l * NK + s))
                        pair = s - BEFORE
                        pool.wait_ge(sem("eq2_ready"), i * 8 + (4 * l * NG + 2 * pair + 1))
                        w = PIECES[:, 1:4, ds(i * (8 * NGT) + 2 * pair * NGT, NGT)].rearrange("p e t -> p t e")
                        pool.tensor_tensor(ONE2[:, 0], bc(EQ2[:, 0], 2, 3), bc(w, 3, QK), ALU.mult).then_inc(sem("one2_by_pool"), 1)
                with pool.Fori(0, NG) as i:
                    pool.wait_ge(sem("eq2_ready"), i + ((4 * l + 1) * NG + 1))
                    w = PIECES[:, 1:4, ds(i * NGT, NGT)].rearrange("p e t -> p t e")
                    pool.tensor_tensor(ONE2[:, 0], bc(EQ2[:, 0], 2, 3), bc(w, 3, QK), ALU.mult).then_inc(sem("one2_by_pool"), 1)

            if live(2):
                peer(0)
            if live(3):
                pool.wait_ge(sem("qk_ready"), 3)
                for b in range(4):
                    pages_of(pool, KPP[0][DR * b:DR * b + DR], I["pool_kpe"], b, "kpp_loaded0")
                pool.wait_ge(sem("s5_bt_ready"), 2)
                n = 0
                for r in range(2):
                    for c in range(2):
                        for b in range(4 * r, 4 * r + 4):
                            if n >= 2:
                                pool.wait_ge(sem("key_squares"), 4 * (n - 1))
                            pages_of(pool, PGB[:, n % 2], I["pool_ckv"][:, :, 0:P], b, f"latents_loaded{n % 2}", 4 * c, 4)
                            n += 1
                pool.wait_ge(sem("states_ready"), 2)
                pages_of(pool, CKP[:, CKP_OF[3]], I["pool_ckv"], 3, "ckp0_loaded_by_pool")
                for b in range(4, DEC_B):
                    pages_of(pool, KPP[1][DR * (b - 4):DR * (b - 3)], I["pool_kpe"], b, "kpp_loaded1")
                pool.wait_ge(sem("pages_used"), 1)
                pages_of(pool, CKP[:, CKP_OF[7], PAGES // 2:], I["pool_ckv"], 7, "ckp1_loaded_by_pool", PAGES // 2, PAGES // 2)
            if live(4):
                peer(1)

        @block.tensor
        def _(pe):
            nd, na = [0], [0]

            def to_dve():
                if nd[0] >= 4:
                    pe.wait_ge(d_free, nd[0] - 3)
                nd[0] += 1
                return DB[(nd[0] - 1) % 4]

            def to_act():
                if na[0] >= 4:
                    pe.wait_ge(a_free, na[0] - 3)
                na[0] += 1
                return AB[(na[0] - 1) % 4]

            def mm(out, pairs):
                for n, (lhsT, rhs) in enumerate(pairs):
                    ins = pe.matmul(out, lhsT, rhs, start=(n == 0), stop=(n == len(pairs) - 1))
                return ins

            def norm(k):
                for t, rows, _ in TILES:
                    pe.wait_ge(sem("h_tok_ready"), 3 * k + t + 1)
                    for c in range(2):
                        bank = to_dve()
                        for j in range(4):
                            src = HTOK[0:rows, t, (4 * c + j) * P:(4 * c + j + 1) * P]
                            ins = pe.transpose(bank[:, j * P:j * P + rows], src, ident[0:rows, 0:rows])
                        ins.then_inc(d_full, 1)

            def prompt_attention(units, name, q_of, k_of, v_of, probs, pt):
                def scores(u):
                    pair, qt = u
                    nk = P * (qt + 1)
                    bank = to_dve()
                    for hh in range(2):
                        h = 2 * pair + hh
                        ins = pe.matmul(bank[:, hh * nk:hh * nk + nk], q_of(h, qt), k_of(h, nk), start=True, stop=True)
                    ins.then_inc(d_full, 1)

                def turn(n, u):
                    pair, qt = u
                    pe.wait_ge(sem(name + "_probs"), n + 1)
                    bank = to_act()
                    for hh in range(2):
                        for kt in range(qt + 1):
                            ins = pe.transpose(bank[:, (hh * (qt + 1) + kt) * P:(hh * (qt + 1) + kt + 1) * P],
                                               probs[:, n % 2, (hh * (qt + 1) + kt) * P:(hh * (qt + 1) + kt + 1) * P], ident)
                    ins.then_inc(a_full, 1)

                def values(n, u):
                    pair, qt = u
                    pe.wait_ge(sem(name + "_pt"), n + 1)
                    bank = to_dve()
                    for hh in range(2):
                        ins = mm(bank[:, hh * HD:hh * HD + HD],
                                 [(pt[:, n % 2, hh * (qt + 1) + kt, :], v_of(2 * pair + hh, kt)) for kt in range(qt + 1)])
                    ins.then_inc(d_full, 1)

                for n in range(len(units) + 2):
                    if n < len(units):
                        scores(units[n])
                    if 1 <= n <= len(units):
                        turn(n - 1, units[n - 1])
                    if n >= 2:
                        values(n - 2, units[n - 2])

            def turn_tokens(src, t, rows, c0, c1, signal_ring):
                for c in range(c0, c1, 4):
                    bank = signal_ring()
                    for j in range(4):
                        ins = pe.transpose(bank[:, j * P:j * P + rows], src(c + j), ident[0:rows, 0:rows])
                    ins.then_inc(a_full if signal_ring is to_act else d_full, 1)

            def out_projection(l, OT):
                pe.wait_ge(sem(f"ot_ready{l}"), 1)
                for n in range(2):
                    if l == 0:
                        w = W_OUT[:, :, 512 * n:512 * n + 512]
                        pe.wait_ge(sem("w_out_loaded"), 16)
                    else:
                        w = W_OUTAB[:, n]
                        pe.wait_ge(sem(f"w_out1_loaded{n}"), 16)
                    for t, rows, a in TILES:
                        bank = to_dve()
                        mm(bank[0:rows, :], [(OT[:, c, a:a + rows], w[:, c, :]) for c in range(KC)]).then_inc(d_full, 1)

            def peer(l):
                norm(2 * l + 1)
                pe.wait_ge(sem("h_ready"), 6 * (2 * l + 2))
                def quad_scores(c):
                    pe.wait_ge(sem("keys_loaded"), 16 * (l + 1))
                    pe.wait_ge(sem("peer_q_ready"), 16 * l + 4 * (c + 1))
                    for t in range(2):
                        bank = to_dve()
                        for j in range(4):
                            ins = pe.matmul(bank[:, j * P:j * P + P], QT[:, 4 * c + j, t * P:t * P + P], KEYS[:, 4 * c + j, :], start=True, stop=True)
                        ins.then_inc(d_full, 1)

                for m in range(2 * PH):
                    if m % 4 == 0:
                        pe.wait_ge(sem(f"w_q_loaded{m // 4}"), 16 * (l + 1))
                    bank = to_act()
                    mm(bank[:, 0:NT], [(W_Q[:, c, m * P:m * P + P], HT[:, c, :]) for c in range(KC)]).then_inc(a_full, 1)
                    if m % 4 == 0 and m >= 4:
                        quad_scores(m // 4 - 1)
                quad_scores(3)
                bank = to_dve()
                for m in range(2 * PH):
                    c, j = m // 4, m % 4
                    ins = pe.matmul(bank[NS * c:NS * c + NS, j * P:j * P + P], QT[:, m, SEQ:NT], KEYS[:, m, :], start=True, stop=True)
                ins.then_inc(d_full, 1)
                if l == 0:
                    pe.nop().then_inc(sem("one_hots_used"), 2)

                def spread(bank, slot, group, pair=None, pool_does=False):
                    pe.wait_ge(sem("one1_ready"), group + 1)
                    by_pool = NG // 2 + NG
                    if slot == 0:
                        pe.wait_ge(sem("one2_by_pool"), pair + (l * by_pool + 1))
                    elif slot == 1:
                        pe.wait_ge(sem("one2_ready"), pair + (l * (4 * NG - by_pool) + 1))
                    elif pool_does:
                        pe.wait_ge(sem("one2_by_pool"), group + (1 + (l + 1) * by_pool - (4 * l + 2) * NG))
                    else:
                        pe.wait_ge(sem("one2_ready"), group + (1 - (l + 1) * by_pool))
                    pe.wait_ge(sem("g_copied"), group + (1 if slot is not None else 2))
                    s = slot or 0
                    for j in range(NGT):
                        for e in range(3):
                            ins = pe.matmul(bank[:, j * QK:(j + 1) * QK], ONE1[:, s, j, :], ONE2[:, s, j, e, :], start=(e == 0), stop=(e == 2))
                    ins.then_inc(sem("one_hots_used"), 1)

                def hidden(s, e):
                    pe.wait_ge(sem("u_split"), e + 1)
                    pe.wait_ge(sem("hidden_bank_free"), e + 2)
                    product(banks[6][:, 0:NT], UV[:, s % 2, 0, :], UV[:, s % 2, 1, :])

                def product(bank, high, low):
                    for c in range(KC):
                        uh, ul = high[:, c * P:(c + 1) * P], low[:, c * P:(c + 1) * P]
                        pe.matmul(bank, uh, HR[:, 0, c, :], start=(c == 0), stop=False)
                        pe.matmul(bank, uh, HR[:, 1, c, :], start=False, stop=False)
                        ins = pe.matmul(bank, ul, HR[:, 0, c, :], start=False, stop=(c == KC - 1))
                    ins.then_inc(sem("hidden_full"), 1)

                def values(s, e):
                    pe.wait_ge(sem("v_split"), e + 1)
                    pe.wait_ge(sem("weights_ready"), e * 2 + 2)
                    k = s % 2
                    for t, rows, a in TILES:
                        for wp, vps in ((0, (2, 3)), (1, (2,))) if t < 2 else ((None, (2, 3)),):
                            lhsT = WR[:, k, wp, a:a + rows] if t < 2 else WRS[:, k, :, :].rearrange("p w t -> p (w t)")
                            for vp in vps:
                                for n in range(2):
                                    ins = pe.matmul(banks[2 * t + n][0:P if t < 2 else 2 * NS, :], lhsT, UV[:, k, vp, 512 * n:512 * n + 512],
                                                    start=False, stop=False, skip_group_check=True)
                    ins.then_inc(sem("values_done"), 1)

                def turn_route(t):
                    pe.wait_ge(sem("route_tok_ready"), 3 * l + t + 1)
                    bank = to_dve()
                    for j in range(3):
                        if t < 2:
                            ins = pe.transpose(bank[:, j * P:j * P + P], ROUTE[:, t, j, :], ident)
                        else:
                            for c in range(4):
                                R = slice(NS * c, NS * c + NS)
                                ins = pe.matmul(bank[R, j * P:j * P + NS], ROUTE[R, t, j, 0:2 * TOPK], ident[R, R], start=True, stop=True)
                    ins.then_inc(d_full, 1)
                e0 = l * NK

                def hidden_ahead(s, e):
                    pe.wait_ge(sem("u_split"), e + 1)
                    pe.wait_ge(sem("hidden_bank_free"), e + 1)
                    product(banks[4 + s % 2][:, 0:NT], UA[:, 2 * (s % 2), :], UA[:, 2 * (s % 2) + 1, :])

                pe.wait_ge(a_free, na[0])
                pe.wait_ge(sem("h_split"), l + 1)
                with pe.Fori(0, BEFORE // 4 - 2) as i:
                    for s in range(4):
                        hidden_ahead(s, i * 4 + (e0 + s))
                turn_route(0)
                for k in (2, 1):
                    for s in range(4):
                        hidden_ahead(s, e0 + BEFORE - 4 * k + s)
                    turn_route(3 - k)
                with pe.Fori(BEFORE // 4, QK // 4) as i:
                    for s in range(4):
                        hidden_ahead(s, i * 4 + (e0 + s))
                        pair = i * 4 + (s - BEFORE)
                        for k in range(2):
                            spread(banks[6 + k], k, i * 8 + (4 * l * NG + 2 * (s - BEFORE) + k), pair)
                pe.wait_ge(d_free, nd[0])
                pe.wait_ge(sem("hidden_bank_free"), e0 + QK + 2)
                pe.wait_ge(sem("g_copied"), (4 * l + 1) * NG + 2)
                pe.wait_ge(sem("zeros_ready"), l + 1)
                for k in range(6):
                    pe.matmul(banks[k][:, :], ZEROS, HT.rearrange("p c n -> p (c n)")[:, 0:512], start=True, stop=False, skip_group_check=True)
                for q in range(4):
                    def body(i, last):
                        for s in range(4):
                            if (q > 0 or (last and s == 3)) and not (last and q == 3 and s == 3):
                                hidden((s + 1) % 4, i * 4 + (e0 + q * QK + s + 1))
                            values(s, i * 4 + (e0 + q * QK + s))
                            if s < 3 and q < 3:
                                spread(banks[7], None, i * 3 + ((4 * l + q + 1) * NG + s), None, q == 0)
                    with pe.Fori(0, QK // 4 - 1) as i:
                        body(i, False)
                    body(QK // 4 - 1, True)
                pe.wait_ge(sem("mix_copied"), l + 1)
                for n in range(2):
                    ins = mm(banks[6 + n][0:NS, :], [(ident[0:2 * NS, NS * w:NS * w + NS], MIXS[:, n, :]) for w in range(2)])
                    ins.then_inc(sem("sample_mix_full"), 1)

            pe.wait_ge(sem("const_loaded"), 80)
            norm(0)
            pe.wait_ge(sem("h_ready"), 6)
            for n in range(4):
                pe.wait_ge(sem(f"w_in0_loaded{n}"), 16)
                for t, rows, a in TILES:
                    bank = to_act()
                    mm(bank[0:rows, :], [(HT[:, c, a:a + rows], W_IN0[:, c, 512 * n:512 * n + 512]) for c in range(KC)]).then_inc(a_full, 1)

            def normed_col(h):
                return h * HD if h < 2 * AH else QB0 + (h - 2 * AH) * HD

            for t, rows, a in TILES:
                pe.wait_ge(sem("heads_normed"), t + 1)
                for c in range(NORMED // 4):
                    bank = to_act()
                    for j in range(4):
                        col = normed_col(4 * c + j)
                        ins = pe.transpose(bank[0:HD, j * P:j * P + rows], Z[0:rows, t, col:col + HD], ident[0:rows, 0:rows])
                    ins.then_inc(a_full, 1)
            pe.wait_ge(sem("qkt_ready"), 18)
            units0 = [(p, qt) for p in range(8) for qt in range(2)]

            def q0(h, qt):
                return QKT[:, h if h < AH else 2 * AH + h - AH, qt * P:qt * P + P]

            def k0(h, nk):
                return QKT[:, AH + h if h < AH else 2 * AH + BH + (h - AH) // GQ, 0:nk]

            def v0(h, kt):
                col = VA0 + h * HD if h < AH else VB0 + (h - AH) // GQ * HD
                return Z[:, kt, col:col + HD]

            prompt_attention(units0, "prompt0", q0, k0, v0, PP_, PTP)
            pe.wait_ge(sem("prompt0_done"), 16)
            for t in range(2):
                turn_tokens(lambda c: O0[:, t, c * P:c * P + P], t, P, 0, 8, to_act)
            def sample_scores(kind, r):
                if kind == "a":
                    pe.wait_ge(sem("ka_loaded"), 4 * 16 * (r + 1))
                    for lo, hi in ((0, 512), (512, AK)):
                        bank = to_dve()
                        for i in range(4):
                            ins = mm(bank[32 * i:32 * i + 32, 0:hi - lo], [(QBA[:, c, 4 * r + i, :], KA[:, i, c, lo:hi]) for c in range(3)])
                        if hi == AK:
                            ins = mm(bank[:, AK - lo:AK - lo + NS],
                                     [(QBA[:, c, 4 * r:4 * r + 4, :].rearrange("p b e -> p (b e)"), KNA[:, c, :]) for c in range(3)])
                        ins.then_inc(d_full, 1)
                else:
                    for i in range(2):
                        pe.wait_ge(sem(f"kvb_loaded{2 * (r % 2) + i}"), 16 * PAGES * (r // 2 + 1))
                    for c in range(2):
                        bank = to_dve()
                        for i in range(2):
                            ins = pe.matmul(bank[64 * i:64 * i + 64, :].rearrange("p (j n) -> p j n", n=P), QBB[:, 2 * r + i, :],
                                            KVS[2 * (r % 2) + i][:, 4 * c:4 * c + 4, 0:P], start=True, stop=True)
                        ins.then_inc(d_full, 1)
                    bank = to_dve()
                    pe.matmul(bank[:, 0:NS], QBB[:, 2 * r:2 * r + 2, :].rearrange("p b e -> p (b e)"), KNB, start=True, stop=True).then_inc(d_full, 1)

            def sample_gate(r):
                pe.wait_ge(sem("gate_ready"), r + 1)
                bank = to_dve()
                pe.matmul(bank[:, 0:NBLK], group, GATE, start=True, stop=True).then_inc(d_full, 1)

            def sample_turn(n, kind):
                pe.wait_ge(sem("sample0_exp"), n + 1)
                chunks = AKC if kind == "a" else PAGES
                for c0 in range(0, chunks + 1, 4):
                    bank = to_act()
                    for c in range(c0, min(c0 + 4, chunks + 1)):
                        w = P if c < chunks else NS
                        ins = pe.transpose(bank[0:w, (c - c0) * P:(c - c0 + 1) * P], SS_[:, n % 2, c * P:c * P + w], ident)
                    ins.then_inc(a_full, 1)

            def sample_values(n, kind, r):
                pe.wait_ge(sem("sample0_pt"), n + 1)
                bank = to_dve()
                if kind == "a":
                    pe.wait_ge(sem("va_loaded"), 4 * 16 * (r + 1))
                    for i in range(4):
                        rows = slice(32 * i, 32 * i + 32)
                        ins = mm(bank[rows, 0:3 * P], [(PTS[:, k, rows], VA[:, i, k, :]) for k in range(AKC)] + [(PTS[0:NS, AKC, rows], Z[0:NS, 2, VA0:QB0])])
                else:
                    for i in range(2):
                        rows = slice(64 * i, 64 * i + 64)
                        ins = mm(bank[rows, 0:P], [(PTS[:, k, rows], KVS[2 * (r % 2) + i][:, k, P:2 * P]) for k in range(PAGES)]
                                 + [(PTS[0:NS, PAGES, rows], Z[0:NS, 2, VB0:EVEN_IN])])
                ins.then_inc(d_full, 1)
                pe.wait_ge(sem("sample0_sums"), n + 1)
                bank = to_dve()
                if kind == "a":
                    for h in range(AH):
                        ins = pe.matmul(bank[HD * (h % 2):HD * (h % 2) + HD, 16 * (h // 2):16 * (h // 2) + 16].rearrange("p (i t) -> p i t", t=DEC_T),
                                        OS_[:, HD * h:HD * h + HD], ident.rearrange("p (i e) -> p i e", e=32)[:, :, 4 * h:4 * h + 4], start=True, stop=True)
                else:
                    for j in range(BH):
                        g, hh = j // GQ, j % GQ
                        at = 32 * g + 4 * hh
                        ins = pe.matmul(bank[HD * (j % 2):HD * (j % 2) + HD, 8 * (j // 2):8 * (j // 2) + 8].rearrange("p (i t) -> p i t", t=DEC_T),
                                        OS_[:, HD * g:HD * g + HD], ident.rearrange("p (i e) -> p i e", e=64)[:, :, at:at + 4], start=True, stop=True)
                ins.then_inc(d_full, 1)

            pe.wait_ge(sem("q_spread"), 1)
            for n in range(len(SUNITS) + 1):
                if n < len(SUNITS):
                    sample_scores(*SUNITS[n])
                if n >= 1:
                    sample_turn(n - 1, SUNITS[n - 1][0])
                if n < len(SUNITS) and SUNITS[n][0] == "b":
                    sample_gate(SUNITS[n][1])
                if n >= 1:
                    sample_values(n - 1, *SUNITS[n - 1])
            out_projection(0, OT0)
            if live(2):
                peer(0)

            def odd():
                norm(2)
                pe.wait_ge(sem("h_ready"), 18)
                pe.wait_ge(sem("w_in1_loaded"), 16)
                for t, rows, a in TILES:
                    bank = to_act()
                    mm(bank[0:rows, 0:416], [(HT[:, c, a:a + rows], W_IN1[:, c, 512:928]) for c in range(KC)]).then_inc(a_full, 1)
                for m in range(4):
                    bank = to_act()
                    mm(bank[:, 0:NT], [(W_IN1[:, c, m * P:m * P + P], HT[:, c, :]) for c in range(KC)]).then_inc(a_full, 1)
                for t, rows, a in TILES:
                    pe.wait_ge(sem("latents_ready"), t + 1)
                    bank = to_dve()
                    for j in range(3):
                        ins = pe.transpose(bank[:, j * P:j * P + rows], Z2[0:rows, t, j * P:j * P + P], ident[0:rows, 0:rows])
                    ins.then_inc(d_full, 1)
                pe.wait_ge(sem("latents_turned"), 3)
                pe.wait_ge(sem("w_uq_loaded"), 16)
                pe.wait_ge(sem("odd_small_loaded"), 16 * 17)
                for t, rows, a in TILES:
                    for n in range(2):
                        bank = to_act()
                        mm(bank[0:rows, 0:384], [(CQT[:, c, a:a + rows], W_UQ[:, c, 384 * n:384 * n + 384]) for c in range(2)]).then_inc(a_full, 1)
                    for w in (W_UK, W_UV):
                        bank = to_act()
                        pe.matmul(bank[0:rows, :], CKT[:, a:a + rows], w, start=True, stop=True).then_inc(a_full, 1)
                for t, rows, a in TILES:
                    pe.wait_ge(sem("qk_ready"), t + 1)
                    for src in (Q, KCAT):
                        if src is KCAT and t == 2:
                            continue
                        for c in range(2):
                            bank = to_act()
                            for j in range(4):
                                ins = pe.transpose(bank[0:DQK, j * P:j * P + rows], src[0:rows, t, 4 * c + j, :], ident[0:rows, 0:rows])
                            ins.then_inc(a_full, 1)
                pe.wait_ge(sem("qct_ready"), 10)
                units = [(p, qt) for p in range(4) for qt in range(2)]
                prompt_attention(units, "prompt1", lambda h, qt: QCT[:, h, qt * P:qt * P + P], lambda h, nk: KCT[:, h, 0:nk],
                                 lambda h, kt: VD[:, kt, h * HD:h * HD + HD], P_D, PT_D)
                pe.wait_ge(sem("prompt1_done"), 8)
                for t in range(2):
                    turn_tokens(lambda c: O1[:, t, c * P:c * P + P], t, P, 0, 4, to_act)
                pe.wait_ge(sem("s5_b_scaled"), 1)
                for k in range(2):
                    bank = to_act()
                    for j in range(4):
                        ins = pe.transpose(bank[:, j * P:j * P + P], BSC[:, k, 4 * j:4 * j + 4, :].rearrange("p s c -> p (s c)"), ident)
                    ins.then_inc(a_full, 1)
                pe.wait_ge(sem("s5_bt_ready"), 2)
                pe.wait_ge(sem("sum_weights_ready"), 1)

                def key_norms(r):
                    total = None
                    for n in range(33):
                        if n < 32:
                            c, i, m = n // 16, n // 4 % 4, n % 4
                            if m == 0:
                                k = 8 * r + 4 * c + i
                                pe.wait_ge(sem(f"latents_loaded{k % 2}"), 64 * (k // 2 + 1))
                            bank = to_act()
                            ins = pe.matmul(bank[:, :], W_UK[:, m * P:m * P + P], PGB[:, k % 2, :, :].rearrange("p j n -> p (j n)"), start=True, stop=True)
                            ins.then_inc(a_full, 1)
                        if n >= 1:
                            i, m = (n - 1) // 4 % 4, (n - 1) % 4
                            if (n - 1) % 16 == 0:
                                total = to_dve()
                            pe.wait_ge(sem("key_squares"), 32 * r + n)
                            ins = pe.matmul(total[32 * i:32 * i + 32, :], SUMW[:, m, :], KSQ[:, (n - 1) % 2, :], start=(m == 0), stop=(m == 3))
                            ins.then_inc(sem("key_squares_used"), 1)
                            if n % 16 == 0:
                                pe.wait_ge(sem("key_squares_used"), 32 * r + n)
                                pe.nop().then_inc(d_full, 1)

                for hf in range(2):
                    for s in range(SG2 * hf, SG2 * hf + SG2):
                        rows = slice(32 * (s % 4), 32 * (s % 4) + 32)
                        for k in range(2):
                            bank = to_act()
                            pe.matmul(bank[:, 0:NT], BT[rows, k, s // 4, :], UT[rows, s // 4, :], start=True, stop=True).then_inc(a_full, 1)
                    key_norms(hf)
                    pe.wait_ge(sem("states_ready"), hf + 1)
                    for c in range(2 * hf, 2 * hf + 2):
                        bank = to_dve()
                        for q in range(4):
                            s = 4 * c + q
                            rows = slice(32 * q, 32 * q + 32)
                            ins = mm(bank[rows, 0:NT], [(CBD[:, k, s, :], BU[:, k, s % SG2, :]) for k in range(2)])
                        ins.then_inc(d_full, 1)
                pe.wait_ge(sem("zg_ready"), 4)
                for m in range(4):
                    bank = to_act()
                    mm(bank[:, 0:NT], [(W_GLU[:, c, m * P:m * P + P], ZG[:, c, :]) for c in range(4)]).then_inc(a_full, 1)
                pe.wait_ge(sem("qg_ready"), 1)
                bank = to_dve()
                for h in range(DH):
                    ins = pe.matmul(bank[:, h * NS:h * NS + NS], W_UKT[:, h, :], QG[:, h, :], start=True, stop=True)
                ins.then_inc(d_full, 1)
                pe.wait_ge(sem("qabs_ready"), 1)
                for r in range(2):
                    slot = CKP_OF[4 * r:4 * r + 4]
                    pe.wait_ge(sem(f"ckp{r}_loaded"), 16 * (3 * PAGES + r * PAGES // 2))
                    pe.wait_ge(sem(f"ckp{r}_loaded_by_pool"), 16 * (PAGES - r * PAGES // 2))
                    pe.wait_ge(sem(f"kpp_loaded{r}"), 4 * 16 * PAGES)
                    for lat in (True, False):
                        for c in range(2):
                            bank = to_dve()
                            for i in range(4):
                                R = slice(0, P) if lat else slice(DR * i, DR * i + DR)
                                q = (QABS if lat else QPE)[R, 4 * r + i, :, :].rearrange("p h t -> p (h t)")
                                key = CKP[:, slot[i], 4 * c:4 * c + 4, 0:P] if lat else KPP[r][R, 4 * c:4 * c + 4, :]
                                ins = pe.matmul(bank[32 * i:32 * i + 32, :].rearrange("p (j n) -> p j n", n=P), q, key, start=True, stop=True)
                            ins.then_inc(d_full, 1)
                    bank = to_dve()
                    B = slice(4 * r, 4 * r + 4)
                    pe.matmul(bank[:, 0:NS], QABS[:, B].rearrange("p b h t -> p (b h t)"), CKT[:, SEQ:NT], start=True, stop=True)
                    pe.matmul(bank[:, NS:2 * NS], QPE[0:DR, B].rearrange("p b h t -> p (b h t)"), KPEN, start=True, stop=True)
                    for i in range(4):
                        ins = pe.matmul(bank[32 * i:32 * i + 32, 2 * NS:3 * NS], RKN[0:NS, :, :].rearrange("p h t -> p (h t)"), ident[0:NS, 0:NS], start=True, stop=True)
                    ins.then_inc(d_full, 1)
                    pe.wait_ge(sem("sd_exp"), r + 1)
                    for c0 in range(0, PAGES + 1, 4):
                        bank = to_act()
                        for c in range(c0, min(c0 + 4, PAGES + 1)):
                            w = P if c < PAGES else NS
                            ins = pe.transpose(bank[0:w, (c - c0) * P:(c - c0 + 1) * P], S_SD[:, c * P:c * P + w], ident)
                        ins.then_inc(a_full, 1)
                    pe.wait_ge(sem("sd_pt"), 3 * (r + 1))
                    bank = to_dve()
                    for i in range(4):
                        rows = slice(32 * i, 32 * i + 32)
                        ins = mm(bank[rows, 0:P], [(PT_SD[:, k, rows], CKP[:, slot[i], k, P:2 * P]) for k in range(PAGES)]
                                 + [(PT_SD[0:NS, PAGES, rows], Z2[0:NS, 2, CQ:CQ + CKV])])
                        ins.then_inc(sem("pages_used"), 1)
                    pe.wait_ge(sem("pages_used"), 4 * (r + 1))
                    pe.nop().then_inc(d_full, 1)
                    pe.wait_ge(sem("osd_ready"), r + 1)
                    bank = to_dve()
                    pe.transpose(bank[:, 0:P], OSD, ident).then_inc(d_full, 1)
                pe.wait_ge(sem("ct_ready"), 2)
                bank = to_dve()
                for h in range(DH):
                    ins = pe.matmul(bank[0:NS, h * HD:h * HD + HD], CT[:, h, :], W_UV[:, h * HD:h * HD + HD], start=True, stop=True)
                ins.then_inc(d_full, 1)
                pe.wait_ge(sem("o1_sample_ready"), 1)
                turn_tokens(lambda c: S_SD[0:NS, c * P:c * P + P], 2, NS, 0, 4, to_act)
                out_projection(1, OT1)

            if live(3):
                odd()
            if live(4):
                peer(1)

        @block.scalar
        def _(act):
            nf, chain, done = [0], [0], {}

            def full():
                act.wait_ge(a_full, nf[0] + 1)
                nf[0] += 1
                return AB[(nf[0] - 1) % 4]

            def link(ins):
                chain[0] += 1
                ins.then_inc(sem("act_step"), 1)
                act.wait_ge(sem("act_step"), chain[0])

            def copy_out(out, src, name):
                link(act.copy(out, src))
                act.nop().then_inc(a_free, 1)
                act.nop().then_inc(sem(name), 1)

            def norm(k):
                if k == 0:
                    act.wait_ge(sem("x_loaded"), 48)
                    act.wait_ge(sem("ss_set"), 1)
                else:
                    act.wait_ge(sem("x_updated"), k)
                for t, rows, _ in TILES:
                    ins = act.activation(HTOK[0:rows, t, :], X[0:rows, t, :], ACT.Square, accum_out=ss[0:rows, t:t + 1])
                    ins.then_inc(sem("squares_ready"), 1)
                act.wait_ge(sem("norm_var"), k + 1)
                act.activation(rinv, rinv, ACT.Sqrt).then_inc(sem("norm_rinv"), 1)

            def exps_prompt(units, name, src, dst, scale):
                for n in range(len(units) + 1):
                    if n < len(units):
                        pair, qt = units[n]
                        nk = P * (qt + 1)
                        act.wait_ge(sem(name + "_scores"), n + 1)
                        if n >= 4:
                            act.wait_ge(sem(name + "_done"), n - 3)
                        for hh in range(2):
                            ins = act.activation(dst[:, n % 2, hh * nk:hh * nk + nk], src[:, n % 2, hh * nk:hh * nk + nk], ACT.Exp,
                                                 bias=MX[:, n % 2, hh:hh + 1], scale=scale, accum_out=SUMS[:, n % 4, hh:hh + 1])
                            if hh == 0:
                                link(ins)
                        ins.then_inc(sem(name + "_probs"), 1)
                    if n >= 1:
                        pair, qt = units[n - 1]
                        bank = full()
                        w = 2 * (qt + 1) * P
                        pt = PTP if name == "prompt0" else PT_D
                        copy_out(pt[:, (n - 1) % 2, 0:2 * (qt + 1), :].rearrange("p a b -> p (a b)"), bank[:, 0:w], name + "_pt")

            def peer(l):
                norm(2 * l + 1)
                for m in range(2 * PH):
                    copy_out(QT[:, m, :], full()[:, 0:NT], "peer_q_ready")
                if l == 0:
                    act.nop().then_inc(sem("g_copied"), 2)
                    act.nop().then_inc(sem("hidden_bank_free"), 2)
                    act.nop().then_inc(sem("hidden_full"), 2)
                    act.nop().then_inc(sem("values_done"), 2)
                e0 = l * NK

                def g_copy(bank, row, t0, group):
                    act.wait_ge(sem("one_hots_used"), group + 3)
                    act.copy(G[:, row:row + QK, ds(t0, NGT)].rearrange("p j t -> p t j"),
                             bank[:, 0:NGT * QK].rearrange("p (t j) -> p t j", j=QK)).then_inc(sem("g_copied"), 1)

                def u_high(s, e, out=None):
                    act.wait_ge(sem(f"u_loaded{s}"), e * 4 + (16 - 4 * s))
                    act.wait_ge(sem("hidden_full"), e + 1)
                    act.copy(UV[:, s % 2, 0, :] if out is None else out, SLOTS[:, s, 0, :]).then_inc(sem("u_high"), 1)

                def v_high(s, e):
                    act.wait_ge(sem(f"v_loaded{s}"), e * 4 + (16 - 4 * s))
                    act.wait_ge(sem("values_done"), e + 1)
                    act.copy(UV[:, s % 2, 2, :], SLOTS[:, s, 1, :]).then_inc(sem("v_high"), 1)

                def hidden_act(s, e):
                    act.wait_ge(sem("hidden_full"), e + 3)
                    act.wait_ge(sem("actv_free"), e + 1)
                    act.activation(ACTV[:, s % 2, :], banks[6][:, 0:NT], ACT.Gelu_apprx_tanh).then_inc(sem("hidden_bank_free"), 1)

                def ahead(i, spreads, last=False):
                    for s in range(4):
                        e = i * 4 + (e0 + s)
                        act.wait_ge(sem("hidden_full"), e + 3)
                        act.activation(G[:, ds(i * 4 + (QK + s), 1), :].rearrange("p a t -> p (a t)"), banks[4 + s % 2][:, 0:NT],
                                       ACT.Gelu_apprx_tanh).then_inc(sem("hidden_bank_free"), 1)
                        if not (last and s >= 2):
                            u_high((s + 2) % 4, e + 2, UA[:, 2 * (s % 2), :])
                        if spreads:
                            for k in range(2):
                                pair = s - BEFORE
                                g_copy(banks[6 + k], 0, i * (8 * NGT) + (2 * pair + k) * NGT, i * 8 + (4 * l * NG + 2 * pair + k))

                def route_exp(t):
                    act.wait_ge(sem("sel_diff"), 3 * l + t + 1)
                    w = P if t < 2 else 2 * TOPK
                    act.activation(ROUTE[:, t, 2, 0:w], ROUTE[:, t, 2, 0:w], ACT.Exp).then_inc(sem("sel_exp"), 1)

                u_high(0, e0, UA[:, 0, :])
                u_high(1, e0 + 1, UA[:, 2, :])
                with act.Fori(0, 2) as i:
                    ahead(i, False)
                for t in range(3):
                    route_exp(t)
                    ahead(2 + t, False)
                assert BEFORE // 4 == 5
                with act.Fori(BEFORE // 4, QK // 4 - 1) as i:
                    ahead(i, True)
                ahead(QK // 4 - 1, True, True)
                v_high(0, e0)
                act.wait_ge(sem("first_weighted"), l + 1)
                for q in range(4):
                    def body(i, last):
                        for s in range(4):
                            e = i * 4 + (e0 + q * QK + s)
                            end = last and q == 3
                            if (q > 0 or (last and s >= 2)) and not (end and s >= 2):
                                u_high((s + 2) % 4, e + 2)
                            if not (end and s == 3):
                                v_high((s + 1) % 4, e + 1)
                            if s >= 1 and q < 3:
                                g_copy(banks[7], (q + 1) % 2 * QK, (i * 3 + (s - 1)) * NGT, i * 3 + ((4 * l + q + 1) * NG + s - 1))
                            if (q > 0 or (last and s == 3)) and not (end and s == 3):
                                hidden_act((s + 1) % 4, e + 1)
                    with act.Fori(0, QK // 4 - 1) as i:
                        body(i, False)
                    body(QK // 4 - 1, True)
                act.wait_ge(sem("values_done"), (l + 1) * NK + 2)
                for n in range(2):
                    link(act.copy(MIXS[:, n, :], banks[4 + n][0:2 * NS, :]))
                act.nop().then_inc(sem("mix_copied"), 1)

            norm(0)
            for n in range(4):
                for t, rows, a in TILES:
                    copy_out(Z[0:rows, t, 512 * n:512 * n + 512], full()[0:rows, :], "z_ready")
            for t, rows, a in TILES:
                act.wait_ge(sem("heads_var"), t + 1)
                act.activation(RS24[0:rows, :], RS24[0:rows, :], ACT.Sqrt).then_inc(sem("heads_rinv"), 1)
            for t, rows, a in TILES:
                for c in range(NORMED // 4):
                    copy_out(QKT[:, 4 * c:4 * c + 4, a:a + rows], full()[0:HD, :].rearrange("p (j n) -> p j n", n=P)[:, :, 0:rows], "qkt_ready")
            units0 = [(p, qt) for p in range(8) for qt in range(2)]
            exps_prompt(units0, "prompt0", SP_, PP_, 1.0)
            for t in range(2):
                for c in range(2):
                    copy_out(OT0[:, 4 * c:4 * c + 4, t * P:t * P + P], full()[:, :].rearrange("p (j n) -> p j n", n=P), "ot0_prompt")
            for n in range(len(SUNITS) + 1):
                if n >= 1:
                    chunks = AKC if SUNITS[n - 1][0] == "a" else PAGES
                    for c0 in range(0, chunks + 1, 4):
                        bank = full()
                        c1 = min(c0 + 4, chunks)
                        if c1 > c0:
                            link(act.copy(PTS[:, c0:c1, :].rearrange("p a b -> p (a b)"), bank[:, 0:(c1 - c0) * P]))
                        if c0 + 4 > chunks:
                            link(act.copy(PTS[0:NS, chunks, :], bank[0:NS, (chunks - c0) * P:(chunks - c0 + 1) * P]))
                        act.nop().then_inc(a_free, 1)
                    act.nop().then_inc(sem("sample0_pt"), 1)
                if n < len(SUNITS):
                    width = (AK if SUNITS[n][0] == "a" else PAST) + NS
                    act.wait_ge(sem("sample0_scores"), n + 1)
                    act.activation(SS_[:, n % 2, 0:width], SS_[:, n % 2, 0:width], ACT.Exp, bias=MX1[:, n % 2:n % 2 + 1],
                                   accum_out=SUM1[:, n % 2:n % 2 + 1]).then_inc(sem("sample0_exp"), 1)
            act.wait_ge(sem("ot0_sample"), 1)
            act.nop().then_inc(sem("ot_ready0"), 1)
            if live(2):
                peer(0)

            def odd():
                norm(2)
                act.wait_ge(sem("odd_small_loaded"), 16 * 17)
                act.activation(S5P[:, 3, :], S5P[:, 2, :], ACT.Exp).then_inc(sem("s5_dt"), 1)
                for t, rows, a in TILES:
                    copy_out(Z2[0:rows, t, :], full()[0:rows, 0:416], "z2_ready")
                act.wait_ge(sem("s5_angles"), 1)
                act.activation(S5P[:, 7, :], S5P[:, 4, :], ACT.Exp).then_inc(sem("s5_mag"), 1)
                act.activation(S5P[:, 8, :], S5P[:, 6, :], ACT.Sin).then_inc(sem("s5_mag"), 1)
                act.activation(S5P[:, 9, :], S5P[:, 5, :], ACT.Sin).then_inc(sem("s5_mag"), 1)
                for m in range(4):
                    copy_out(UT[:, m, :], full()[:, 0:NT], "ut_ready")
                    if m < 3:
                        rows = TILES[m][1]
                        act.wait_ge(sem("latent_var"), m + 1)
                        act.activation(ST8I[0:rows, m, 0:3], ST8[0:rows, m, 0:3], ACT.Sqrt).then_inc(sem("latent_rinv"), 1)
                for t, rows, a in TILES:
                    for n in range(2):
                        copy_out(Q[0:rows, t, 4 * n:4 * n + 4, :].rearrange("p a b -> p (a b)"), full()[0:rows, 0:384], "qkv_ready")
                    copy_out(KR[0:rows, t, :], full()[0:rows, :], "qkv_ready")
                    copy_out(VD[0:rows, t, :], full()[0:rows, :], "qkv_ready")
                    act.wait_ge(sem("qk_var"), t + 1)
                    act.activation(ST8I[0:rows, t, 0:24], ST8[0:rows, t, 0:24], ACT.Sqrt).then_inc(sem("qk_rinv"), 1)
                for t, rows, a in TILES:
                    for dst in (QCT, KCT):
                        if dst is KCT and t == 2:
                            continue
                        for c in range(2):
                            copy_out(dst[:, 4 * c:4 * c + 4, a:a + rows], full()[0:DQK, :].rearrange("p (j n) -> p j n", n=P)[:, :, 0:rows], "qct_ready")
                units = [(p, qt) for p in range(4) for qt in range(2)]
                exps_prompt(units, "prompt1", S_D, P_D, SCALE_D)
                for t in range(2):
                    copy_out(OT1[:, 4:8, t * P:t * P + P], full()[:, :].rearrange("p (j n) -> p j n", n=P), "ot1_prompt")
                for k in range(2):
                    copy_out(BT[:, k, :, :].rearrange("p a b -> p (a b)"), full()[:, :], "s5_bt_ready")
                for hf in range(2):
                    if hf == 1:
                        act.wait_ge(sem("y_ready"), 2)
                    for s in range(SG2):
                        for k in range(2):
                            copy_out(BU[:, k, s, :], full()[:, 0:NT], "bu_ready")
                    for n in range(32 * hf, 32 * hf + 32):
                        bank = full()
                        if n >= 2:
                            act.wait_ge(sem("key_squares_used"), n - 1)
                        link(act.activation(KSQ[:, n % 2, :], bank[:, :], ACT.Square))
                        act.nop().then_inc(a_free, 1)
                        act.nop().then_inc(sem("key_squares"), 1)
                act.wait_ge(sem("y_ready"), 4)
                for m in range(4):
                    act.activation(ZG[:, m, :], Y[:, m, :], ACT.Gelu_apprx_tanh).then_inc(sem("zg_ready"), 1)
                for m in range(4):
                    bank = full()
                    link(act.activation(SGM[:, m, :], bank[:, 0:NT], ACT.Sigmoid, bias=BGLU[:, m:m + 1]))
                    act.nop().then_inc(a_free, 1)
                    act.nop().then_inc(sem("sgm_ready"), 1)
                act.wait_ge(sem("key_vars"), 2)
                act.activation(RK, RK, ACT.Sqrt).then_inc(sem("key_roots"), 1)
                for r in range(2):
                    act.wait_ge(sem("sd_scores"), r + 1)
                    act.activation(S_SD, S_SD, ACT.Exp, bias=MX1[:, 0:1], scale=SCALE_D, accum_out=SUM1[:, 0:1]).then_inc(sem("sd_exp"), 1)
                    for c0 in range(0, PAGES + 1, 4):
                        bank = full()
                        if c0 < PAGES:
                            link(act.copy(PT_SD[:, c0:c0 + 4, :].rearrange("p a b -> p (a b)"), bank[:, :]))
                        else:
                            link(act.copy(PT_SD[0:NS, PAGES, :], bank[0:NS, 0:P]))
                        act.nop().then_inc(a_free, 1)
                        act.nop().then_inc(sem("sd_pt"), 1)
                act.wait_ge(sem("qabs_ready"), 1)
                bank = full()
                link(act.copy(OT1[:, 4:8, SEQ:NT], bank[:, :].rearrange("p (j n) -> p j n", n=P)[:, :, 0:NS]))
                act.nop().then_inc(a_free, 1)
                act.wait_ge(sem("oc_ready"), 4)
                act.nop().then_inc(sem("ot_ready1"), 1)

            if live(3):
                odd()
            if live(4):
                peer(1)

        @block.vector
        def _(dve):
            nf, chain = [0], [0]

            def full():
                dve.wait_ge(d_full, nf[0] + 1)
                nf[0] += 1
                return DB[(nf[0] - 1) % 4]

            def free():
                dve.nop().then_inc(d_free, 1)

            def step(ins):
                chain[0] += 1
                ins.then_inc(sem("dve_step"), 1)

            def settle():
                dve.wait_ge(sem("dve_step"), chain[0])

            def link(ins):
                step(ins)
                settle()

            def say(name, n=1):
                dve.nop().then_inc(sem(name), n)

            def TT(out, a, b, op):
                link(dve.tensor_tensor(out, a, b, op))

            def TS(out, a, s1, s2, op0, op1=None):
                link(dve.tensor_scalar(out, a, s1, s2, op0, op1) if op1 is not None else dve.tensor_scalar(out, a, s1, None, op0))

            def STT(out, a, s, b, op0, op1):
                link(dve.scalar_tensor_tensor(out=out, in0=a, scalar=s, in1=b, op0=op0, op1=op1))

            def norm(k):
                dve.wait_ge(sem("squares_ready"), 3 * (k + 1))
                TS(rinv, ss, 1.0 / D, EPS, ALU.mult, ALU.add)
                link(dve.reciprocal(rinv, rinv))
                say("norm_var")
                dve.wait_ge(sem("norm_rinv"), k + 1)
                for t, rows, _ in TILES:
                    TS(HTOK[0:rows, t, :], X[0:rows, t, :], rinv[0:rows, t:t + 1], None, ALU.mult)
                    say("h_tok_ready")
                for t, rows, a in TILES:
                    for c in range(2):
                        bank = full()
                        TT(HT[:, 4 * c:4 * c + 4, a:a + rows], bank[:, :].rearrange("p (j n) -> p j n", n=P)[:, :, 0:rows],
                           bc(gain[:, k, 4 * c:4 * c + 4], 2, rows), ALU.mult)
                        free()
                        say("h_ready")

            def prompt_attention(units, name, scores, tables, out, scale):
                def first(n):
                    pair, qt = units[n]
                    nk = P * (qt + 1)
                    bank = full()
                    s = scores[:, n % 2, 0:2 * nk]
                    if n >= 2:
                        dve.wait_ge(sem(name + "_probs"), n - 1)
                    tables(s, bank, pair, qt, nk)
                    free()
                    link(dve.tensor_reduce(MX[:, n % 2, :], s.rearrange("p (h k) -> p h k", h=2), AX, ALU.max, negate=True))
                    if scale != 1.0:
                        TS(MX[:, n % 2, :], MX[:, n % 2, :], scale, None, ALU.mult)
                    say(name + "_scores")

                def second(n):
                    pair, qt = units[n]
                    dve.wait_ge(sem(name + "_probs"), n + 1)
                    link(dve.reciprocal(RSUM, SUMS[:, n % 4, :]))
                    bank = full()
                    TT(out[:, qt, pair * P:pair * P + P].rearrange("p (h d) -> p h d", h=2), bank[:, 0:P].rearrange("p (h d) -> p h d", h=2),
                       bc(RSUM, 2, HD), ALU.mult)
                    free()
                    say(name + "_done")

                for n in range(len(units) + 2):
                    if n < len(units):
                        first(n)
                    if n >= 2:
                        second(n - 2)

            def add_to_x(k):
                for n in range(2):
                    for t, rows, a in TILES:
                        bank = full()
                        TT(X[0:rows, t, 512 * n:512 * n + 512], X[0:rows, t, 512 * n:512 * n + 512], bank[0:rows, :], ALU.add)
                        free()
                say("x_updated")

            def top16(values, rest, top, index, groups):
                for g in groups:
                    step(dve.max(top(g)[:, 0:8], values(g)))
                settle()
                for g in groups:
                    step(dve.match_replace(rest(g), top(g)[:, 0:8], values(g), NEG))
                    step(dve.max_index(index(g)[:, 0:8], top(g)[:, 0:8], values(g)))
                settle()
                for g in groups:
                    step(dve.max(top(g)[:, 8:16], rest(g)))
                settle()
                for g in groups:
                    step(dve.max_index(index(g)[:, 8:16], top(g)[:, 8:16], rest(g)))
                settle()

            def peer(l):
                norm(2 * l + 1)
                link(dve.tensor_copy(HR[:, 0], HT))
                TT(HR[:, 1], HT, HR[:, 0].bitcast(F32), ALU.subtract)
                say("h_split")

                def search(t, h0):
                    bank = full()
                    top16(lambda g: bank[:, g * NK:(g + 1) * NK], lambda g: SC2[:, g, :], lambda g: TOPV[:, t, h0 + g // 2, g % 2, :],
                          lambda g: TOPI[:, t, h0 + g // 2, g % 2, :], range(4))
                    free()
                    H = slice(h0, h0 + 2)
                    TT(CAND, bc(TOPV[:, t, H, 0, :], 3, TOPK), bc(TOPV[:, t, H, 1, :], 2, TOPK), ALU.add)
                    top16(lambda g: CAND[:, g].rearrange("p a b -> p (a b)"), lambda g: CAND2[:, g].rearrange("p a b -> p (a b)"),
                          lambda g: SELV[:, t, h0 + g, :], lambda g: SELJ[:, t, h0 + g, :], range(2))

                for c in range(4):
                    for t in range(2):
                        search(t, 2 * c)
                search(2, 0)
                for t, rows, a in TILES:
                    nh = PH if t < 2 else 2
                    H = slice(0, nh)
                    gw = ROUTE[:, t, 2, 0:nh * TOPK].rearrange("p (h k) -> p h k", h=nh)
                    TT(gw, SELV[:, t, H], SELV[:, t, H, 0:1].broadcast_to([P, nh, TOPK]), ALU.subtract)
                    say("sel_diff")
                    step(dve.tensor_copy(TOPIF[:, H], TOPI[:, t, H]))
                    step(dve.tensor_scalar(SELAB[:, 0, H], SELJ[:, t, H], 4, None, ALU.logical_shift_right))
                    step(dve.tensor_scalar(SELAB[:, 1, H], SELJ[:, t, H], 15, None, ALU.bitwise_and))
                    settle()
                    link(dve.tensor_copy(SELABF[:, :, H], SELAB[:, :, H]))
                    for k in range(2):
                        TT(EQ[:, H].rearrange("p h k c -> p (h k) c"), bc(SELABF[:, k, H].rearrange("p h k -> p (h k)"), 2, TOPK),
                           bc(iota[:, 0:TOPK], 1, nh * TOPK), ALU.is_equal)
                        TT(EQ[:, H], EQ[:, H], bc(TOPIF[:, H, k, :], 2, TOPK), ALU.mult)
                        link(dve.tensor_reduce(ROUTE[:, t, k, 0:nh * TOPK], EQ[:, H].rearrange("p h k c -> p (h k) c"), AX, ALU.add))
                    dve.wait_ge(sem("sel_exp"), 3 * l + t + 1)
                    link(dve.tensor_reduce(GSUM[:, H], gw, AX, ALU.add))
                    link(dve.reciprocal(GSUM[:, H], GSUM[:, H]))
                    TT(gw, gw, bc(GSUM[:, H], 2, TOPK), ALU.mult)
                    say("route_tok_ready")
                for t, rows, a in TILES:
                    bank = full()
                    link(dve.tensor_copy(ROUTET[:, :, a:a + rows], bank[:, 0:3 * P].rearrange("p (j n) -> p j n", n=P)[:, :, 0:rows]))
                    free()
                link(dve.memset(ZEROS, 0.0))
                say("zeros_ready")
                if l == 0:
                    say("actv_free", 2)
                g, rest = ROUTET[:, 2, :], WFULL[:, 0, :]
                link(dve.tensor_copy(PIECES[:, 0, :], ROUTET[:, 1, :]))
                link(dve.tensor_copy(PIECES[:, 4, :], ROUTET[:, 0, :]))
                link(dve.tensor_copy(PIECES[:, 1, :], g))
                TT(rest, g, PIECES[:, 1, :], ALU.subtract)
                link(dve.tensor_copy(PIECES[:, 2, :], rest))
                TT(rest, rest, PIECES[:, 2, :], ALU.subtract)
                link(dve.tensor_copy(PIECES[:, 3, :], rest))
                say("pieces_ready")
                e0 = l * NK

                def u_low(s, e):
                    dve.wait_ge(sem("u_high"), e + 1)
                    dve.tensor_tensor(UV[:, s % 2, 1, :], SLOTS[:, s, 0, :], UV[:, s % 2, 0, :].bitcast(F32), ALU.subtract).then_inc(sem("u_split"), 1)

                def v_low(s, e):
                    dve.wait_ge(sem("v_high"), e + 1)
                    dve.tensor_tensor(UV[:, s % 2, 3, :], SLOTS[:, s, 1, :], UV[:, s % 2, 2, :].bitcast(F32), ALU.subtract).then_inc(sem("v_split"), 1)

                def one_hots(t0, slot, group):
                    dve.wait_ge(sem("one_hots_used"), group + (1 if slot is not None else 2))
                    s = slot or 0
                    q = q_of[0]
                    dve.tensor_tensor(EQ2[:, s], bc(PIECES[:, 0, ds(t0, NGT)], 2, QK), bc(iota[:, QK * q:QK * q + QK], 1, NGT), ALU.is_equal).then_inc(sem("eq2_ready"), 1)
                    dve.tensor_tensor(ONE1[:, s], bc(PIECES[:, 4, ds(t0, NGT)], 2, NK), bc(iota, 1, NGT), ALU.is_equal).then_inc(sem("one1_ready"), 1)
                    if slot == 0 or q_of[0] == 1:
                        return
                    dve.wait_ge(sem("eq2_ready"), group + 1)
                    dve.tensor_tensor(ONE2[:, s], bc(EQ2[:, s], 2, 3), bc(PIECES[:, 1:4, ds(t0, NGT)].rearrange("p e t -> p t e"), 3, QK), ALU.mult)\
                       .then_inc(sem("one2_ready"), 1)

                def weights(s, e, row, weighted):
                    k = s % 2
                    dve.wait_ge(sem("values_done"), e + 1)
                    full_ = G[:, ds(row, 1), :].rearrange("p a t -> p (a t)")
                    if not weighted:
                        dve.wait_ge(sem("hidden_bank_free"), e + 3)
                        dve.tensor_tensor(WFULL[:, k, :], ACTV[:, k, :], full_, ALU.mult).then_inc(sem("w_full"), 1)
                        dve.wait_ge(sem("w_full"), e + (1 - (l + 1) * QK))
                        full_ = WFULL[:, k, :]
                    dve.tensor_copy(WR[:, k, 0, :], full_[:, 0:SEQ]).then_inc(sem("w_high"), 1)
                    dve.tensor_copy(WRS[:, k, 0, :], full_[:, SEQ:NT]).then_inc(sem("actv_free"), 1)
                    dve.wait_ge(sem("w_high"), e + 1)
                    dve.tensor_tensor(WR[:, k, 1, :], full_[:, 0:SEQ], WR[:, k, 0, :].bitcast(F32), ALU.subtract).then_inc(sem("weights_ready"), 1)
                    dve.wait_ge(sem("actv_free"), e + 3)
                    dve.tensor_tensor(WRS[:, k, 1, :], full_[:, SEQ:NT], WRS[:, k, 0, :].bitcast(F32), ALU.subtract).then_inc(sem("weights_ready"), 1)

                q_of = [0]
                with dve.Fori(0, NG // 2) as i:
                    for s in range(2):
                        one_hots(i * (2 * NGT) + s * NGT, s, i * 2 + (4 * l * NG + s))
                dve.wait_ge(sem("g_copied"), (4 * l + 1) * NG + 2)
                dve.wait_ge(sem("hidden_bank_free"), e0 + QK + 2)
                v_low(0, e0)
                for k in range(4):
                    rows = slice(QK // 4 * k, QK // 4 * k + QK // 4)
                    TT(G[:, rows, :], G[:, rows, :], G[:, QK + QK // 4 * k:QK + QK // 4 * k + QK // 4, :], ALU.mult)
                    if k == 0:
                        weights(0, e0, 0, True)
                say("first_weighted")
                for q in range(4):
                    q_of[0] = q + 1

                    def body(i, last):
                        for s in range(4):
                            e = i * 4 + (e0 + q * QK + s)
                            end = last and q == 3
                            if (q > 0 or (last and s >= 2)) and not (end and s >= 2):
                                u_low((s + 2) % 4, e + 2)
                            if not (end and s == 3):
                                v_low((s + 1) % 4, e + 1)
                            if s < 3 and q < 3:
                                one_hots((i * 3 + s) * NGT, None, i * 3 + ((4 * l + q + 1) * NG + s))
                            if last and s == 3 and q < 3:
                                dve.wait_ge(sem("g_copied"), (4 * l + q + 2) * NG + 2)
                            if not (end and s == 3):
                                row = q % 2 * QK + s + 1
                                weights((s + 1) % 4, e + 1, i * 4 + row if not (last and s == 3) else (q + 1) % 2 * QK,
                                        q == 0 and not (last and s == 3))
                    with dve.Fori(0, QK // 4 - 1) as i:
                        body(i, False)
                    body(QK // 4 - 1, True)
                dve.wait_ge(sem("values_done"), (l + 1) * NK + 2)
                for t in range(2):
                    for n in range(2):
                        x = X[:, t, 512 * n:512 * n + 512]
                        TT(x, x, banks[2 * t + n][:, :], ALU.add)
                dve.wait_ge(sem("sample_mix_full"), 2 * (l + 1))
                for n in range(2):
                    x = X[0:NS, 2, 512 * n:512 * n + 512]
                    TT(x, x, banks[6 + n][0:NS, :], ALU.add)
                say("x_updated")

            link(dve.memset(ss, 1.0))
            say("ss_set")
            dve.wait_ge(sem("x_loaded"), 48)
            dve.wait_ge(sem("const_loaded"), 80)
            norm(0)
            dve.wait_ge(sem("gain0_loaded"), 16)
            dve.wait_ge(sem("z_ready"), 12)
            half = NORMED // 2
            for t, rows, a in TILES:
                R = slice(0, rows)
                parts = ((0, half, Z[R, t, 0:half * HD]), (half, NORMED, Z[R, t, QB0:QB0 + half * HD]))
                for lo, hi, z in parts:
                    TT(SQ[R, lo:hi, :].rearrange("p h d -> p (h d)"), z, z, ALU.mult)
                link(dve.tensor_reduce(RS24[R], SQ[R], AX, ALU.add))
                TS(RS24[R], RS24[R], 1.0 / HD, EPS, ALU.mult, ALU.add)
                link(dve.reciprocal(RS24[R], RS24[R]))
                say("heads_var")
                dve.wait_ge(sem("heads_rinv"), t + 1)
                for lo, hi, z in parts:
                    zh = z.rearrange("p (h d) -> p h d", d=HD)
                    TT(zh, zh, bc(RS24[R, lo:hi], 2, HD), ALU.mult)
                    TT(zh, zh, GAIN0[R, lo:hi, :], ALU.mult)
                say("heads_normed")
            dve.wait_ge(sem("tbl0_loaded"), 16)
            dve.wait_ge(sem("qkt_ready"), 18)

            def tables0(s, bank, pair, qt, nk):
                at = 0 if qt == 0 else 256
                STT(s, bank[:, 0:2 * nk], SCALE_AB, TBL0[:, pair, at:at + 2 * nk], ALU.mult, ALU.add)

            prompt_attention([(p, qt) for p in range(8) for qt in range(2)], "prompt0", SP_, tables0, O0, 1.0)
            link(dve.memset(QBA, 0.0))
            link(dve.memset(QBB, 0.0))
            for h in range(AH):
                half_ = slice(64 * (h % 2), 64 * (h % 2) + 64)
                step(dve.tensor_copy(QBA[half_, h // 2, :, 4 * h:4 * h + 4], QKT[:, h, SEQ:NT].rearrange("p (b t) -> p b t", t=DEC_T)))
                step(dve.tensor_copy(KNA[half_, h // 2, :], QKT[:, AH + h, SEQ:NT]))
            for j in range(BH):
                g, hh = j // GQ, j % GQ
                step(dve.tensor_copy(QBB[64 * g:64 * g + 64, :, 32 * g + 4 * hh:32 * g + 4 * hh + 4],
                                     QKT[:, 2 * AH + j, SEQ:NT].rearrange("p (b t) -> p b t", t=DEC_T)))
            for g in range(BKV):
                step(dve.tensor_copy(KNB[64 * g:64 * g + 64, :], QKT[:, 2 * AH + BH + g, SEQ:NT]))
            settle()
            say("q_spread")
            dve.wait_ge(sem("tbls_loaded"), 48)
            def sample_first(n, kind, r):
                S = SS_[:, n % 2]
                if kind == "a":
                    for lo, hi in ((0, 512), (512, AK + NS)):
                        bank = full()
                        STT(S[:, lo:hi], bank[:, 0:hi - lo], SCALE_AB, TBLA[:, r, lo:hi], ALU.mult, ALU.add)
                        free()
                else:
                    for c in range(2):
                        bank = full()
                        step(dve.tensor_reduce(GATE[:, 2 * c:2 * c + 2], bank[:, :].rearrange("p (n k) -> p n k", k=BLK), AX, ALU.add))
                        STT(S[:, 512 * c:512 * c + 512], bank[:, :], SCALE_AB, TBLB[:, 512 * c:512 * c + 512], ALU.mult, ALU.add)
                        free()
                        if c == 1:
                            say("gate_ready")
                    bank = full()
                    STT(S[:, PAST:PAST + NS], bank[:, 0:NS], SCALE_AB, TBLBN[:, r, :], ALU.mult, ALU.add)
                    free()
                    bank = full()
                    link(dve.tensor_copy(GATE, bank[:, 0:NBLK]))
                    free()
                    mine, other = bc(GATE, 2, NBLK), bc(GATE, 1, NBLK)
                    step(dve.tensor_tensor(CMP, other, mine, ALU.is_equal))
                    TT(CMP2, other, mine, ALU.is_gt)
                    TT(CMP, CMP, before, ALU.mult)
                    TT(CMP, CMP, CMP2, ALU.add)
                    link(dve.tensor_reduce(RANK, CMP, AX, ALU.add))
                    TS(RANK, RANK, 3.0, -BIG, ALU.is_ge, ALU.mult)
                    ps = S[:, 0:PAST].rearrange("p (n k) -> p n k", k=BLK)
                    TT(ps, ps, bc(RANK, 2, BLK), ALU.add)
                width = (AK if kind == "a" else PAST) + NS
                link(dve.tensor_reduce(MX1[:, n % 2:n % 2 + 1], S[:, 0:width], AX, ALU.max, negate=True))
                say("sample0_scores")

            def sample_second(n, kind, r):
                dve.wait_ge(sem("sample0_exp"), n + 1)
                total = SUM1[:, n % 2:n % 2 + 1]
                link(dve.reciprocal(total, total))
                w = 3 * P if kind == "a" else P
                bank = full()
                TS(OS_[:, 0:w], bank[:, 0:w], total, None, ALU.mult)
                free()
                say("sample0_sums")
                bank = full()
                if kind == "a":
                    link(dve.tensor_copy(OT0[:, 0:3, SEQ + 16 * r:SEQ + 16 * r + 16], bank[:, 0:48].rearrange("p (c n) -> p c n", c=3)))
                else:
                    link(dve.tensor_copy(OT0[:, 3:8, SEQ + 8 * r:SEQ + 8 * r + 8], bank[:, 0:40].rearrange("p (c n) -> p c n", c=5)))
                free()
                say("sample0_done")

            for n in range(len(SUNITS) + 1):
                if n < len(SUNITS):
                    sample_first(n, *SUNITS[n])
                if n >= 1:
                    sample_second(n - 1, *SUNITS[n - 1])
            dve.wait_ge(sem("ot0_prompt"), 4)
            say("ot0_sample")
            add_to_x(0)
            if live(2):
                peer(0)

            def rope(x1, x2, cos, sin, tmp):
                TT(tmp[0], x1, cos, ALU.mult)
                TT(tmp[1], x2, sin, ALU.mult)
                TT(tmp[2], x1, sin, ALU.mult)
                TT(tmp[3], x2, cos, ALU.mult)
                TT(x1, tmp[0], tmp[1], ALU.subtract)
                TT(x2, tmp[2], tmp[3], ALU.add)

            def cmul(out, a, b, tmp, conj=False):
                TT(tmp[0], a[0], b[0], ALU.mult)
                TT(tmp[1], a[1], b[1], ALU.mult)
                TT(out[0], tmp[0], tmp[1], ALU.add if conj else ALU.subtract)
                TT(tmp[0], a[0], b[1], ALU.mult)
                TT(tmp[1], a[1], b[0], ALU.mult)
                TT(out[1], tmp[0], tmp[1], ALU.subtract if conj else ALU.add)

            def odd():
                link(dve.memset(ST8, 1.0))
                norm(2)
                dve.wait_ge(sem("odd_small_loaded"), 16 * 17)
                par = [S5P[:, n, :] for n in range(24)]
                dve.wait_ge(sem("s5_dt"), 1)
                TT(par[4], par[0], par[3], ALU.mult)
                TT(par[5], par[1], par[3], ALU.mult)
                TS(par[10], par[5], 1.0 / TWO_PI, None, ALU.mult)
                TS(par[10], par[10], MAGIC, MAGIC, ALU.add, ALU.subtract)
                for c in (C1, C2, C3):
                    STT(par[5], par[10], -c, par[5], ALU.mult, ALU.add)
                PI_DOWN = 3.1415925
                TS(par[5], par[5], PI_DOWN, -PI_DOWN, ALU.min, ALU.max)
                TS(par[6], par[5], -1.0, None, ALU.mult)
                TT(par[6], par[6], par[5], ALU.max)
                TS(par[6], par[6], -1.0, math.pi / 2, ALU.mult, ALU.add)
                say("s5_angles")
                spans = ((0, CQ), (CQ, CQ + CKV), (CQ + CKV, CQ + CKV + DR))
                SQL = SGM.rearrange("p a b -> p (a b)")
                for t, rows, a in TILES:
                    R = slice(0, rows)
                    dve.wait_ge(sem("z2_ready"), t + 1)
                    TT(SQL[R, 0:416], Z2[R, t, :], Z2[R, t, :], ALU.mult)
                    for k, (lo, hi) in enumerate(spans):
                        step(dve.tensor_reduce(ST8[R, t, k:k + 1], SQL[R, lo:hi], AX, ALU.add))
                    settle()
                    for k, (lo, hi) in enumerate(spans):
                        TS(ST8[R, t, k:k + 1], ST8[R, t, k:k + 1], 1.0 / (hi - lo), EPS, ALU.mult, ALU.add)
                    link(dve.reciprocal(ST8[R, t, 0:3], ST8[R, t, 0:3]))
                    say("latent_var")
                    dve.wait_ge(sem("latent_rinv"), t + 1)
                    for k, (lo, hi) in enumerate(spans):
                        STT(Z2[R, t, lo:hi], Z2[R, t, lo:hi], ST8I[R, t, k:k + 1], GROW[R, lo:hi], ALU.mult, ALU.mult)
                    lo = CQ + CKV
                    rope(Z2[R, t, lo:lo + 16], Z2[R, t, lo + 16:lo + 32], COS[R, t, :], SIN[R, t, :], [SQL[R, 16 * n:16 * n + 16] for n in range(4)])
                    say("latents_ready")
                    bank = full()
                    link(dve.tensor_copy(CQT[:, :, a:a + rows], bank[:, 0:2 * P].rearrange("p (j n) -> p j n", n=P)[:, :, 0:rows]))
                    link(dve.tensor_copy(CKT[:, a:a + rows], bank[:, 2 * P:2 * P + rows]))
                    free()
                    say("latents_turned")
                dve.wait_ge(sem("s5_mag"), 3)
                TT(par[11], par[7], par[8], ALU.mult)
                TT(par[12], par[7], par[9], ALU.mult)
                TS(par[13], par[11], -1.0, None, ALU.add)
                TT(par[14], par[0], par[0], ALU.mult)
                TT(par[15], par[1], par[1], ALU.mult)
                TT(par[14], par[14], par[15], ALU.add)
                link(dve.reciprocal(par[14], par[14]))
                TT(par[15], par[13], par[0], ALU.mult)
                TT(par[16], par[12], par[1], ALU.mult)
                TT(par[15], par[15], par[16], ALU.add)
                TT(par[15], par[15], par[14], ALU.mult)
                TT(par[16], par[12], par[0], ALU.mult)
                TT(par[17], par[13], par[1], ALU.mult)
                TT(par[16], par[16], par[17], ALU.subtract)
                TT(par[16], par[16], par[14], ALU.mult)
                SQH = T12.rearrange("p k a b -> p (k a b)")
                for t, rows, a in TILES:
                    R = slice(0, rows)
                    dve.wait_ge(sem("qkv_ready"), 4 * (t + 1))
                    sq = SQH[R, 0:768].rearrange("p (h e) -> p h e", e=DQK)
                    sk = SQH[R, 768:1280].rearrange("p (h e) -> p h e", e=DN)
                    kr = KR[R, t, :].rearrange("p (h e) -> p h e", e=DN)
                    TT(sq, Q[R, t], Q[R, t], ALU.mult)
                    TT(sk, kr, kr, ALU.mult)
                    link(dve.tensor_reduce(ST8[R, t, 0:8], sq[:, :, 0:DN], AX, ALU.add))
                    link(dve.tensor_reduce(ST8[R, t, 8:16], sk, AX, ALU.add))
                    link(dve.tensor_reduce(ST8[R, t, 16:24], sq[:, :, DN:DQK], AX, ALU.add))
                    TS(ST8[R, t, 0:16], ST8[R, t, 0:16], 1.0 / DN, EPS, ALU.mult, ALU.add)
                    TS(ST8[R, t, 16:24], ST8[R, t, 16:24], 1.0 / DR, EPS, ALU.mult, ALU.add)
                    link(dve.reciprocal(ST8[R, t, 0:24], ST8[R, t, 0:24]))
                    say("qk_var")
                    dve.wait_ge(sem("qk_rinv"), t + 1)
                    qn, qp = Q[R, t, :, 0:DN], Q[R, t, :, DN:DQK]
                    TT(qn, qn, bc(ST8I[R, t, 0:8], 2, DN), ALU.mult)
                    TT(qn, qn, bc(GQN[R], 1, DH), ALU.mult)
                    TT(qp, qp, bc(ST8I[R, t, 16:24], 2, DR), ALU.mult)
                    TT(qp, qp, bc(GQR[R], 1, DH), ALU.mult)
                    rope(Q[R, t, :, DN:DN + 16], Q[R, t, :, DN + 16:DQK], bc(COS[R, t, :], 1, DH), bc(SIN[R, t, :], 1, DH), [RTT[R, n] for n in range(4)])
                    if t < 2:
                        kn = KCAT[R, t, :, 0:DN]
                        TT(kn, kr, bc(ST8I[R, t, 8:16], 2, DN), ALU.mult)
                        TT(kn, kn, bc(GKN[R], 1, DH), ALU.mult)
                        link(dve.tensor_copy(KCAT[R, t, :, DN:DQK], bc(Z2[R, t, CQ + CKV:], 1, DH)))
                    say("qk_ready")
                dve.wait_ge(sem("qct_ready"), 10)

                def tables1(s, bank, pair, qt, nk):
                    at = 0 if qt == 0 else P
                    sh = s.rearrange("p (h k) -> p h k", h=2)
                    TT(sh, bank[:, 0:2 * nk].rearrange("p (h k) -> p h k", h=2), bc(TBLD[:, at:at + nk], 1, 2), ALU.add)

                prompt_attention([(p, qt) for p in range(4) for qt in range(2)], "prompt1", S_D, tables1, O1, SCALE_D)
                link(dve.memset(SUMW, 0.0))
                for h in range(DH):
                    step(dve.memset(SUMW[HD * (h % 2):HD * (h % 2) + HD, h // 2, DEC_T * h:DEC_T * h + DEC_T], 1.0))
                settle()
                say("sum_weights_ready")
                dve.wait_ge(sem("s5_b_loaded"), 16)
                tmp = [T12[:, k, 0:2, :].rearrange("p a b -> p (a b)").rearrange("p (s c) -> p s c", c=32) for k in range(2)]
                f = [bc(par[15], 2, 32), bc(par[16], 2, 32)]
                cmul([BSC[:, 0], BSC[:, 1]], f, [BBD[:, 0], BBD[:, 1]], tmp)
                say("s5_b_scaled")
                TS(CBD[:, 1], CBD[:, 1], -1.0, None, ALU.mult)
                dve.wait_ge(sem("ut_ready"), 4)
                for hf in range(2):
                    S = slice(SG2 * hf, SG2 * hf + SG2)
                    if hf == 0:
                        dve.wait_ge(sem("ot1_prompt"), 2)
                    for s in range(2):
                        step(dve.memset(E[:, s, :, 0:1], 1.0 - s))
                    step(dve.tensor_copy(par[18], par[8]))
                    step(dve.tensor_copy(par[19], par[9]))
                    settle()
                    m = 1
                    while m < SEQ:
                        pw = [bc(par[18][:, S], 2, m), bc(par[19][:, S], 2, m)]
                        t = [T12[:, k, :, 0:m] for k in range(2)]
                        cmul([E[:, k, :, m:2 * m] for k in range(2)], [E[:, k, :, 0:m] for k in range(2)], pw, t)
                        if 2 * m < SEQ:
                            cmul([par[20], par[21]], [par[18], par[19]], [par[18], par[19]], [par[22], par[23]])
                            step(dve.tensor_copy(par[18], par[20]))
                            step(dve.tensor_copy(par[19], par[21]))
                            settle()
                        m *= 2
                    link(dve.tensor_copy(RARR, bc(par[7][:, S], 2, SEQ)))
                    link(dve.memset(RARR[:, :, 0:1], 0.0))
                    dve.wait_ge(sem("bu_ready"), 16 * (hf + 1))
                    bu = [BU[:, k, :, 0:SEQ] for k in range(2)]
                    e = [E[:, k] for k in range(2)]
                    t = [T12[:, k] for k in range(2)]
                    x = [XR[:, k] for k in range(2)]
                    cmul(x, e, bu, t, conj=True)
                    for k in range(2):
                        link(dve.tensor_tensor_scan(t[k].rearrange("p a b -> p (a b)"), RARR.rearrange("p a b -> p (a b)"),
                                                    x[k].rearrange("p a b -> p (a b)"), 0.0, ALU.mult, ALU.add))
                    cmul(bu, e, t, x)
                    ab = [bc(par[11][:, S], 2, DEC_B), bc(par[12][:, S], 2, DEC_B)]
                    prev = [S0[:, k, S, :] for k in range(2)]
                    for n in range(DEC_T):
                        now = [BU[:, k, :, SEQ + n:NT:DEC_T] for k in range(2)]
                        tm = [STMP[:, k] for k in range(4)]
                        cmul([tm[0], tm[1]], ab, prev, [tm[2], tm[3]])
                        for k in range(2):
                            TT(now[k], now[k], tm[k], ALU.add)
                        prev = now
                    for k in range(2):
                        step(dve.tensor_copy(LASTP[:, k, S], BU[:, k, :, SEQ - 1]))
                        step(dve.tensor_copy(LASTS[:, k, S, :], BU[:, k, :, SEQ + DEC_T - 1:NT:DEC_T]))
                    settle()
                    say("states_ready")
                    for c in range(2):
                        bank = full()
                        TS(RK[:, hf, 512 * c:512 * c + 512], bank[:, :], 1.0 / DN, EPS, ALU.mult, ALU.add)
                        free()
                    say("key_vars")
                    for c in range(2 * hf, 2 * hf + 2):
                        bank = full()
                        STT(Y[:, c, :], UT[:, c, :], DSKIP[:, c:c + 1], bank[:, 0:NT], ALU.mult, ALU.add)
                        free()
                        say("y_ready")
                for m in range(4):
                    dve.wait_ge(sem("sgm_ready"), m + 1)
                    TT(OT1[:, m, :], ZG[:, m, :], SGM[:, m, :], ALU.mult)
                    say("oc_ready")
                link(dve.tensor_scalar(QG, QCT[0:DN, :, SEQ:NT], GKNP, None, ALU.mult))
                say("qg_ready")
                for k in range(DH):
                    step(dve.tensor_copy(QPE[0:DR, :, k, :], QCT[DN:DQK, k, SEQ:NT].rearrange("p (b t) -> p b t", t=DEC_T)))
                kp = S_SD[0:NS, 0:DR]
                step(dve.tensor_copy(kp, Z2[0:NS, 2, CQ + CKV:]))
                settle()
                for i in range(1, 4):
                    step(dve.tensor_copy(QPE[DR * i:DR * i + DR], QPE[0:DR]))
                link(dve.transpose(KPEN, kp))
                link(dve.tensor_copy(RKN[0:NS], bc(ST8I[0:NS, 2, 8:16], 2, DEC_T)))
                bank = full()
                link(dve.tensor_copy(QABS.rearrange("p b h t -> p h b t"), bank[:, 0:DH * NS].rearrange("p (h b t) -> p h b t", h=DH, t=DEC_T)))
                free()
                say("qabs_ready")
                dve.wait_ge(sem("tbldn_loaded"), 16)
                dve.wait_ge(sem("key_roots"), 1)
                link(dve.reciprocal(RK, RK))
                for r in range(2):
                    for c in range(2):
                        bank = full()
                        TT(S_SD[:, 512 * c:512 * c + 512], RK[:, r, 512 * c:512 * c + 512], bank[:, :], ALU.mult)
                        free()
                    for c in range(2):
                        bank = full()
                        TT(S_SD[:, 512 * c:512 * c + 512], S_SD[:, 512 * c:512 * c + 512], bank[:, :], ALU.add)
                        free()
                    new = S_SD[:, PAST:]
                    bank = full()
                    link(dve.tensor_copy(RKNX, bank[:, 2 * NS:3 * NS]))
                    TT(new, RKNX, bank[:, 0:NS], ALU.mult)
                    TT(new, new, bank[:, NS:2 * NS], ALU.add)
                    free()
                    TT(new, new, TBLDN[:, r, :], ALU.add)
                    link(dve.tensor_reduce(MX1[:, 0:1], S_SD, AX, ALU.max, negate=True))
                    TS(MX1[:, 0:1], MX1[:, 0:1], SCALE_D, None, ALU.mult)
                    say("sd_scores")
                    dve.wait_ge(sem("sd_exp"), r + 1)
                    link(dve.reciprocal(SUM1[:, 0:1], SUM1[:, 0:1]))
                    bank = full()
                    TS(OSD, bank[:, 0:P], SUM1[:, 0:1], None, ALU.mult)
                    free()
                    say("osd_ready")
                    bank = full()
                    link(dve.tensor_copy(CT[:, :, 16 * r:16 * r + 16].rearrange("p h (i t) -> p i h t", t=DEC_T),
                                         bank[:, 0:P].rearrange("p (i h t) -> p i h t", i=4, t=DEC_T)))
                    free()
                    say("ct_ready")
                bank = full()
                link(dve.tensor_copy(S_SD[0:NS, 0:512], bank[0:NS, :]))
                free()
                say("o1_sample_ready")
                add_to_x(2)

            RTT = Carver(arena, R1_0, R1_N).skip_to(18944 - 2048).take(4, DH, DR // 2)
            if live(3):
                odd()
            if live(4):
                peer(1)
    return nc


def lay_out(x):
    c = np.ascontiguousarray
    f = np.float32
    a = {}
    a["x_prompt"] = c(x["x_prompt"][0])
    a["x_sample"] = c(x["x_sample"].reshape(NS, D))

    def rows(w):
        return c(w.reshape(-1, P, w.shape[-1]).transpose(1, 0, 2))

    a["ev_w_in"], a["ev_w_out"] = rows(x["ev_w_in"][0]), rows(x["ev_w_out"][0])
    a["od_w_in"], a["od_w_out"] = rows(x["od_w_in"][0]), rows(x["od_w_out"][0])
    a["mla_w_uq"] = rows(x["mla_w_uq"][0])
    a["mla_w_uk"], a["mla_w_uv"] = c(x["mla_w_uk"][0]), c(x["mla_w_uv"][0])
    a["mla_w_ukt"] = c(x["mla_w_uk"][0].reshape(P, DH, DN).transpose(2, 1, 0))
    a["s5_w_glu"] = rows(x["s5_w_glu"][0])
    a["peer_w_q"] = c(x["peer_w_q"].reshape(2, KC, P, 2048).transpose(0, 2, 1, 3))
    keys = np.stack([x["peer_k1"], x["peer_k2"]], 2)
    a["peer_k"] = c(keys.transpose(0, 4, 1, 2, 3).reshape(2, P, 2 * PH, NK))
    a["peer_ut"] = c(x["peer_u"].reshape(2, NK, NK, KC, P).transpose(0, 2, 4, 3, 1).reshape(2, NK, P, D))
    a["peer_v"] = c(x["peer_v"].reshape(2, NK, NK, D).transpose(0, 2, 1, 3))
    g = np.stack([x["g_mix"][0], x["g_ffn"][0], x["g_mix"][1], x["g_ffn"][1]])
    a["gain"] = c(g.reshape(4, KC, P).transpose(2, 0, 1))
    a["gain0"] = c(np.concatenate([np.tile(x["ev_g_qa"][0], (AH, 1)), np.tile(x["ev_g_ka"][0], (AH, 1)),
                                   np.tile(x["ev_g_qb"][0], (BH, 1)), np.tile(x["ev_g_kb"][0], (BKV, 1))]))
    a["grow"] = c(np.concatenate([x["mla_g_cq"][0], x["mla_g_ckv"][0], x["mla_g_kr"][0]]))
    a["mla_g_qn"], a["mla_g_qr"], a["mla_g_kn"] = c(x["mla_g_qn"][0]), c(x["mla_g_qr"][0]), c(x["mla_g_kn"][0])
    a["mla_g_kn_col"] = c(x["mla_g_kn"][0].reshape(DN, 1))
    a["page_table"] = c(x["page_table"].reshape(1, -1).astype(np.int32))
    def reach(z):
        far = z[:, :512].reshape(DEC_B, 32, 16, AH * HD)[:, :, 0:DEC_T].reshape(DEC_B, P, AH * HD)
        return np.concatenate([far, z[:, 512:].reshape(DEC_B, 512, AH * HD)], 1)
    a["cache_a_kt"] = c(reach(x["cache_a_k"][0]).reshape(DEC_B, AK, 3, P).transpose(0, 3, 2, 1))
    a["cache_a_v"] = c(reach(x["cache_a_v"][0]).reshape(DEC_B, AKC, P, AH * HD).transpose(0, 2, 1, 3))
    kt = x["cache_b_k"][0].reshape(-1, PAGE, P).transpose(0, 2, 1)
    a["pool_kv"] = c(np.concatenate([kt, x["cache_b_v"][0].reshape(-1, PAGE, P)], 2))
    ck = x["cache_d_ckv"][0]
    a["pool_ckv"] = c(np.concatenate([ck.transpose(0, 2, 1), ck], 2))
    a["pool_kpe"] = c(x["cache_d_kpe"][0].transpose(0, 2, 1))
    def states(z):
        return z.reshape(SCH, P).T
    a["s5_par"] = c(np.stack([states(x["s5_a_re"][0]), states(x["s5_a_im"][0]),
                              states(np.repeat(x["s5_log_dt"][0][:, None], 64, 1))], 1))
    def diag(z):
        out = np.zeros((2, 64, SCH, 2, 16), z.dtype)
        z = z.reshape(SCH, 2, 64, 16)
        for k in range(2):
            out[k, :, :, k, :] = z[:, k].transpose(1, 0, 2)
        return out.reshape(P, SCH, 32)
    a["s5_b"] = c(np.stack([diag(x["s5_b_re"][0]), diag(x["s5_b_im"][0])], 1))
    a["s5_c"] = c(np.stack([diag(x["s5_c_re"][0].transpose(0, 2, 1)), diag(x["s5_c_im"][0].transpose(0, 2, 1))], 1))
    a["state_c"] = c(np.stack([z[0].reshape(DEC_B, SCH, P).transpose(2, 1, 0) for z in (x["state_c_re"], x["state_c_im"])], 1))
    a["s5_d"] = c(x["s5_d"][0].reshape(4, P).T)
    a["s5_b_glu"] = c(x["s5_b_glu"][0].reshape(4, P).T)

    a["ident"] = np.eye(P, dtype=f)
    a["iota"] = c(np.broadcast_to(np.arange(NK, dtype=f), (P, NK)))
    p = np.arange(P)
    row = np.stack([p // 32, p % DEC_T])
    a["group"] = c((row[:, :, None] == row[:, None, :]).all(0).astype(f))
    a["before"] = c(np.broadcast_to(np.tri(NBLK, k=-1, dtype=f), (P, NBLK, NBLK)))
    nh = AH + BH
    slopes = 2.0 ** (-8.0 * np.arange(1, nh + 1) / nh)

    def a_bias(dist, h):
        n = ((dist <= 128) * 1 + ((dist % 4 == 0) & (dist <= 512)) + ((dist % 16 == 0) & (dist <= 2048))) * (dist >= 0)
        return np.where(n > 0, -slopes[h] * dist + np.log(np.maximum(n, 1)), -BIG)

    def b_bias(dist, h):
        return np.where(dist >= 0, -slopes[h] * dist, -BIG)

    q = np.arange(P)[:, None]
    tbl = np.zeros((P, 8, 768))
    for h in range(nh):
        fn = a_bias if h < AH else b_bias
        for qt in range(2):
            nk = P * (qt + 1)
            at = (0 if qt == 0 else 256) + (h % 2) * nk
            tbl[:, h // 2, at:at + nk] = fn(q + P * qt - np.arange(nk)[None, :], h)
    a["tbl0"] = tbl.astype(f)
    far = (np.arange(32)[:, None] * 16 + np.arange(DEC_T)[None, :]).reshape(-1)
    kpos = np.concatenate([far, np.arange(512, PAST)])
    ta = np.zeros((P, 2, AK + NS))
    tb, tbn = np.zeros((P, PAST)), np.zeros((P, 4, NS))
    tdn = np.zeros((P, 2, NS))
    nb, ntk = np.arange(NS) // DEC_T, np.arange(NS) % DEC_T
    for p in range(P):
        i, h, t = p // 32, (p % 32) // 4, p % 4
        for r in range(2):
            if h < AH:
                ta[p, r, :AK] = a_bias(PAST + t - kpos, h)
                ta[p, r, AK:] = np.where(nb == 4 * r + i, a_bias(t - ntk, h), -BIG)
            tdn[p, r] = np.where((nb == 4 * r + i) & (ntk <= t), 0, -BIG)
        i, g, hh, t = p // 64, (p % 64) // 32, (p % 32) // 4, p % 4
        if hh < GQ:
            h = AH + GQ * g + hh
            tb[p] = b_bias(PAST + t - np.arange(PAST), h)
            for r in range(4):
                tbn[p, r] = np.where(nb == 2 * r + i, b_bias(t - ntk, h), -BIG)
    a["tbla"], a["tblb"], a["tblbn"], a["tbldn"] = ta.astype(f), tb.astype(f), tbn.astype(f), tdn.astype(f)
    td = np.zeros((P, 384))
    td[:, 0:P] = np.where(q >= np.arange(P)[None, :], 0, -BIG)
    td[:, P:] = np.where(q + P >= np.arange(SEQ)[None, :], 0, -BIG)
    a["tbld"] = td.astype(f)
    half = DR // 2
    freqs = (np.float32(10000.0) ** (-np.arange(half, dtype=f) / np.float32(half))).astype(f)
    pos = np.zeros((P, 3), f)
    pos[:, 0], pos[:, 1] = np.arange(P), np.arange(P) + P
    pos[0:NS, 2] = PAST + np.arange(NS) % DEC_T
    ang = (pos[:, :, None] * freqs).astype(f)
    a["cos"], a["sin"] = np.cos(ang.astype(np.float64)).astype(f), np.sin(ang.astype(np.float64)).astype(f)
    return a


OUTS = {
    "y_prompt": (SEQ, D), "y_sample": (NS, D),
    "a_k_prompt": (SEQ, AH * HD), "a_v_prompt": (SEQ, AH * HD), "b_k_prompt": (SEQ, BKV * HD), "b_v_prompt": (SEQ, BKV * HD),
    "c_re_prompt": (P, SCH), "c_im_prompt": (P, SCH), "d_ckv_prompt": (SEQ, CKV), "d_kpe_prompt": (SEQ, DR),
    "a_k_sample": (NS, AH * HD), "a_v_sample": (NS, AH * HD), "b_k_sample": (NS, BKV * HD), "b_v_sample": (NS, BKV * HD),
    "c_re_sample": (P, SCH, DEC_B), "c_im_sample": (P, SCH, DEC_B), "d_ckv_sample": (NS, CKV), "d_kpe_sample": (NS, DR),
}


def finish(r):
    lead = {"prompt": (1, 1, SEQ), "sample": (1, DEC_B, DEC_T)}
    out = []
    for name in OUTS:
        v, kind = r[name], name.rsplit("_", 1)[1]
        if name[0] == "y":
            out.append(v.reshape(lead[kind][1:] + (D,)))
        elif name[0] in "ab":
            out.append(v.reshape(lead[kind] + (-1, HD)))
        elif name[0] == "d":
            out.append(v.reshape(lead[kind] + (-1,)))
        elif kind == "prompt":
            out.append(np.ascontiguousarray(v.T).reshape(1, 1, 32, 64))
        else:
            out.append(np.ascontiguousarray(v.transpose(2, 1, 0)).reshape(1, DEC_B, 32, 64))
    return tuple(out)


def declare(nc, arrays):
    ins = {n: nc.dram_tensor(f"in_{n}", a.shape, mybir.dt.from_np(a.dtype), kind="ExternalInput").ap() for n, a in arrays.items()}
    outs = {n: nc.dram_tensor(n, s, F32, kind="ExternalOutput").ap() for n, s in OUTS.items()}
    return ins, outs


def kernel(**inputs):
    import concourse.bacc as bacc
    from concourse.bass_utils import run_bass_kernel_spmd
    arrays = lay_out({n: np.asarray(v) for n, v in inputs.items()})
    nc = bacc.Bacc("TRN2", target_bir_lowering=False, num_devices=1)
    build(nc, *declare(nc, arrays))
    r = run_bass_kernel_spmd(nc, [{f"in_{n}": a for n, a in arrays.items()}], core_ids=[0])
    return finish(r.results[0])
```
